# Optimizing a Trainium2 kernel written in Bass

```python
import math
import jax, jax.numpy as jnp
from jax import lax
import numpy as np

D_MODEL = 1024
BATCH = 1
SEQ = 2048
DEPTH = 1
DEC_BATCH = 8
DEC_SEQ = 1
PAST_LEN = 512
PAGE_SIZE = 128

D_MIX = D_MODEL
C_CONV = D_MIX // 2
N_HEADS = 8
HEAD_DIM = (D_MIX - C_CONV) // N_HEADS
N_KV_HEADS = 2
GROUP = N_HEADS // N_KV_HEADS
CONV_W = 31
N_IDX_HEADS = 4
IDX_DIM = 64
TOPK_MAX = 256
N_META = 16
NUM_BUCKETS = 32
MAX_DISTANCE = 128
Q_BLOCK = 128
EPS = 1e-6
LN_EPS = 1e-5

PROJ_SIZES = (C_CONV, C_CONV, C_CONV,
              N_HEADS * HEAD_DIM, N_KV_HEADS * HEAD_DIM,
              N_KV_HEADS * HEAD_DIM, N_HEADS * HEAD_DIM,
              N_IDX_HEADS * IDX_DIM, IDX_DIM, N_IDX_HEADS)
PROJ_SPLITS = tuple(int(s) for s in np.cumsum(PROJ_SIZES)[:-1])
D_IN = int(sum(PROJ_SIZES))

kernel_name = "hymba_conformer_dsa_decode_step"

def rmsnorm(x, g):
    xf = x.astype(jnp.float32)
    y = xf * lax.rsqrt(jnp.mean(xf * xf, axis=-1, keepdims=True) + EPS) * g.astype(jnp.float32)
    return y.astype(x.dtype)

def project(xn, w_in):
    B, T = xn.shape[:2]
    h = xn @ w_in
    ua, ub, gc, q, k, v, ga, iq, ik, iw = jnp.split(h, PROJ_SPLITS, axis=-1)
    u = ua * jax.nn.sigmoid(ub)
    q = q.reshape(B, T, N_HEADS, HEAD_DIM)
    k = k.reshape(B, T, N_KV_HEADS, HEAD_DIM)
    v = v.reshape(B, T, N_KV_HEADS, HEAD_DIM)
    iq = iq.reshape(B, T, N_IDX_HEADS, IDX_DIM) * (IDX_DIM ** -0.5)
    iw = iw * (N_IDX_HEADS ** -0.5)
    return u, gc, q, k, v, ga, iq, ik, iw

def conv_branch(u_ext, w, b, ln_g, ln_b):
    y = lax.conv_general_dilated(u_ext, w[:, None, :], window_strides=(1,), padding='VALID',
                                 dimension_numbers=('NWC', 'WIO', 'NWC'),
                                 feature_group_count=C_CONV) + b
    yf = y.astype(jnp.float32)
    mu = jnp.mean(yf, axis=-1, keepdims=True)
    var = jnp.mean(jnp.square(yf - mu), axis=-1, keepdims=True)
    yn = (yf - mu) * lax.rsqrt(var + LN_EPS) * ln_g.astype(jnp.float32) + ln_b.astype(jnp.float32)
    return jax.nn.silu(yn).astype(u_ext.dtype)

def t5_bucket(rel):
    n = jnp.maximum(rel, 0)
    max_exact = NUM_BUCKETS // 2
    large = max_exact + (jnp.log(jnp.maximum(n, 1).astype(jnp.float32) / max_exact)
                         / math.log(MAX_DISTANCE / max_exact)
                         * (NUM_BUCKETS - max_exact)).astype(jnp.int32)
    large = jnp.minimum(large, NUM_BUCKETS - 1)
    return jnp.where(n < max_exact, n, large)

def sparse_attend(q, iq, iw, qpos, k_all, v_all, ik_all, rel_bias, topk):
    B, T = q.shape[:2]
    L = k_all.shape[1]
    kpos = jnp.arange(L, dtype=jnp.int32)
    s = jnp.einsum('bthd,bsd->bths', iq.astype(jnp.float32), ik_all.astype(jnp.float32))
    score = jnp.einsum('bth,bths->bts', iw.astype(jnp.float32), jax.nn.relu(s))
    admissible = kpos[None, :] <= qpos[:, None]
    score = jnp.where(admissible[None], score, -jnp.inf)
    _, idx = lax.top_k(score, topk)
    valid = idx <= qpos[None, :, None]
    gather = jax.vmap(lambda a, i: a[i])
    k_sel = gather(k_all, idx)
    v_sel = gather(v_all, idx)
    qg = q.reshape(B, T, N_KV_HEADS, GROUP, HEAD_DIM)
    logits = jnp.einsum('btngd,btknd->btngk', qg, k_sel).astype(jnp.float32) * (HEAD_DIM ** -0.5)
    bias = rel_bias[t5_bucket(qpos[None, :, None] - idx)]
    bias = jnp.moveaxis(bias.reshape(B, T, topk, N_KV_HEADS, GROUP), 2, -1)
    logits = logits + bias.astype(jnp.float32)
    logits = jnp.where(valid[:, :, None, None, :], logits, -jnp.inf)
    p = jax.nn.softmax(logits, axis=-1)
    o = jnp.einsum('btngk,btknd->btngd', p.astype(v_sel.dtype), v_sel)
    return o.reshape(B, T, N_HEADS * HEAD_DIM)

def to_blocks(a, l_pad, n_blk):
    B, L = a.shape[:2]
    a = jnp.pad(a, ((0, 0), (0, l_pad - L)) + ((0, 0),) * (a.ndim - 2))
    return jnp.moveaxis(a.reshape((B, n_blk, Q_BLOCK) + a.shape[2:]), 1, 0)

def merge(conv_y, gc, attn_o, ga, w_out):
    mix = jnp.concatenate([conv_y * jax.nn.silu(gc), attn_o * jax.nn.silu(ga)], axis=-1)
    return mix @ w_out

def setup_inputs(seed: int = 0) -> dict:
    key = jax.random.key(seed)
    ks = jax.random.split(key, 17)
    n_pages = PAST_LEN // PAGE_SIZE
    n_pool = (DEC_BATCH * n_pages * 5) // 4
    nrm = jax.random.normal
    page_table = jax.random.permutation(ks[6], n_pool)[:DEC_BATCH * n_pages].reshape(DEC_BATCH, n_pages).astype(jnp.int32)
    return {
        "x_prompt": nrm(ks[0], (BATCH, SEQ, D_MODEL), jnp.float32),
        "x_sample": nrm(ks[1], (DEC_BATCH, DEC_SEQ, D_MODEL), jnp.float32),
        "cache_k": nrm(ks[2], (DEPTH, n_pool, PAGE_SIZE, N_KV_HEADS, HEAD_DIM), jnp.float32),
        "cache_v": nrm(ks[3], (DEPTH, n_pool, PAGE_SIZE, N_KV_HEADS, HEAD_DIM), jnp.float32),
        "cache_idx_k": nrm(ks[4], (DEPTH, n_pool, PAGE_SIZE, IDX_DIM), jnp.float32),
        "state_conv": 0.5 * nrm(ks[5], (DEPTH, DEC_BATCH, CONV_W - 1, C_CONV), jnp.float32),
        "page_table": page_table,
        "meta_tokens": nrm(ks[7], (N_META, D_MODEL), jnp.float32),
        "rel_bias": 0.5 * nrm(ks[8], (NUM_BUCKETS, N_HEADS), jnp.float32),
        "norm_g": 1.0 + 0.05 * nrm(ks[9], (DEPTH, D_MODEL), jnp.float32),
        "w_in": nrm(ks[10], (DEPTH, D_MODEL, D_IN), jnp.float32) * D_MODEL ** -0.5,
        "conv_w": nrm(ks[11], (DEPTH, CONV_W, C_CONV), jnp.float32) * CONV_W ** -0.5,
        "conv_b": 0.02 * nrm(ks[12], (DEPTH, C_CONV), jnp.float32),
        "conv_ln_g": 1.0 + 0.05 * nrm(ks[13], (DEPTH, C_CONV), jnp.float32),
        "conv_ln_b": 0.02 * nrm(ks[14], (DEPTH, C_CONV), jnp.float32),
        "w_out": nrm(ks[15], (DEPTH, D_MIX, D_MODEL), jnp.float32) * D_MIX ** -0.5,
        "final_norm_g": 1.0 + 0.05 * nrm(ks[16], (D_MODEL,), jnp.float32),
    }

def reference(x_prompt, x_sample, cache_k, cache_v, cache_idx_k, state_conv, page_table,
              meta_tokens, rel_bias, norm_g, w_in, conv_w, conv_b, conv_ln_g, conv_ln_b,
              w_out, final_norm_g):
    B, S, _ = x_prompt.shape
    L_p = S + N_META
    topk_p = min(TOPK_MAX, L_p // 4)
    n_blk = -(-L_p // Q_BLOCK)
    L_pad = n_blk * Q_BLOCK
    pos_blocks = jnp.arange(L_pad, dtype=jnp.int32).reshape(n_blk, Q_BLOCK)

    DB, T_s, _ = x_sample.shape
    n_pages = page_table.shape[1]
    past = n_pages * cache_k.shape[2]
    L_s = past + T_s
    topk_s = min(TOPK_MAX, L_s // 4)
    pos_s = past + jnp.arange(T_s, dtype=jnp.int32)

    xp = jnp.concatenate([jnp.broadcast_to(meta_tokens[None].astype(x_prompt.dtype), (B, N_META, D_MODEL)),
                          x_prompt], axis=1)
    xs = x_sample
    kp, vp, ikp, cp = [], [], [], []
    ksm, vsm, iks, cs = [], [], [], []
    for l in range(DEPTH):
        xn = rmsnorm(xp, norm_g[l])
        u, gc, q, k, v, ga, iq, ik, iw = project(xn, w_in[l])
        u_ext = jnp.pad(u, ((0, 0), (CONV_W - 1, 0), (0, 0)))
        cy = conv_branch(u_ext, conv_w[l], conv_b[l], conv_ln_g[l], conv_ln_b[l])
        o_blk = lax.map(lambda a: sparse_attend(a[0], a[1], a[2], a[3], k, v, ik, rel_bias, topk_p),
                        (to_blocks(q, L_pad, n_blk), to_blocks(iq, L_pad, n_blk),
                         to_blocks(iw, L_pad, n_blk), pos_blocks))
        o = jnp.moveaxis(o_blk, 0, 1).reshape(B, L_pad, N_HEADS * HEAD_DIM)[:, :L_p]
        xp = xp + merge(cy, gc, o, ga, w_out[l])
        kp.append(k); vp.append(v); ikp.append(ik); cp.append(u_ext[:, -(CONV_W - 1):])

        xn = rmsnorm(xs, norm_g[l])
        u, gc, q, k, v, ga, iq, ik, iw = project(xn, w_in[l])
        u_ext = jnp.concatenate([state_conv[l].astype(u.dtype), u], axis=1)
        cy = conv_branch(u_ext, conv_w[l], conv_b[l], conv_ln_g[l], conv_ln_b[l])
        k_past = cache_k[l][page_table].reshape(DB, past, N_KV_HEADS, HEAD_DIM)
        v_past = cache_v[l][page_table].reshape(DB, past, N_KV_HEADS, HEAD_DIM)
        ik_past = cache_idx_k[l][page_table].reshape(DB, past, IDX_DIM)
        k_all = jnp.concatenate([k_past.astype(k.dtype), k], axis=1)
        v_all = jnp.concatenate([v_past.astype(v.dtype), v], axis=1)
        ik_all = jnp.concatenate([ik_past.astype(ik.dtype), ik], axis=1)
        o = sparse_attend(q, iq, iw, pos_s, k_all, v_all, ik_all, rel_bias, topk_s)
        xs = xs + merge(cy, gc, o, ga, w_out[l])
        ksm.append(k); vsm.append(v); iks.append(ik); cs.append(u_ext[:, -(CONV_W - 1):])

    y_prompt = rmsnorm(xp, final_norm_g)[:, N_META:]
    y_sample = rmsnorm(xs, final_norm_g)
    return (y_prompt, y_sample,
            jnp.stack(kp), jnp.stack(vp), jnp.stack(ikp), jnp.stack(cp),
            jnp.stack(ksm), jnp.stack(vsm), jnp.stack(iks), jnp.stack(cs))


_drawn_inputs = setup_inputs


def setup_inputs(seed=0):
    import zlib

    import numpy as np

    out = dict(_drawn_inputs(seed))
    spreads = {}
    factors = {'rel_bias': 3.731, 'conv_b': 5.936, 'conv_ln_g': 3.434, 'conv_ln_b': 8.0}
    for name, (base, spread) in spreads.items():
        noise = np.random.default_rng([zlib.crc32(name.encode()), seed]).standard_normal(out[name].shape)
        drawn = base * np.exp(spread * noise) if base else spread * noise
        out[name] = __import__('jax').numpy.asarray(drawn.astype(out[name].dtype))
    for name, factor in factors.items():
        out[name] = (out[name] * factor).astype(out[name].dtype)
    return out
```

```python
import concourse.bass as bass
from concourse import mybir
from contextlib import ExitStack
import math
import numpy as np

f32 = mybir.dt.float32
f32r = mybir.dt.float32r
bf16 = mybir.dt.bfloat16
i32 = mybir.dt.int32
ALU = mybir.AluOpType
ACT = mybir.ActivationFunctionType
AX = mybir.AxisListType

D = 1024
KC = D // 128
SEQ, META = 2048, 16
LP = SEQ + META
P = 128
NT = -(-LP // P)
LAST = NT - 1
LREM = LP - LAST * P
SROW, NS = 32, 8
C = 512
CC = C // 128
NH, HD, NKV, GRP = 8, 64, 2, 4
IH = 4
TAPS = 31
PAST, PAGE = 512, 128
NPAGE = PAST // PAGE
LS = PAST + 1
TOPK_P, TOPK_S = 256, 128
NBUCKET = 32
OFF = dict(ua=0, ub=512, gc=1024, q=1536, k=2048, v=2176, ga=2304, iq=2816, ik=3072, iw=3136)
NAT = 2 * 128 + 64 + IH
NEG = -1.0e30
EPS, LN_EPS = 1e-6, 1e-5
HALF = 8
SLOTS = NT - HALF
HALVES = ([[14, 15, 16], [11, 12, 13], [8, 9, 10]], [[5, 6, 7], [2, 3, 4], [0, 1]])
UNIT = 1024


def width(i):
    return min((i + 1) * P, LP)


def pieces(i):
    return [(a, min(UNIT, width(i) - a)) for a in range(0, width(i), UNIT)]


def t5_bucket(rel):
    n = np.maximum(rel, 0)
    exact = NBUCKET // 2
    large = exact + (np.log(np.maximum(n, 1).astype(np.float32) / np.float32(exact))
                     / np.float32(math.log(128 / exact)) * np.float32(NBUCKET - exact)).astype(np.int32)
    return np.where(n < exact, n, np.minimum(large, NBUCKET - 1))


BANDX = 384
CONST_COLS = dict(ident=(0, 128), causal=(128, 128), e8=(256, 64), e4=(320, 32), iota=(352, 24), kk=(376, NT),
                  ones=(393, 128), e8t=(521, 8), band=(529, BANDX), samp=(529 + BANDX, LS))
NCONST = 529


def constants():
    c = np.zeros((128, NCONST + BANDX + LS), np.float32)

    def at(name):
        a, n = CONST_COLS[name]
        return c[:, a:a + n]
    at("ident")[:] = np.eye(128)
    at("causal")[:] = np.where(np.arange(128)[None] <= np.arange(128)[:, None], 0, NEG)
    for b in range(NS):
        at("e8")[[b, SROW + b], b * NH:(b + 1) * NH] = 1
        at("e4")[SROW + b, b * IH:(b + 1) * IH] = 1
        at("e8t")[b * NH:(b + 1) * NH, b] = 1
    for x in range(BANDX):
        at("band")[t5_bucket(np.array(255 - x)), x] += 1
        at("band")[NBUCKET - 1, x] -= 1
    for s in range(LS):
        at("samp")[t5_bucket(np.array(PAST - s)), s] += 1
        at("samp")[NBUCKET - 1, s] -= 1
    at("iota")[:] = np.tile(np.arange(8), 3)
    at("kk")[:] = TOPK_P
    at("kk")[SROW:SROW + NS, LAST] = TOPK_S
    at("ones")[:] = 1.0 / C
    return c


def part(cst, name):
    a, n = CONST_COLS[name]
    return cst[:, a:a + n]


def tile_rows(i):
    if i == 0:
        return [(0, META, "meta", 0), (META, P - META, "x", 0)]
    if i == LAST:
        return [(0, LREM, "x", LAST * P - META), (SROW, NS, "sample", 0)]
    return [(0, P, "x", i * P - META)]


class Jobs:

    def __init__(self, jobs, slots=4):
        self.jobs, self.slots = jobs, slots

    def count(self, n, kinds):
        return sum(1 for j in self.jobs[:n] if j[0] in kinds)


def project_norm_and_keys(nc, t, mem):
    jobs = [("xT", 0)]
    for i in range(NT):
        if i + 1 < NT:
            jobs.append(("xT", i + 1))
        jobs.append(("nat", i))
        if i:
            jobs.append(("ikT", i - 1))
    jobs.append(("ikT", NT - 1))
    J = Jobs(jobs)
    with ExitStack() as ctx:
        sb = lambda n, s, d=f32: ctx.enter_context(nc.sbuf_tensor(n, s, d))
        sem = lambda n: ctx.enter_context(nc.semaphore(n))
        xst = sb("xst", [128, 2, D])
        xs = sb("xs", [128, 2, D])
        sq = sb("sq", [128, D])
        ssq = sb("ssq", [128, NT])
        ms = sb("ms", [128, NT])
        rstd = sb("rstd", [128, NT])
        mhalf = sb("mhalf", [128, 1])
        wn = sb("wn", [128, KC, NAT])
        wnh = sb("wnh", [128, KC, NAT], f32r)
        wnl = sb("wnl", [128, KC, NAT], f32r)
        natst = sb("natst", [128, 2, 384])
        psum = ctx.enter_context(nc.psum_tensor("psum0", [128, 4, UNIT], f32))
        x_in = [sem(f"x_in{s}") for s in range(2)]
        c_in, w_in_s = sem("c_in"), sem("w_in_s")
        sq_done, rstd_done, xs_done, zeroed = sem("sq_done"), sem("rstd_done"), sem("xs_done"), sem("zeroed")
        pool_step, w_mul, w_hi, w_lo = sem("pool_step"), sem("w_mul"), sem("w_hi"), sem("w_lo")
        pe_job, act_job, dve_job = sem("pe_job0"), sem("act_job0"), sem("dve_job0")
        xh_done, nat_done, ikh_done = sem("xh_done"), sem("nat_done"), sem("ikh_done")
        spill = [sem(f"x_spill{s}") for s in range(HALF)]
        nat_out = [sem(f"nat_out{s}") for s in range(2)]
        n_in = [len(tile_rows(i)) for i in range(NT)]

        def x_arrived(eng, i):
            eng.wait_ge(x_in[i % 2], 16 * sum(n_in[j] for j in range(i % 2, i + 1, 2)))

        def nat_written(eng, i):
            n = sum(3 * n for n in ([1] * LAST + [2])[i % 2:i + 1:2])
            eng.wait_ge(nat_out[i % 2], 16 * n)

        def slot(i):
            return i if i < HALF else i - HALF
        block = ctx.enter_context(nc.Block())

        @block.sync
        def _(sp):
            def load_x(i):
                if i >= 2:
                    sp.wait_ge(xs_done, i - 1)
                if i == LAST:
                    sp.wait_ge(zeroed, 1)
                for p0, n, what, r0 in tile_rows(i):
                    src = {"meta": t.meta_tokens, "x": t.x_prompt[0], "sample": t.x_sample[:, 0, :]}[what]
                    sp.dma_start(xst[p0:p0 + n, i % 2, :], src[r0:r0 + n, :]).then_inc(x_in[i % 2], 16)
            load_x(0)
            sp.dma_start(mem.cst[:, :], t.consts[:, 0:NCONST]).then_inc(c_in, 16)
            sp.dma_start(mem.g[:, :], t.norm_g[0].rearrange("(c p) -> p c", p=128),
                         allow_slow_non_contiguous=True).then_inc(c_in, 16)
            w3 = t.w_in[0].rearrange("(c p) n -> p c n", p=128)
            sp.dma_start(wn[:, :, 0:256], w3[:, :, OFF["k"]:OFF["k"] + 256]).then_inc(w_in_s, 16)
            sp.dma_start(wn[:, :, 256:NAT], w3[:, :, OFF["ik"]:OFF["ik"] + 68]).then_inc(w_in_s, 16)
            load_x(1)
            for i in range(NT):
                if i + 2 < NT:
                    load_x(i + 2)
                if i < HALF:
                    sp.wait_ge(dve_job, J.count(J.jobs.index(("xT", i)) + 1, ("xT", "ikT")))
                    sp.dma_start(t.d_xh[i], mem.xh[:, slot(i)].rearrange("p c t -> p (c t)").bitcast(f32)).then_inc(spill[i], 16)
                    sp.dma_start(t.d_xl[i], mem.xl[:, slot(i)].rearrange("p c t -> p (c t)").bitcast(f32)).then_inc(spill[i], 16)
                sp.wait_ge(nat_done, i + 1)
                n = natst[:, i % 2]
                for p0, rows, what, r0 in ([(0, P, "p", 0)] if i < LAST else [(0, LREM, "p", 0), (SROW, NS, "s", 0)]):
                    r = slice(i * P, i * P + rows)
                    ko = t.nk_p[0, 0, r] if what == "p" else t.nk_s[0, :, 0]
                    vo = t.nv_p[0, 0, r] if what == "p" else t.nv_s[0, :, 0]
                    io = t.nik_p[0, 0, r] if what == "p" else t.nik_s[0, :, 0]
                    q = slice(p0, p0 + rows)
                    sp.dma_start(ko.rearrange("t n d -> t (n d)"), n[q, 0:128]).then_inc(nat_out[i % 2], 16)
                    sp.dma_start(vo.rearrange("t n d -> t (n d)"), n[q, 128:256]).then_inc(nat_out[i % 2], 16)
                    sp.dma_start(io, n[q, 256:320]).then_inc(nat_out[i % 2], 16)
            nat_written(sp, LAST)
            nat_written(sp, LAST - 1)
            for s in range(HALF):
                sp.wait_ge(spill[s], 32)

        @block.gpsimd
        def _(pool):
            nc.gpsimd.memset(mhalf[:, :], -0.5).then_inc(pool_step, 1)
            pool.wait_ge(c_in, 32)
            pool.wait_ge(w_in_s, 32)
            nc.gpsimd.tensor_tensor(out=wn[:, :, :], in0=wn[:, :, :], in1=mem.g[:, :].unsqueeze(2).to_broadcast([128, KC, NAT]),
                                    op=ALU.mult).then_inc(w_mul, 1)
            pool.wait_ge(w_mul, 1)
            pool.wait_ge(w_hi, 1)
            nc.gpsimd.tensor_tensor(out=wnl[:, :, :], in0=wn[:, :, :], in1=wnh[:, :, :].bitcast(f32),
                                    op=ALU.subtract).then_inc(w_lo, 1)
            for i in range(NT):
                if i == LAST - 1:
                    pool.wait_ge(xs_done, LAST - 1)
                    nc.gpsimd.memset(xst[:, LAST % 2, :], 0.0).then_inc(zeroed, 1)
                pool.wait_ge(sq_done, i + 1)
                nc.gpsimd.tensor_scalar(ms[:, i:i + 1], ssq[:, i:i + 1], 1.0 / D, EPS, ALU.mult, ALU.add).then_inc(pool_step, 1)
                pool.wait_ge(pool_step, i + 2)
                nc.gpsimd.tensor_tensor(out=rstd[:, i:i + 1], in0=ms[:, i:i + 1], in1=mhalf[:, :], op=ALU.pow).then_inc(rstd_done, 1)

        @block.scalar
        def _(act):
            def square(i):
                x_arrived(act, i)
                if i:
                    act.wait_ge(sq_done, i)
                nc.scalar.activation(sq[:, :], xst[:, i % 2, :], ACT.Square, accum_out=ssq[:, i:i + 1]).then_inc(sq_done, 1)
            square(0)
            act.wait_ge(w_mul, 1)
            nc.scalar.activation(wnh[:, :, :], wn[:, :, :], ACT.Copy).then_inc(w_hi, 1)
            for n, (kind, i) in enumerate(J.jobs):
                if kind == "xT" and i + 1 < NT:
                    square(i + 1)
                act.wait_ge(pe_job, n + 1)
                u = psum[:, n % 4]
                if kind == "xT":
                    if i >= HALF:
                        if i < 2 * HALF:
                            act.wait_ge(spill[i - HALF], 32)
                    nc.scalar.activation(mem.xh[:, slot(i)].rearrange("p c t -> p (c t)"), u, ACT.Copy).then_inc(act_job, 1)
                elif kind == "nat":
                    if i >= 2:
                        nat_written(act, i - 2)
                    nc.scalar.activation(natst[:, i % 2, 0:256], u[:, 0:256], ACT.Copy)
                    nc.scalar.activation(natst[:, i % 2, 256:384].rearrange("p (a d) -> p a d", a=2),
                                         u[:, 256:320].unsqueeze(1).to_broadcast([128, 2, 64]), ACT.Copy).then_inc(nat_done, 1)
                    nc.scalar.activation(mem.iw[:, i], u[:, 320:324], ACT.Copy, scale=float(IH) ** -0.5).then_inc(act_job, 1)
                else:
                    nc.scalar.activation(mem.ikh[:, i * P:(i + 1) * P], u[:, 0:128], ACT.Copy).then_inc(act_job, 1)

        @block.vector
        def _(dve):
            def scale(i):
                dve.wait_ge(rstd_done, i + 1)
                if i >= 2:
                    dve.wait_ge(pe_job, J.jobs.index(("xT", i - 2)) + 1)
                nc.vector.tensor_scalar(xs[:, i % 2, :], xst[:, i % 2, :], rstd[:, i:i + 1], None, ALU.mult).then_inc(xs_done, 1)
            scale(0)
            for n, (kind, i) in enumerate(J.jobs):
                u = psum[:, n % 4]
                if kind == "xT":
                    if i + 1 < NT:
                        scale(i + 1)
                    dve.wait_ge(act_job, n + 1)
                    nc.vector.tensor_tensor(out=mem.xl[:, slot(i)].rearrange("p c t -> p (c t)"), in0=u,
                                            in1=mem.xh[:, slot(i)].rearrange("p c t -> p (c t)").bitcast(f32),
                                            op=ALU.subtract).then_inc(dve_job, 1)
                elif kind == "ikT":
                    dve.wait_ge(act_job, n + 1)
                    nc.vector.tensor_tensor(out=mem.ikl[:, i * P:(i + 1) * P], in0=u[:, 0:128],
                                            in1=mem.ikh[:, i * P:(i + 1) * P].bitcast(f32), op=ALU.subtract).then_inc(dve_job, 1)

        @block.tensor
        def _(pe):
            ident = part(mem.cst, "ident")
            for n, (kind, i) in enumerate(J.jobs):
                u = psum[:, n % 4]
                if n >= 4:
                    pe.wait_ge(act_job, n - 3)
                    if J.count(n - 3, ("xT", "ikT")):
                        pe.wait_ge(dve_job, J.count(n - 3, ("xT", "ikT")))
                if kind == "xT":
                    if n == 0:
                        pe.wait_ge(c_in, 32)
                    pe.wait_ge(xs_done, i + 1)
                    for c in range(KC):
                        last = nc.tensor.transpose(u[:, c * P:(c + 1) * P], xs[:, i % 2, c * P:(c + 1) * P], ident)
                elif kind == "nat":
                    if i == 0:
                        pe.wait_ge(w_lo, 1)
                    pe.wait_ge(dve_job, J.count(J.jobs.index(("xT", i)) + 1, ("xT", "ikT")))
                    xh, xl = mem.xh[:, slot(i)], mem.xl[:, slot(i)]
                    for c in range(KC):
                        for k, (a, b) in enumerate(((xh, wnh), (xh, wnl), (xl, wnh))):
                            last = nc.tensor.matmul(u[:, 0:NAT], a[:, c, :], b[:, c, :], start=(c == 0 and k == 0),
                                                    stop=(c == KC - 1 and k == 2))
                else:
                    pe.wait_ge(nat_done, i + 1)
                    last = nc.tensor.transpose(u[:, 0:128], natst[:, i % 2, 256:384], ident)
                last.then_inc(pe_job, 1)


_IQ = [("iq", 0), ("iq", 1)]
_REST = [("q", j) for j in range(4)] + [(a, j) for j in range(4) for a in ("ub", "ua")] + \
        [(a, j) for a in ("gc", "ga") for j in range(4)]
IQ_AT = 6
CHUNKS = (_IQ + _REST, _REST[:IQ_AT] + _IQ + _REST[IQ_AT:])
NCHUNK = len(CHUNKS[0])
SCORE_AT = {(0, 2): 0, (0, 14): 1, (1, 4): 2, (1, 12): 3, (1, 18): 4}
GROUPS = [[16, 15, 14], [13, 12, 11], [10, 9, 8], [7, 6, 5], [4, 3, 2]]
SEARCH = [8, 8, 8, 8, 9]
TINY = 1e-30


def chunk_columns(name, j):
    if name in ("q", "ga"):
        return [(OFF[name] + 64 * j, 64), (OFF[name] + 256 + 64 * j, 64)]
    return [(OFF[name] + 128 * j, 128)]


def select_jobs():
    jobs = []
    for h, blocks in enumerate(HALVES):
        for c, (name, j) in enumerate(CHUNKS[h]):
            if (h, c) in SCORE_AT:
                g = SCORE_AT[h, c]
                if g == 0:
                    jobs += [("we", 0)] + [("page", b) for b in range(NS)] + [("ss", 0), ("sw", 0)]
                jobs += [("score", i, head, a, n) for i in GROUPS[g] for head in range(IH) for a, n in pieces(i)]
            jobs += [("proj", h, c, b) for b in range(len(blocks))]
    return jobs


def project_and_select(nc, t, mem):
    jobs = select_jobs()
    uses = [(h, c) for h in range(2) for c in range(NCHUNK)]
    first = {}
    lastjob = {}
    for n, j in enumerate(jobs):
        if j[0] == "proj":
            first.setdefault((j[1], j[2]), n)
            lastjob[j[1], j[2]] = n
    W3 = 3 * P
    with ExitStack() as ctx:
        sb = lambda n, s, d=f32: ctx.enter_context(nc.sbuf_tensor(n, s, d))
        sem = lambda n: ctx.enter_context(nc.semaphore(n))
        wst = sb("wst", [128, 2, KC, P])
        wh = sb("wh", [128, 2, KC, P], f32r)
        wl = sb("wl", [128, 2, KC, P], f32r)
        iqs = sb("iqs", [128, IH, SLOTS * P], f32r)
        fst = sb("fst", [128, 2, W3])
        hst = sb("hst", [128, 2, W3], f32r)
        lst = sb("lst", [128, 2, W3], f32r)
        ust = sb("ust", [128, 2, W3])
        sig = sb("sig", [128, 3, W3])
        r = sb("r", [128, 2, UNIT])
        scores = sb("scores", [128, 3, LP])
        hit = sb("hit", [128, LP], bf16)
        run = sb("run", [128, LP])
        iqpad = sb("iqpad", [64, NS * NS * IH])
        qpad = sb("qpad", [128, NS * NS * NH])
        iks = sb("iks", [64, NS])
        we = sb("we", [SROW + NS, NS * IH])
        ws = sb("ws", [NS * IH, NS])
        sscore = sb("sscore", [SROW + NS, LS])
        ptab = sb("ptab", [1, NS * NPAGE], i32)
        G3 = lambda n, *s, d=f32: sb(n, [128, *s], d)
        amax, lo, hi, T = G3("amax", 3), G3("lo", 2, 3), G3("hi", 2, 3), G3("T", 2, 3)
        kt, k4, slope, sum4 = G3("kt", 3), G3("k4", 3), G3("slope", 3), G3("sum4", 3)
        m8s, m8, hot = G3("m8s", 3, 4, 8), G3("m8", 3, 8), G3("hot", 3, 8)
        gap, num, jj, jc, more, rest = G3("gap", 2, 3), G3("num", 3), G3("jj", 3), G3("jc", 3), G3("more", 3), G3("rest", 3)
        above, tie_room, tiny, zero = G3("above", 3), G3("tie_room", 3), G3("tiny", 3), G3("zero", 3)
        ge, lt, upd = G3("ge", 3, d=i32), G3("lt", 3, d=i32), G3("upd", 3, d=i32)
        gef, fall = G3("gef", 3), G3("fall", 3, d=i32)
        flag, flagT, flag1, flagi = G3("flag", 32), G3("flagT", 32), G3("flag1", 1), G3("flagi", 1, d=i32)
        psum = ctx.enter_context(nc.psum_tensor("psum1", [128, 4, UNIT], f32))
        kp = scores[:, :, :].rearrange("p a b -> p (a b)")
        ikp = kp[:, 0:NS * NPAGE * 64].rearrange("p (n d) -> p n d", d=64)
        ikTs = kp[0:64, NS * NPAGE * 64:NS * NPAGE * 64 + NS * PAST].rearrange("p (b s) -> p b s", b=NS)

        w_ld = [sem(f"w_ld{s}") for s in range(2)]
        x_ld = [sem(f"x_ld{s}") for s in range(HALF)]
        w_mul, w_hi, w_lo = sem("w_mul1"), sem("w_hi1"), sem("w_lo1")
        pe_job, act_job = sem("pe_job1"), sem("act_job1")
        staged, combined = sem("staged"), sem("combined")
        out_s = [sem(f"out_s{s}") for s in range(2)]
        iq_in = sem("iq_in")
        relu_done, added = sem("relu_done"), sem("added")
        pages_in, zero_pad, iks_done, we_done = sem("pages_in"), sem("zero_pad"), sem("iks_done"), sem("we_done")
        ptab_in, page_copied, srelu, ws_done, ss_done = sem("ptab_in"), sem("page_copied"), sem("srelu"), sem("ws_done"), sem("ss_done")
        mask_ready = sem("mask_ready")
        mask_out = [sem(f"mask_out{s}") for s in range(3)]
        qpad_done, qs_out = sem("qpad_done"), sem("qs_out")

        staged_jobs = [(n, *CHUNKS[j[1]][j[2]], j[1], j[3]) for n, j in enumerate(jobs) if j[0] == "proj"
                       and CHUNKS[j[1]][j[2]][0] != "ub"]
        stage_no = {s[0]: m for m, s in enumerate(staged_jobs)}
        dmas = lambda kind: 4 if kind in ("iq", "q") else 1

        def slot_written(eng, m):
            eng.wait_ge(out_s[m % 2], 16 * sum(dmas(s[1]) for s in staged_jobs[m % 2:m + 1:2]))

        def slots(h, b):
            tiles = HALVES[h][b]
            return tiles[0] - (HALF if h == 0 else 0), len(tiles)
        score_jobs = [n for n, j in enumerate(jobs) if j[0] == "score"]
        score_no = {n: m for m, n in enumerate(score_jobs)}
        act_no = lambda n: n + 1 - sum(1 for s in staged_jobs if s[0] <= n)
        block = ctx.enter_context(nc.Block())

        @block.sync
        def _(sp):
            w3 = t.w_in[0].rearrange("(c p) n -> p c n", p=128)

            def load_w(n):
                h, c = uses[n]
                if n >= 2:
                    sp.wait_ge(w_lo, n - 1)
                cols = chunk_columns(*CHUNKS[h][c])
                at = 0
                for a, k in cols:
                    sp.dma_start(wst[:, n % 2, :, at:at + k], w3[:, :, a:a + k]).then_inc(w_ld[n % 2], 32 // len(cols))
                    at += k
            load_w(0)
            load_w(1)
            sp.dma_start(ptab[:, :], t.page_table.rearrange("b n -> (b n)").unsqueeze(0)).then_inc(ptab_in, 16)
            sp.wait_ge(ptab_in, 16)
            pool_pages = t.cache_idx_k.shape[1]
            for b in range(NS):
                for g in range(NPAGE):
                    n = b * NPAGE + g
                    v = sp.value_load(ptab[0:1, n:n + 1], min_val=0, max_val=pool_pages - 1)
                    sp.dma_start(ikp[:, n, :], t.cache_idx_k[0, bass.ds(v, 1)].rearrange("o s d -> (o s) d")).then_inc(pages_in, 16)
            def write_masks(g):
                for k, i in enumerate(GROUPS[g]):
                    sp.wait_ge(mask_ready, 3 * g + k + 1)
                    sp.dma_start(t.d_mask[i, :, 0:width(i)], scores[:, k, :].bitcast(bf16)[:, 0:width(i)]).then_inc(mask_out[k], 16)
            for n, (h, c) in enumerate(uses):
                if n + 2 < len(uses):
                    load_w(n + 2)
                if SCORE_AT.get((h, c)):
                    write_masks(SCORE_AT[h, c] - 1)
                if n == NCHUNK:
                    sp.wait_ge(pe_job, lastjob[0, NCHUNK - 1] + 1)
                    for i in range(HALF - 1, -1, -1):
                        sp.dma_start(mem.xh[:, i].rearrange("p c t -> p (c t)").bitcast(f32), t.d_xh[i]).then_inc(x_ld[i], 16)
                        sp.dma_start(mem.xl[:, i].rearrange("p c t -> p (c t)").bitcast(f32), t.d_xl[i]).then_inc(x_ld[i], 16)
                for m, (job, kind, j, hh, b) in enumerate(staged_jobs):
                    if (hh, jobs[job][2]) != (h, c):
                        continue
                    s0, k = slots(hh, b)
                    cols = slice(s0 * P, (s0 + k) * P)
                    tiles = HALVES[hh][b]
                    tok = slice(tiles[0] * P, (tiles[-1] + 1) * P)
                    sp.wait_ge(combined, m + 1)
                    s = m % 2
                    if kind in ("iq", "q"):
                        if kind == "iq" and hh == 1 and j == 0 and b == 0:
                            sp.wait_ge(pe_job, max(x for x in score_jobs if jobs[x][1] in GROUPS[2]) + 1)
                        for part_no, src in enumerate((hst, lst)):
                            for side in range(2):
                                rows = slice(64 * side, 64 * side + 64)
                                to = slice(64 * part_no, 64 * part_no + 64)
                                if kind == "iq":
                                    sp.dma_start(iqs[to, 2 * j + side, cols].bitcast(f32),
                                                 src[rows, s, 0:k * P].bitcast(f32)).then_inc(out_s[s], 16)
                                else:
                                    head = j + 4 * side
                                    sp.dma_start(t.d_q[tiles[0]:tiles[-1] + 1, to, head, :].rearrange("i p t -> p i t"),
                                                 src[rows, s, 0:k * P].bitcast(f32).rearrange("p (i t) -> p i t", t=P))\
                                      .then_inc(out_s[s], 16)
                    else:
                        dst = {"ua": t.d_u, "gc": t.d_gc, "ga": t.d_ga}[kind]
                        sp.dma_start(dst[j, :, tok], ust[:, s, 0:k * P]).then_inc(out_s[s], 16)
                if (h, c) == (0, 5):
                    sp.wait_ge(qpad_done, 8)
                    sp.dma_start(t.d_qs, qpad[:, :]).then_inc(qs_out, 16)
            write_masks(len(GROUPS) - 1)
            slot_written(sp, len(staged_jobs) - 1)
            slot_written(sp, len(staged_jobs) - 2)
            sp.wait_ge(qs_out, 16)
            for k in range(3):
                sp.wait_ge(mask_out[k], 16 * len(GROUPS))

        @block.gpsimd
        def _(pool):
            nc.gpsimd.memset(iqpad[:, :], 0.0).then_inc(zero_pad, 1)
            nc.gpsimd.memset(qpad[:, :], 0.0).then_inc(zero_pad, 1)
            own = slice(LAST * P + SROW, LAST * P + SROW + NS)
            nc.gpsimd.tensor_tensor(out=iks[:, :], in0=mem.ikh[0:64, own].bitcast(f32), in1=mem.ikl[0:64, own].bitcast(f32),
                                    op=ALU.add).then_inc(iks_done, 1)

            def gain(n):
                pool.wait_ge(w_ld[n % 2], 32 * (n // 2 + 1))
                nc.gpsimd.tensor_tensor(out=wst[:, n % 2], in0=wst[:, n % 2],
                                        in1=mem.g[:, :].unsqueeze(2).to_broadcast([128, KC, P]), op=ALU.mult).then_inc(w_mul, 1)

            def low(n):
                pool.wait_ge(w_hi, n + 1)
                nc.gpsimd.tensor_tensor(out=wl[:, n % 2], in0=wst[:, n % 2], in1=wh[:, n % 2].bitcast(f32),
                                        op=ALU.subtract).then_inc(w_lo, 1)
            gain(0)
            low(0)
            gain(1)
            for n, (h, c) in enumerate(uses):
                if n + 1 < len(uses):
                    low(n + 1)
                if n + 2 < len(uses):
                    gain(n + 2)
                for m, (job, kind, j, hh, b) in enumerate(staged_jobs):
                    if (hh, jobs[job][2]) != (h, c):
                        continue
                    k = slots(hh, b)[1] * P
                    s = m % 2
                    pool.wait_ge(staged, m + 1)
                    if kind in ("iq", "q"):
                        nc.gpsimd.tensor_tensor(out=lst[:, s, 0:k], in0=fst[:, s, 0:k], in1=hst[:, s, 0:k].bitcast(f32),
                                                op=ALU.subtract).then_inc(combined, 1)
                    elif kind == "ua":
                        if m >= 2:
                            slot_written(pool, m - 2)
                        nc.gpsimd.tensor_tensor(out=ust[:, s, 0:k], in0=fst[:, s, 0:k], in1=sig[:, b, 0:k],
                                                op=ALU.mult).then_inc(combined, 1)
                    else:
                        nc.gpsimd.tensor_tensor(out=ust[:, s, 0:k], in0=fst[:, s, 0:k], in1=ust[:, s, 0:k],
                                                op=ALU.mult).then_inc(combined, 1)

        @block.scalar
        def _(act):
            def high(n):
                act.wait_ge(w_mul, n + 1)
                if n >= 2:
                    act.wait_ge(pe_job, lastjob[uses[n - 2]] + 1)
                nc.scalar.activation(wh[:, n % 2], wst[:, n % 2], ACT.Copy).then_inc(w_hi, 1)
            high(0)
            for n, job in enumerate(jobs):
                if job[0] == "proj" and job[3] == 0:
                    c = uses.index(job[1:3])
                    if c + 1 < len(uses):
                        high(c + 1)
                act.wait_ge(pe_job, n + 1)
                u = psum[:, n % 4]
                if job[0] == "proj":
                    _, h, c, b = job
                    kind, j = CHUNKS[h][c]
                    k = slots(h, b)[1] * P
                    if kind == "ub":
                        if j or h:
                            act.wait_ge(combined, 1 + max(m for m, s in enumerate(staged_jobs) if s[0] < n and s[1] == "ua"))
                        nc.scalar.activation(sig[:, b, 0:k], u[:, 0:k], ACT.Sigmoid).then_inc(act_job, 1)
                        continue
                    m = stage_no[n]
                    s = m % 2
                    if m >= 2:
                        act.wait_ge(combined, m - 1)
                        slot_written(act, m - 2)
                    if kind in ("iq", "q"):
                        if h == 0 and b == 0:
                            cols = u[:, 2 * P + SROW:2 * P + SROW + NS]
                            act.wait_ge(zero_pad, 2)
                            if kind == "iq":
                                for side in range(2):
                                    nc.scalar.activation(iqpad[:, 2 * j + side::NS * IH + IH], cols[64 * side:64 * side + 64],
                                                         ACT.Copy, scale=0.125)
                            else:
                                for side in range(2):
                                    rows = slice(64 * side, 64 * side + 64)
                                    nc.scalar.activation(qpad[rows, j + 4 * side::NS * NH + NH], cols[rows],
                                                         ACT.Copy, scale=0.125).then_inc(qpad_done, 1)
                        nc.scalar.activation(fst[:, s, 0:k], u[:, 0:k], ACT.Copy, scale=0.125)
                        nc.scalar.activation(hst[:, s, 0:k], u[:, 0:k], ACT.Copy, scale=0.125).then_inc(staged, 1)
                    elif kind == "ua":
                        nc.scalar.activation(fst[:, s, 0:k], u[:, 0:k], ACT.Copy).then_inc(staged, 1)
                    else:
                        nc.scalar.activation(fst[:, s, 0:k], u[:, 0:k], ACT.Copy)
                        nc.scalar.activation(ust[:, s, 0:k], u[:, 0:k], ACT.Sigmoid).then_inc(staged, 1)
                elif job[0] == "score":
                    m = score_no[n]
                    if m >= 2:
                        act.wait_ge(added, m - 1)
                    nc.scalar.activation(r[:, m % 2, 0:job[4]], u[:, 0:job[4]], ACT.Relu).then_inc(act_job, 1)
                elif job[0] == "we":
                    nc.scalar.activation(ws[:, :], u[0:NS * IH, 0:NS], ACT.Copy).then_inc(act_job, 1)
                elif job[0] == "page":
                    nc.scalar.activation(ikTs[:, job[1]], u[0:64, 0:PAST], ACT.Copy).then_inc(act_job, 1)
                elif job[0] == "ss":
                    nc.scalar.activation(r[0:NS * IH, 0, 0:LS], u[0:NS * IH, 0:LS], ACT.Relu).then_inc(act_job, 1)
                elif job[0] == "sw":
                    nc.scalar.activation(sscore[SROW:SROW + NS, :], u[SROW:SROW + NS, 0:LS], ACT.Copy).then_inc(act_job, 1)

        @block.tensor
        def _(pe):
            ident = part(mem.cst, "ident")

            def arrived(n):
                if n in stage_no:
                    pe.wait_ge(staged, stage_no[n] + 1)
                else:
                    pe.wait_ge(act_job, act_no(n))
            for n, job in enumerate(jobs):
                u = psum[:, n % 4]
                if n >= 4:
                    arrived(n - 4)
                if job[0] == "proj":
                    _, h, c, b = job
                    w = uses.index((h, c))
                    s0, k = slots(h, b)
                    if b == 0:
                        pe.wait_ge(w_lo, w + 1)
                    if h == 1 and c == 0:
                        for i in range(s0, s0 + k):
                            pe.wait_ge(x_ld[i], 32)
                    for cc in range(KC):
                        for e, (a, x) in enumerate(((wh, mem.xh), (wh, mem.xl), (wl, mem.xh))):
                            last = nc.tensor.matmul(u[:, 0:k * P], a[:, w % 2, cc, :], x[:, s0:s0 + k, cc, :],
                                                    start=(cc == 0 and e == 0), stop=(cc == KC - 1 and e == 2))
                elif job[0] == "score":
                    _, i, head, a, k = job
                    need = max(m for m, x in enumerate(staged_jobs) if x[0] < n and x[1] == "iq")
                    for m in (need, need - 1):
                        slot_written(pe, m)
                    q = iqs[:, head, (i - (HALF if i >= HALF else 0)) * P:][:, 0:P]
                    for b0 in range(0, k, 512):
                        bn = min(512, k - b0)
                        nc.tensor.matmul(u[:, b0:b0 + bn], q, mem.ikh[:, a + b0:a + b0 + bn], start=True, stop=False)
                        last = nc.tensor.matmul(u[:, b0:b0 + bn], q, mem.ikl[:, a + b0:a + b0 + bn], start=False, stop=True)
                elif job[0] == "we":
                    pe.wait_ge(we_done, 1)
                    last = nc.tensor.matmul(u[0:NS * IH, 0:NS], we[SROW:SROW + NS, :], ident[SROW:SROW + NS, SROW:SROW + NS],
                                            start=True, stop=True)
                elif job[0] == "page":
                    pe.wait_ge(pages_in, 16 * NS * NPAGE)
                    for g in range(NPAGE):
                        last = nc.tensor.matmul(u[0:64, g * PAGE:(g + 1) * PAGE], ikp[:, job[1] * NPAGE + g, :], ident,
                                                start=True, stop=True)
                elif job[0] == "ss":
                    arrived(n - 1)
                    pe.wait_ge(iks_done, 1)
                    for b in range(NS):
                        q = iqpad[:, b * NS * IH:(b + 1) * NS * IH]
                        nc.tensor.matmul(u[0:NS * IH, 0:PAST], q, ikTs[:, b], start=(b == 0), stop=(b == NS - 1))
                    for b in range(NS):
                        q = iqpad[:, b * NS * IH:(b + 1) * NS * IH]
                        last = nc.tensor.matmul(u[0:NS * IH, PAST:LS], q, iks[:, b:b + 1], start=(b == 0), stop=(b == NS - 1))
                elif job[0] == "sw":
                    arrived(n - 1)
                    nc.tensor.matmul(u[SROW:SROW + NS, 0:PAST], ws[:, :], r[0:NS * IH, 0, 0:PAST], start=True, stop=True)
                    last = nc.tensor.matmul(u[SROW:SROW + NS, PAST:LS], ws[:, :], r[0:NS * IH, 0, PAST:LS], start=True, stop=True)
                last.then_inc(pe_job, 1)

        @block.vector
        def _(dve):
            V = nc.vector
            dr = V.drain
            B3 = lambda ap: ap.unsqueeze(1).to_broadcast([128, 2, 3])
            B8 = lambda ap: ap.unsqueeze(2).to_broadcast([128, 3, 8])
            TT = lambda out, a, b, op: V.tensor_tensor(out=out, in0=a, in1=b, op=op)
            own = slice(SROW, SROW + NS)
            TT(we[own, :].rearrange("p (b h) -> p b h", h=IH), part(mem.cst, "e4")[own].rearrange("p (b h) -> p b h", h=IH),
               mem.iw[own, LAST].unsqueeze(1).to_broadcast([NS, NS, IH]), ALU.mult).then_inc(we_done, 1)
            V.memset(flag[:, :], 0.0)
            V.memset(tiny[:, :], TINY)
            V.memset(zero[:, :], 0.0)
            sw_job = jobs.index(("sw", 0))
            m = 0
            for gno, tiles in enumerate(GROUPS):
                for c, i in enumerate(tiles):
                    if gno:
                        dve.wait_ge(mask_out[c], 16 * gno)
                    for head in range(IH):
                        for a, n in pieces(i):
                            dve.wait_ge(act_job, act_no(score_jobs[m]))
                            if head:
                                dve.wait_ge(added, m + 1 - len(pieces(i)))
                            w = mem.iw[:, i, head:head + 1]
                            o = scores[:, c, a:a + n]
                            if head == 0:
                                V.tensor_scalar(o, r[:, m % 2, 0:n], w, None, ALU.mult).then_inc(added, 1)
                            else:
                                V.scalar_tensor_tensor(o, r[:, m % 2, 0:n], w, o, ALU.mult, ALU.add).then_inc(added, 1)
                            m += 1
                dr()
                for c, i in enumerate(tiles):
                    V.tensor_reduce(amax[:, c:c + 1], scores[:, c, 0:width(i)], AX.X, ALU.max, apply_absolute_value=True)
                    V.tensor_copy(kt[:, c:c + 1], part(mem.cst, "kk")[:, i:i + 1])
                dr()
                for c, i in enumerate(tiles):
                    k = width(i) - i * P
                    o = scores[:, c, i * P:i * P + k]
                    TT(o, o, part(mem.cst, "causal")[:, 0:k], ALU.add)
                    if i == LAST:
                        dve.wait_ge(act_job, act_no(sw_job))
                        dr()
                        V.tensor_reduce(amax[own, c:c + 1], sscore[own, :], AX.X, ALU.max, apply_absolute_value=True)
                        V.memset(scores[own, c, :], NEG)
                        dr()
                        V.tensor_copy(scores[own, c, 0:LS], sscore[own, :])
                dr()
                V.tensor_scalar(hi[:, 0, :], amax[:, :], 1.0001, 1e-30, ALU.mult, ALU.add)
                V.memset(hi[:, 1, :], 0.0)
                V.memset(lo[:, 1, :], float(LP))
                V.tensor_scalar(k4[:, :], kt[:, :], -4.0, None, ALU.add)
                for c, i in enumerate(tiles):
                    for o in range(4):
                        V.max(m8s[:, c, o, :], scores[:, c, 8 * o:width(i):32])
                dr()
                V.tensor_scalar(lo[:, 0, :], hi[:, 0, :], -1.0, None, ALU.mult)
                V.tensor_reduce(sum4[:, :], m8s[:, :, :, 7], AX.X, ALU.add)
                V.tensor_reduce(slope[:, :], m8s[:, :, :, 3], AX.X, ALU.add)
                dr()
                TT(slope[:, :], slope[:, :], sum4[:, :], ALU.subtract)
                V.tensor_scalar(T[:, 0, :], sum4[:, :], 0.25, None, ALU.mult)
                dr()
                V.tensor_scalar(slope[:, :], slope[:, :], 0.25 / 128, None, ALU.mult)

                def inside():
                    TT(gef[:, :], T[:, 0, :], lo[:, 0, :], ALU.is_le)
                    TT(num[:, :], T[:, 0, :], hi[:, 0, :], ALU.is_ge)
                    TT(jj[:, :], lo[:, 0, :], hi[:, 0, :], ALU.add)
                    dr()
                    TT(fall[:, :], gef[:, :], num[:, :], ALU.max)
                    V.tensor_scalar(jj[:, :], jj[:, :], 0.5, None, ALU.mult)
                    dr()
                    V.copy_predicated(out=T[:, 0, :], mask=fall[:, :], data=jj[:, :])
                    dr()

                def count(at, into):
                    for c, i in enumerate(tiles):
                        V.tensor_scalar(hit[:, 0:width(i)], scores[:, c, 0:width(i)], at[:, c:c + 1] if len(at.shape) == 2 else at[:, c], 0.0,
                                        ALU.is_ge, ALU.add, accum_out=into[:, c:c + 1])
                        dr()

                def narrow():
                    count(T[:, 0, :], T[:, 1, :])
                    TT(ge[:, :], T[:, 1, :], kt[:, :], ALU.is_ge)
                    TT(lt[:, :], T[:, 1, :], kt[:, :], ALU.is_lt)
                    dr()
                    V.copy_predicated(out=lo[:, :, :], mask=B3(ge[:, :]), data=T[:, :, :])
                    V.copy_predicated(out=hi[:, :, :], mask=B3(lt[:, :]), data=T[:, :, :])
                    dr()
                inside()
                narrow()
                V.tensor_scalar(gef[:, :], ge[:, :], 8.0, -4.0, ALU.mult, ALU.add)
                TT(num[:, :], T[:, 1, :], k4[:, :], ALU.subtract)
                dr()
                TT(num[:, :], num[:, :], gef[:, :], ALU.add)
                dr()
                TT(num[:, :], num[:, :], slope[:, :], ALU.mult)
                dr()
                TT(T[:, 0, :], T[:, 0, :], num[:, :], ALU.add)
                dr()
                inside()
                narrow()
                def between():
                    TT(gap[:, :, :], lo[:, :, :], hi[:, :, :], ALU.subtract)
                    TT(num[:, :], lo[:, 1, :], k4[:, :], ALU.subtract)
                    dr()
                    V.reciprocal(jj[:, :], gap[:, 1, :])
                    dr()
                    TT(num[:, :], num[:, :], jj[:, :], ALU.mult)
                    dr()
                    V.tensor_scalar(num[:, :], num[:, :], 0.75, 0.125, ALU.mult, ALU.add)
                    dr()
                    TT(num[:, :], num[:, :], gap[:, 0, :], ALU.mult)
                    dr()
                    TT(T[:, 0, :], lo[:, 0, :], num[:, :], ALU.subtract)
                    dr()
                for op_lo, op_hi, guess in ((ALU.is_le, ALU.is_gt, tiny), (ALU.is_lt, ALU.is_equal, zero)):
                    between()
                    V.tensor_scalar(gef[:, :], lo[:, 0, :], 0.0, None, op_lo)
                    dr()
                    V.scalar_tensor_tensor(upd[:, :], hi[:, 0, :], TINY, gef[:, :], op_hi, ALU.mult)
                    dr()
                    V.copy_predicated(out=T[:, 0, :], mask=upd[:, :], data=guess[:, :])
                    dr()
                    narrow()
                with V.Fori(0, SEARCH[gno] - 4):
                    between()
                    narrow()

                def eight_below():
                    for c, i in enumerate(tiles):
                        s = scores[:, c, 0:width(i)]
                        V.tensor_scalar(run[:, 0:width(i)], s, hi[:, 0, c:c + 1], NEG, ALU.is_ge, ALU.mult)
                        dr()
                        TT(run[:, 0:width(i)], run[:, 0:width(i)], s, ALU.add)
                        dr()
                        V.max(m8[:, c, :], run[:, 0:width(i)])
                        dr()
                    TT(jj[:, :], kt[:, :], hi[:, 1, :], ALU.subtract)
                    TT(num[:, :], lo[:, 0, :], m8[:, :, 7], ALU.is_ge)
                    dr()
                    V.tensor_scalar(more[:, :], jj[:, :], 8.0, None, ALU.is_gt)
                    dr()
                    TT(more[:, :], more[:, :], num[:, :], ALU.is_gt)
                    dr()
                    V.tensor_reduce(flag[:, 0:1], more[:, :], AX.X, ALU.max)
                    dr()
                    V.transpose(flagT[:, :], flag[:, :])
                    dr()
                    V.reduce_max(flag1[:, :], flagT[:, :], AX.X)
                    dr()
                    V.tensor_copy(flagi[:, :], flag1[:, :])
                    dr()
                    return sum(V.value_load(flagi[32 * q:32 * q + 1, 0:1], min_val=0, max_val=1) for q in range(4))
                left = V.alloc_register(f"left{gno}")
                V.reg_mov(left, eight_below())
                with V.While(left):
                    V.tensor_copy(T[:, 0, :], m8[:, :, 7])
                    dr()
                    narrow()
                    V.reg_mov(left, eight_below())
                V.tensor_scalar(jc[:, :], jj[:, :], 8.0, -1.0, ALU.min, ALU.add)
                dr()
                TT(hot[:, :, :], part(mem.cst, "iota").rearrange("p (c e) -> p c e", e=8), B8(jc[:, :]), ALU.is_equal)
                dr()
                TT(hot[:, :, :], hot[:, :, :], m8[:, :, :], ALU.mult)
                dr()
                V.tensor_reduce(T[:, 0, :], hot[:, :, :], AX.X, ALU.add)
                dr()
                TT(hot[:, :, :], m8[:, :, :], B8(T[:, 0, :]), ALU.is_gt)
                dr()
                V.tensor_reduce(above[:, :], hot[:, :, :], AX.X, ALU.add)
                dr()
                TT(tie_room[:, :], jj[:, :], above[:, :], ALU.subtract)
                dr()
                for c, i in enumerate(tiles):
                    w = width(i)
                    s, e, k = scores[:, c, 0:w], hit[:, 0:w], run[:, 0:w]
                    V.tensor_scalar(e, s, T[:, 0, c:c + 1], None, ALU.is_equal)
                    dr()
                    V.tensor_tensor_scan(k, e, e, 0.0, ALU.add, ALU.max)
                    dr()
                    V.scalar_tensor_tensor(k, k, tie_room[:, c:c + 1], e, ALU.is_le, ALU.mult)
                    dr()
                    V.scalar_tensor_tensor(k, s, T[:, 0, c:c + 1], k, ALU.is_gt, ALU.add)
                    dr()
                    V.tensor_scalar(scores[:, c, :].bitcast(bf16)[:, 0:w], k, -1.0, -NEG, ALU.add, ALU.mult).then_inc(mask_ready, 1)
                    dr()

TILE_ORDER = [LAST] + list(range(LAST - 1, -1, -1))
HALFW = NT * P // 2


def attend_and_convolve(nc, t, mem):
    pairs = [(i, j) for i in TILE_ORDER for j in range(GRP)]
    NP_ = len(pairs)
    ujobs = [("bias", 0)] + [("kT", i, n) for i in range(NT) for n in range(NKV)] + [("S", 0)]
    for p, (i, j) in enumerate(pairs):
        ujobs += [("L", p, side, a, k) for side in range(2) for a, k in pieces(i)]
    u_no = {j: n for n, j in enumerate(ujobs)}
    nblk = lambda i: -(-width(i) // P)
    groups = lambda i: [(b, min(2, nblk(i) - b)) for b in range(0, nblk(i), 2)]
    ptjobs = [("own", 0)] + [("page", b) for b in range(NS)] + [("sT", 0), ("sP", 0)]
    for p, (i, j) in enumerate(pairs):
        ptjobs += [("T", p, b, k) for b, k in groups(i)]
        if j == GRP - 1:
            ptjobs.append(("R", p))
    pt_no = {j: n for n, j in enumerate(ptjobs)}
    tjobs = [j for j in ptjobs if j[0] == "T"]
    t_no = {j: n for n, j in enumerate(tjobs)}
    pv_after = lambda p: NS + 1 + sum(len(groups(i)) for i, _ in pairs[:p + 1])
    tile_no = {i: n for n, i in enumerate(TILE_ORDER)}
    band0 = lambda i: max(0, (i - 1) * P)
    dconv = [(c, h) for h in range(2) for c in range(3)]
    pconv = [(3, h) for h in range(2)]
    per_pair = -(-len(dconv) * TAPS // (NP_ - 4))
    per_tile = -(-len(pconv) * TAPS // (NT - 1))
    LW = NT * P
    with ExitStack() as ctx:
        sb = lambda n, s, d=f32: ctx.enter_context(nc.sbuf_tensor(n, s, d))
        sem = lambda n: ctx.enter_context(nc.semaphore(n))
        kh = sb("kh", [128, NKV, LW], f32r)
        kl = sb("kl", [128, NKV, LW], f32r)
        vs = sb("vs", [128, NT, 128])
        L = sb("L", [128, 4, LW])
        kn = sb("kn", [128, 2, NKV, 2, HD])
        band = sb("band", [128, NH, 2 * P])
        bm = sb("bm", [128, 2, NH, 2 * P])
        mask = sb("mask", [128, 2, LP], bf16)
        qt = sb("qt", [128, 2, NH, P], f32r)
        gate = sb("gate", [128, 2, GRP, P])
        pts = sb("pts", [128, 3, 4 * P])
        rb = sb("rb", [128, 2, GRP, P])
        mix = sb("mix", [128, 2, GRP, P])
        es = sb("es", [128, 2, NH])
        ri = sb("ri", [128, 2, NH])
        rx = sb("rx", [128, GRP, 2, HD])
        mx = sb("mx", [128, 4, 6])
        nm = sb("nm", [128, 4])
        bc = sb("bc", [32, BANDX + LS])
        rel = sb("rel", [32, NH])
        relrep = sb("relrep", [32, NS, NH])
        rrow = sb("rrow", [NH, BANDX])
        qp = sb("qp", [128, NS, NS * NH])
        own = sb("own", [NS, 2 * 128])
        ownT = sb("ownT", [128, NS])
        m16b = sb("m16b", [NS, LS], bf16)
        m16 = sb("m16", [NS, LS])
        sS = sb("sS", [NS * NH, LS])
        smx, ssum = sb("smx", [NS * NH, 1]), sb("ssum", [NS * NH, 1])
        spick = sb("spick", [NS * NH, NS])
        sown = sb("sown", [NS, NS * NH])
        som = sb("som", [128, GRP, NS])
        cu = sb("cu", [128, 2, HALFW + TAPS - 1])
        cy = sb("cy", [128, 2, HALFW])
        pu = sb("pu", [128, HALFW + TAPS - 1])
        py = sb("py", [128, HALFW])
        ptmp = sb("ptmp", [128, HALFW])
        cw = sb("cw", [128, CC, TAPS])
        cb = sb("cb", [128, CC])
        ptab = sb("ptab2", [1, NS * NPAGE], i32)
        U = ctx.enter_context(nc.psum_tensor("psU", [128, 2, UNIT], f32))
        PT = ctx.enter_context(nc.psum_tensor("psT", [128, 2, 512], f32))
        OT = ctx.enter_context(nc.psum_tensor("psO", [128, 2, 512], f32))
        kpage = L[:, 0:2, :].rearrange("p a b -> p (a b)")[:, 0:NS * NPAGE * 128].rearrange("p (n d) -> p n d", d=128)
        vpage = L[:, 2:4, :].rearrange("p a b -> p (a b)")[:, 0:NS * NPAGE * 128].rearrange("p (n d) -> p n d", d=128)

        kn_in = [sem(f"kn_in{s}") for s in range(2)]
        c_in, r_out, band_in, v_in, s_in, pg_in = sem("c_in2"), sem("r_out"), sem("band_in"), sem("v_in"), sem("s_in"), sem("pg_in")
        pt_in = sem("pt_in2")
        q_in = [sem(f"q_in{s}") for s in range(2)]
        m_in = [sem(f"m_in{s}") for s in range(2)]
        g_in = [sem(f"g_in{s}") for s in range(2)]
        pe_u, dve_u, kh_done = sem("pe_u"), sem("dve_u"), sem("kh_done")
        pe_pt, act_pt, pe_pv = sem("pe_pt"), sem("act_pt"), sem("pe_pv")
        nm_ready, exp_done, ri_ready, bm_ready, tile_done = sem("nm_ready"), sem("exp_done"), sem("ri_ready"), sem("bm_ready"), sem("tile_done")
        mix_out = [sem(f"mix_out{s}") for s in range(2)]
        rrow_done, rel_done, m16_done, s_neg, s_exp, s_norm = sem("rrow_done"), sem("rel_done"), sem("m16_done"), sem("s_neg"), sem("s_exp"), sem("s_norm")
        spick_done, som_done, pad_done = sem("spick_done"), sem("som_done"), sem("pad_done")
        cu_in = [sem(f"cu_in{s}") for s in range(2)]
        cy_out = [sem(f"cy_out{s}") for s in range(2)]
        pu_in, py_out, conv_done, pconv_done, cz, pstep, cw_in = sem("pu_in"), sem("py_out"), sem("conv_done"), sem("pconv_done"), sem("cz"), sem("pstep"), sem("cw_in")
        block = ctx.enter_context(nc.Block())

        def tile_of_step(p):
            return pairs[p][0] if 0 <= p < NP_ and pairs[p][1] == GRP - 1 else None

        @block.sync
        def _(sp):
            sp.dma_start(bc[:, :], t.consts[0:32, NCONST:NCONST + BANDX + LS]).then_inc(c_in, 16)
            sp.dma_start(rel[:, :], t.rel_bias).then_inc(c_in, 16)

            def load_k(i):
                n = P if i < LAST else LREM
                if i >= 2:
                    sp.wait_ge(pe_u, u_no["kT", i - 2, NKV - 1] + 1)
                for d in range(2):
                    sp.dma_start(kn[0:n, i % 2, :, d, :], t.nk_p[0, 0, i * P:i * P + n]).then_inc(kn_in[i % 2], 16)
            load_k(0)
            load_k(1)
            for c in range(CC):
                sp.dma_start(cw[:, c, :], t.conv_w[0][:, c * P:(c + 1) * P].rearrange("k p -> p k"),
                             allow_slow_non_contiguous=True).then_inc(cw_in, 16)
            sp.dma_start(cb[:, :], t.conv_b[0].rearrange("(c p) -> p c", p=128), allow_slow_non_contiguous=True).then_inc(cw_in, 16)
            sp.dma_start(qp[:, :, :].rearrange("p a b -> p (a b)"), t.d_qs).then_inc(s_in, 16)
            sp.dma_start(own[:, 0:128], t.nk_s[0, :, 0].rearrange("b n d -> b (n d)")).then_inc(s_in, 16)
            sp.dma_start(own[:, 128:256], t.nv_s[0, :, 0].rearrange("b n d -> b (n d)")).then_inc(s_in, 16)
            sp.dma_start(m16b[:, :], t.d_mask[LAST, SROW:SROW + NS, 0:LS]).then_inc(s_in, 16)
            sp.dma_start(ptab[:, :], t.page_table.rearrange("b n -> (b n)").unsqueeze(0)).then_inc(pt_in, 16)
            sp.wait_ge(pt_in, 16)
            for b in range(NS):
                for g in range(NPAGE):
                    n = b * NPAGE + g
                    v = sp.value_load(ptab[0:1, n:n + 1], min_val=0, max_val=t.cache_k.shape[1] - 1)
                    sp.dma_start(kpage[:, n, :], t.cache_k[0, bass.ds(v, 1)].rearrange("o s n d -> (o s) (n d)")).then_inc(pg_in, 16)
                    sp.dma_start(vpage[:, n, :], t.cache_v[0, bass.ds(v, 1)].rearrange("o s n d -> (o s) (n d)")).then_inc(pg_in, 16)

            def load_tile(n):
                i = TILE_ORDER[n]
                s = n % 2
                if n >= 2:
                    sp.wait_ge(tile_done, n - 1)
                sp.dma_start(qt[:, s].bitcast(f32), t.d_q[i]).then_inc(q_in[s], 16)
                sp.dma_start(gate[:, s], t.d_ga[:, :, i * P:(i + 1) * P].rearrange("c p t -> p c t")).then_inc(g_in[s], 16)
                if i >= 2:
                    sp.dma_start(mask[:, s, 0:width(i)], t.d_mask[i, :, 0:width(i)]).then_inc(m_in[s], 16)

            def load_u(e, units, dst, s):
                c, h = units[e]
                if h == 0:
                    sp.dma_start(dst[:, TAPS - 1:], t.d_u[c, :, 0:HALFW]).then_inc(s, 16)
                else:
                    sp.dma_start(dst[:, :], t.d_u[c, :, HALFW - (TAPS - 1):2 * HALFW]).then_inc(s, 16)
            load_tile(0)
            load_tile(1)
            for i in range(2, NT):
                load_k(i)
            sp.wait_ge(rrow_done, 1)
            sp.dma_start(t.d_r.rearrange("t h x -> h t x"), rrow[:, :].unsqueeze(1).to_broadcast([NH, P, BANDX])).then_inc(r_out, 16)
            sp.wait_ge(r_out, 16)
            sp.dma_start(band[:, :, :], bass.AP(t.d_r.tensor, P - 1, [[NH * BANDX - 1, P], [BANDX, NH], [1, 2 * P]])).then_inc(band_in, 16)
            sp.dma_start(vs[:, 0:LAST, :], t.nv_p[0, 0, 0:LAST * P].rearrange("(i p) n d -> p i (n d)", p=P)).then_inc(v_in, 16)
            sp.dma_start(vs[0:LREM, LAST, :], t.nv_p[0, 0, LAST * P:LP].rearrange("p n d -> p (n d)")).then_inc(v_in, 16)
            sp.wait_ge(cz, 2)
            load_u(0, dconv, cu[:, 0], cu_in[0])
            load_u(1, dconv, cu[:, 1], cu_in[1])
            load_u(0, pconv, pu[:, :], pu_in)
            dunit = punit = 0
            for p in range(NP_ + 3):
                while dunit < len(dconv) and (p - 1) * per_pair >= (dunit + 1) * TAPS:
                    sp.wait_ge(conv_done, dunit + 1)
                    c, h = dconv[dunit]
                    sp.dma_start(t.d_y[c, :, h * HALFW:(h + 1) * HALFW], cy[:, dunit % 2]).then_inc(cy_out[dunit % 2], 16)
                    if dunit + 2 < len(dconv):
                        load_u(dunit + 2, dconv, cu[:, dunit % 2], cu_in[dunit % 2])
                    dunit += 1
                if tile_of_step(p - 2) is not None:
                    n = tile_no[tile_of_step(p - 2)]
                    sp.wait_ge(tile_done, n + 1)
                    sp.dma_start(t.d_mix[TILE_ORDER[n]], mix[:, n % 2]).then_inc(mix_out[n % 2], 16)
                    if n + 2 < NT:
                        load_tile(n + 2)
                    while punit < len(pconv) and n + 1 >= (punit + 1) * TAPS // per_tile:
                        sp.wait_ge(pconv_done, punit + 1)
                        c, h = pconv[punit]
                        sp.dma_start(t.d_y[c, :, h * HALFW:(h + 1) * HALFW], py[:, :]).then_inc(py_out, 16)
                        if punit + 1 < len(pconv):
                            load_u(punit + 1, pconv, pu[:, :], pu_in)
                        punit += 1
            while dunit < len(dconv):
                sp.wait_ge(conv_done, dunit + 1)
                c, h = dconv[dunit]
                sp.dma_start(t.d_y[c, :, h * HALFW:(h + 1) * HALFW], cy[:, dunit % 2]).then_inc(cy_out[dunit % 2], 16)
                dunit += 1
            while punit < len(pconv):
                sp.wait_ge(pconv_done, punit + 1)
                c, h = pconv[punit]
                sp.dma_start(t.d_y[c, :, h * HALFW:(h + 1) * HALFW], py[:, :]).then_inc(py_out, 16)
                punit += 1
            for s in range(2):
                sp.wait_ge(mix_out[s], 16 * len(TILE_ORDER[s::2]))
                sp.wait_ge(cy_out[s], 16 * len(dconv[s::2]))
            sp.wait_ge(py_out, 16 * len(pconv))

        @block.gpsimd
        def _(pool):
            G = nc.gpsimd
            G.memset(cu[:, 0, 0:TAPS - 1], 0.0)
            G.memset(cu[:, 1, 0:TAPS - 1], 0.0).then_inc(cz, 1)
            G.memset(pu[:, 0:TAPS - 1], 0.0).then_inc(cz, 1)
            steps = [0]

            def chained(ins):
                steps[0] += 1
                ins.then_inc(pstep, 1)
                pool.wait_ge(pstep, steps[0])
            pool.wait_ge(cw_in, 80)
            tap = 0

            def conv_tap(tap):
                e, k = divmod(tap, TAPS)
                c, h = pconv[e]
                w = cw[:, c, k:k + 1]
                if k == 0:
                    pool.wait_ge(pu_in, 16 * (e + 1))
                    if e:
                        pool.wait_ge(py_out, 16 * e)
                    chained(G.tensor_scalar(py[:, :], pu[:, 0:HALFW], w, cb[:, c:c + 1], ALU.mult, ALU.add))
                else:
                    chained(G.tensor_scalar(ptmp[:, :], pu[:, k:k + HALFW], w, 0.0, ALU.mult, ALU.add))
                    chained(G.tensor_tensor(out=py[:, :], in0=py[:, :], in1=ptmp[:, :], op=ALU.add))
                if k == TAPS - 1:
                    G.sem_inc(pconv_done, 1)
            pool.wait_ge(band_in, 16)
            for n, i in enumerate(TILE_ORDER):
                s = n % 2
                a, k = band0(i), width(i) - band0(i)
                j0 = a - (i - 1) * P
                if n >= 2:
                    pool.wait_ge(tile_done, n - 1)
                if i >= 2:
                    pool.wait_ge(m_in[s], 16 * (n // 2 + 1))
                else:
                    chained(G.memset(mask[:, s, 0:P], 0.0))
                    chained(G.tensor_copy(mask[:, s, i * P:(i + 1) * P], part(mem.cst, "causal")))
                G.tensor_tensor(out=bm[:, s, :, 0:k], in0=band[:, :, j0:j0 + k],
                                in1=mask[:, s, a:a + k].unsqueeze(1).to_broadcast([128, NH, k]), op=ALU.add).then_inc(bm_ready, 1)
                for _ in range(per_tile):
                    if tap < len(pconv) * TAPS:
                        conv_tap(tap)
                        tap += 1
            while tap < len(pconv) * TAPS:
                conv_tap(tap)
                tap += 1

        @block.scalar
        def _(act):
            A = nc.scalar

            def evac(job, out, src):
                act.wait_ge(pe_pt, pt_no[job] + 1)
                A.activation(out, src, ACT.Copy).then_inc(act_pt, 1)
            act.wait_ge(c_in, 32)
            A.activation(relrep[:, :, :], rel[:, :].unsqueeze(1).to_broadcast([32, NS, NH]), ACT.Copy).then_inc(rel_done, 1)
            for i in range(NT):
                for n in range(NKV):
                    job = u_no["kT", i, n]
                    k = P if i < LAST else LREM
                    act.wait_ge(pe_u, job + 1)
                    A.activation(kh[:, n, i * P:i * P + k], U[:, job % 2, 0:k], ACT.Copy).then_inc(kh_done, 1)
            act.wait_ge(s_in, 64)
            A.activation(m16[:, :], m16b[:, :], ACT.Copy).then_inc(m16_done, 1)
            evac(("own", 0), ownT[:, :], PT[:, 0, 0:NS])
            for b in range(NS):
                if b >= 3:
                    act.wait_ge(pe_pv, b - 2)
                evac(("page", b), pts[:, b % 3, :], PT[:, pt_no["page", b] % 2, :])
            act.wait_ge(s_neg, 1)
            A.activation(sS[:, :], sS[:, :], ACT.Exp, bias=smx[:, :], accum_out=ssum[:, :]).then_inc(s_exp, 1)
            act.wait_ge(pe_pv, NS)
            evac(("sT", 0), pts[:, 0, 0:256], PT[:, pt_no["sT", 0] % 2, 0:256])
            evac(("sP", 0), sown[:, :], PT[0:NS, pt_no["sP", 0] % 2, 0:NS * NH])

            def exps(p):
                i, j = pairs[p]
                for side in range(2):
                    act.wait_ge(nm_ready, 2 * p + side + 1)
                    b = (2 * p + side) % 4
                    A.activation(L[:, b, 0:width(i)], L[:, b, 0:width(i)], ACT.Exp, bias=nm[:, b:b + 1],
                                 accum_out=es[:, tile_no[i] % 2, j + 4 * side:j + 4 * side + 1]).then_inc(exp_done, 1)
            exps(0)
            for p, (i, j) in enumerate(pairs):
                for b, k in groups(i):
                    job = ("T", p, b, k)
                    n = t_no[job]
                    act.wait_ge(pe_pv, NS + 1 + max(0, n - 2))
                    kk = min(P, width(i) - b * P)
                    m = 2 * k * P
                    evac(job, pts[:, n % 3, 0:m], PT[:, pt_no[job] % 2, 0:m])
                if j == GRP - 1:
                    n = tile_no[i]
                    if n >= 2:
                        act.wait_ge(tile_done, n - 1)
                    evac(("R", p), rb[:, n % 2].rearrange("p c t -> p (c t)"), PT[:, pt_no["R", p] % 2, :])
                if p + 1 < NP_:
                    if j == GRP - 1 and tile_no[i] >= 1:
                        act.wait_ge(ri_ready, tile_no[i])
                    exps(p + 1)

        @block.vector
        def _(dve):
            V = nc.vector
            dr = V.drain
            TT = lambda out, a, b, op: V.tensor_tensor(out=out, in0=a, in1=b, op=op)
            dve.wait_ge(pe_u, 1)
            V.tensor_copy(rrow[:, :], U[0:NH, 0, 0:BANDX]).then_inc(dve_u, 1)
            dr().then_inc(rrow_done, 1)
            for i in range(NT):
                for n in range(NKV):
                    job = u_no["kT", i, n]
                    k = P if i < LAST else LREM
                    dve.wait_ge(kh_done, NKV * i + n + 1)
                    TT(kl[:, n, i * P:i * P + k], U[:, job % 2, 0:k], kh[:, n, i * P:i * P + k].bitcast(f32), ALU.subtract).then_inc(dve_u, 1)
            job = u_no["S", 0]
            dve.wait_ge(pe_u, job + 1)
            V.tensor_copy(sS[:, :], U[0:NS * NH, job % 2, 0:LS]).then_inc(dve_u, 1)
            dr()
            V.tensor_reduce(smx[:, :], sS[:, :], AX.X, ALU.max, negate=True).then_inc(s_neg, 1)
            dve.wait_ge(s_exp, 1)
            V.reciprocal(ssum[:, :], ssum[:, :])
            dr()
            V.tensor_scalar(sS[:, :], sS[:, :], ssum[:, 0:1], None, ALU.mult).then_inc(s_norm, 1)
            dr()
            V.tensor_scalar(spick[:, :], part(mem.cst, "e8t")[0:NS * NH, 0:NS], sS[:, PAST:LS], None, ALU.mult).then_inc(spick_done, 1)
            dve.wait_ge(pe_pv, NS + 1)
            for side in range(2):
                rows = slice(64 * side, 64 * side + 64)
                V.tensor_copy(som[rows, :, :], OT[rows, 0, 0:NS * NH].rearrange("p (b g h) -> p g h b", b=NS, g=2)[:, side])
            V.memset(L[:, :, LP:LW], 0.0).then_inc(pad_done, 1)
            dr().then_inc(som_done, 1)
            tap = 0

            def conv_tap(tap):
                e, k = divmod(tap, TAPS)
                c, h = dconv[e]
                w = cw[:, c, k:k + 1]
                y, u = cy[:, e % 2], cu[:, e % 2]
                if k == 0:
                    dve.wait_ge(cu_in[e % 2], 16 * (e // 2 + 1))
                    if e >= 2:
                        dve.wait_ge(cy_out[e % 2], 16 * (e // 2))
                    V.tensor_scalar(y, u[:, 0:HALFW], w, cb[:, c:c + 1], ALU.mult, ALU.add)
                else:
                    V.scalar_tensor_tensor(y, u[:, k:k + HALFW], w, y, ALU.mult, ALU.add)
                if k == TAPS - 1:
                    dr().then_inc(conv_done, 1)
                else:
                    dr()

            def finish(n):
                i = TILE_ORDER[n]
                s = n % 2
                dve.wait_ge(act_pt, pt_no["R", (n + 1) * GRP - 1] + 1)
                dve.wait_ge(g_in[s], 16 * (n // 2 + 1))
                if n >= 2:
                    dve.wait_ge(mix_out[s], 16 * (n // 2))
                TT(rb[:, s], rb[:, s], gate[:, s], ALU.mult)
                dr()
                dve.wait_ge(pe_pv, pv_after((n + 1) * GRP - 1))
                TT(mix[:, s], OT[:, s, :].rearrange("p (c t) -> p c t", t=P), rb[:, s], ALU.mult)
                if i == LAST:
                    dr()
                    TT(mix[:, s, :, SROW:SROW + NS], som[:, :, :], gate[:, s, :, SROW:SROW + NS], ALU.mult)
                dr().then_inc(tile_done, 1)

            def invert(n):
                V.reciprocal(ri[:, n % 2, :], es[:, n % 2, :])
                dr()
                V.tensor_copy(rx[:, :, :, :], ri[:, n % 2, :].rearrange("p (a g) -> p g a", a=NKV).unsqueeze(3)
                              .to_broadcast([128, GRP, NKV, HD])).then_inc(ri_ready, 1)
            dve.wait_ge(cw_in, 80)
            for p, (i, j) in enumerate(pairs):
                n = tile_no[i]
                s = n % 2
                if j == 0:
                    dve.wait_ge(bm_ready, n + 1)
                    if i >= 2:
                        dve.wait_ge(m_in[s], 16 * (n // 2 + 1))
                if p >= 2:
                    dve.wait_ge(pe_pv, pv_after(p - 2))
                for side in range(2):
                    head, b = j + 4 * side, (2 * p + side) % 4
                    m = 0
                    for a, k in pieces(i):
                        job = u_no["L", p, side, a, k]
                        dve.wait_ge(pe_u, job + 1)
                        bs = band0(i)
                        spans = [(a, min(a + k, bs), mask[:, s, :]), (max(a, bs), a + k, None)]
                        spans = [x for x in spans if x[0] < x[1]]
                        for x0, x1, far in spans:
                            in1 = mask[:, s, x0:x1] if far is not None else bm[:, s, head, x0 - bs:x1 - bs]
                            last = V.tensor_tensor_reduce(out=L[:, b, x0:x1], in0=U[:, job % 2, x0 - a:x1 - a], in1=in1,
                                                          scale=1.0, scalar=3 * NEG, op0=ALU.add, op1=ALU.max, accum_out=mx[:, b, m:m + 1])
                            m += 1
                        last.then_inc(dve_u, 1)
                    dr()
                    V.tensor_reduce(nm[:, b:b + 1], mx[:, b, 0:m], AX.X, ALU.max, negate=True).then_inc(nm_ready, 1)
                if p and pairs[p - 1][1] == GRP - 1:
                    nn = tile_no[pairs[p - 1][0]]
                    dve.wait_ge(exp_done, 2 * p)
                    invert(nn)
                if p >= 2 and pairs[p - 2][1] == GRP - 1:
                    finish(tile_no[pairs[p - 2][0]])
                for _ in range(per_pair):
                    if tap < len(dconv) * TAPS:
                        conv_tap(tap)
                        tap += 1
            dve.wait_ge(exp_done, 2 * NP_)
            invert(NT - 1)
            finish(NT - 1)
            while tap < len(dconv) * TAPS:
                conv_tap(tap)
                tap += 1

        @block.tensor
        def _(pe):
            ident = part(mem.cst, "ident")
            T = nc.tensor

            def take_u(job):
                n = u_no[job]
                if n >= 2:
                    pe.wait_ge(dve_u, n - 1)
                return U[:, n % 2]

            def take_pt(job):
                n = pt_no[job]
                if n >= 2:
                    pe.wait_ge(act_pt, n - 1)
                return PT[:, n % 2]
            pe.wait_ge(c_in, 32)
            T.matmul(take_u(("bias", 0))[0:NH, 0:BANDX], rel[:, :], bc[:, 0:BANDX], start=True, stop=True).then_inc(pe_u, 1)
            for i in range(NT):
                pe.wait_ge(kn_in[i % 2], 32 * (i // 2 + 1))
                for n in range(NKV):
                    k = P if i < LAST else LREM
                    T.transpose(take_u(("kT", i, n))[:, 0:k], kn[0:k, i % 2, n].rearrange("p a d -> p (a d)"), ident[0:k, 0:k]).then_inc(pe_u, 1)
            pe.wait_ge(s_in, 64)
            T.transpose(take_pt(("own", 0))[:, 0:NS], own[:, 0:128], ident[0:NS, 0:NS]).then_inc(pe_pt, 1)
            pe.wait_ge(pg_in, 32 * NS * NPAGE)
            S = take_u(("S", 0))

            def page(b):
                pt = take_pt(("page", b))
                for g in range(NPAGE):
                    last = T.transpose(pt[:, g * P:(g + 1) * P], kpage[:, b * NPAGE + g, :], ident)
                last.then_inc(pe_pt, 1)
            page(0)
            for b in range(NS):
                if b + 1 < NS:
                    page(b + 1)
                pe.wait_ge(act_pt, pt_no["page", b] + 1)
                T.matmul(S[0:NS * NH, 0:PAST], qp[:, b, :], pts[:, b % 3, :], start=(b == 0), stop=False).then_inc(pe_pv, 1)
            pe.wait_ge(m16_done, 1)
            pe.wait_ge(rel_done, 1)
            e8 = part(mem.cst, "e8")[0:NS, :]
            rr = relrep[:, :, :].rearrange("p b h -> p (b h)")
            T.matmul(S[0:NS * NH, 0:PAST], e8, m16[:, 0:PAST], start=False, stop=False)
            T.matmul(S[0:NS * NH, 0:PAST], rr, bc[:, BANDX:BANDX + PAST], start=False, stop=True)
            for b in range(NS):
                T.matmul(S[0:NS * NH, PAST:LS], qp[:, b, :], ownT[:, b:b + 1], start=(b == 0), stop=False)
            T.matmul(S[0:NS * NH, PAST:LS], e8, m16[:, PAST:LS], start=False, stop=False)
            T.matmul(S[0:NS * NH, PAST:LS], rr, bc[:, BANDX + PAST:BANDX + LS], start=False, stop=True).then_inc(pe_u, 1)
            pe.wait_ge(s_norm, 1)
            pt = take_pt(("sT", 0))
            for g in range(NPAGE):
                last = T.transpose(pt[:, g * 64:(g + 1) * 64], sS[:, g * P:(g + 1) * P], ident[0:64, 0:64])
            last.then_inc(pe_pt, 1)
            pe.wait_ge(spick_done, 1)
            T.matmul(take_pt(("sP", 0))[0:NS, 0:NS * NH], spick[:, :], ident[0:64, 0:64], start=True, stop=True).then_inc(pe_pt, 1)
            pe.wait_ge(act_pt, pt_no["sP", 0] + 1)
            T.matmul(OT[:, 0, 0:NS * NH], own[:, 128:256], sown[:, :], start=True, stop=False, skip_group_check=True)
            for b in range(NS):
                for g in range(NPAGE):
                    last = T.matmul(OT[:, 0, b * NH:(b + 1) * NH], vpage[:, b * NPAGE + g, :],
                                    pts[:, 0, g * 64 + b * NH:g * 64 + (b + 1) * NH], start=False,
                                    stop=(b == NS - 1 and g == NPAGE - 1), skip_group_check=True)
            last.then_inc(pe_pv, 1)

            def logits(p):
                i, j = pairs[p]
                s = tile_no[i] % 2
                if j == 0:
                    pe.wait_ge(q_in[s], 16 * (tile_no[i] // 2 + 1))
                if p == 0:
                    pe.wait_ge(dve_u, u_no["S", 0] + 1)
                for side in range(2):
                    q = qt[:, s, j + 4 * side, :]
                    for a, k in pieces(i):
                        u = take_u(("L", p, side, a, k))
                        for b0 in range(0, k, 512):
                            bn = min(512, k - b0)
                            T.matmul(u[:, b0:b0 + bn], q, kh[:, side, a + b0:a + b0 + bn], start=True, stop=False)
                            last = T.matmul(u[:, b0:b0 + bn], q, kl[:, side, a + b0:a + b0 + bn], start=False, stop=True)
                        last.then_inc(pe_u, 1)

            def transposes(p, b, k):
                pt = take_pt(("T", p, b, k))
                for side in range(2):
                    for e in range(k):
                        last = T.transpose(pt[:, (side * k + e) * P:(side * k + e + 1) * P],
                                           L[:, (2 * p + side) % 4, (b + e) * P:(b + e + 1) * P], ident)
                last.then_inc(pe_pt, 1)

            def products(p, b, k):
                i, j = pairs[p]
                job = ("T", p, b, k)
                pe.wait_ge(act_pt, pt_no[job] + 1)
                for e in range(k):
                    rows = min(P, width(i) - (b + e) * P)
                    for side in range(2):
                        last = T.matmul(OT[64 * side:64 * side + 64, tile_no[i] % 2, j * P:(j + 1) * P],
                                        vs[0:rows, b + e, 64 * side:64 * side + 64],
                                        pts[0:rows, t_no[job] % 3, (side * k + e) * P:(side * k + e + 1) * P],
                                        start=(b + e == 0), stop=(b + e == nblk(i) - 1))
                last.then_inc(pe_pv, 1)
            logits(0)
            pe.wait_ge(v_in, 32)
            pe.wait_ge(pad_done, 1)
            for p, (i, j) in enumerate(pairs):
                if p + 1 < NP_:
                    logits(p + 1)
                pe.wait_ge(exp_done, 2 * p + 2)
                if j == 0:
                    if p == 0:
                        pe.wait_ge(som_done, 1)
                    if tile_no[i] >= 2:
                        pe.wait_ge(tile_done, tile_no[i] - 1)
                gs = groups(i)
                transposes(p, *gs[0])
                for e, g in enumerate(gs):
                    if e + 1 < len(gs):
                        transposes(p, *gs[e + 1])
                    products(p, *g)
                if j == GRP - 1:
                    n = tile_no[i]
                    pe.wait_ge(ri_ready, n + 1)
                    pt = take_pt(("R", p))
                    for jj in range(GRP):
                        last = T.matmul(pt[:, jj * P:(jj + 1) * P],
                                        rx[:, jj].rearrange("p a d -> p (a d)"), ident, start=True, stop=True)
                    last.then_inc(pe_pt, 1)


BLOCKS = [[LAST]] + [list(range(i, i + 4)) for i in range(0, LAST, 4)]


def mix_out(nc, t, mem):
    order = [i for b in BLOCKS for i in b]
    NB = len(BLOCKS)
    UW = LP - (TAPS - 1)
    SB = NS // 2 * (TAPS - 1)
    with ExitStack() as ctx:
        sb = lambda n, s, d=f32: ctx.enter_context(nc.sbuf_tensor(n, s, d))
        sem = lambda n: ctx.enter_context(nc.semaphore(n))
        wst = sb("wost", [128, 2, D])
        wh = sb("woh", [128, KC, D], f32r)
        wl = sb("wol", [128, KC, D], f32r)
        y = sb("y", [128, 2, CC, 4 * P])
        gc = sb("gc", [128, 2, CC, 4 * P])
        tmp = sb("tmp", [128, CC, 4 * P])
        z = sb("z", [128, CC, 4 * P])
        std = sb("std", [128, 2, 4 * P])
        am = sb("am", [128, 2, CC, P])
        fh = sb("fh", [128, 2, KC, P], f32r)
        fl = sb("fl", [128, 2, KC, P], f32r)
        xr = sb("xr", [128, 2, D])
        res = sb("res", [128, 2, D])
        fin = sb("fin", [128, 2, D])
        sq = sb("sq3", [128, D])
        gf = sb("gf", [128, D])
        lg, lb, cb, cw = sb("lg", [128, CC]), sb("lb", [128, CC]), sb("cb3", [128, CC]), sb("cw3", [128, CC, TAPS])
        ssq, ms, rstd = sb("ssq3", [128, NT]), sb("ms3", [128, NT]), sb("rstd3", [128, NT])
        epsb, eps6 = sb("epsb", [128, 1]), sb("eps6", [128, 1])
        st = sb("st", [SB, 2, C])
        ext = sb("ext", [128, CC, NS, TAPS])
        ys = sb("ys", [128, CC, NS])
        un = sb("un", [128, CC, TAPS - 1])
        us = sb("us", [128, CC, NS])
        uo = sb("uo", [TAPS - 1, C])
        uso = sb("uso", [NS, C])
        O = ctx.enter_context(nc.psum_tensor("psO3", [128, 2, D], f32))
        ST = ctx.enter_context(nc.psum_tensor("psS3", [128, 2, 512], f32))
        M = ctx.enter_context(nc.psum_tensor("psM3", [128, 2, 512], f32))
        w_ld = [sem(f"wo_ld{s}") for s in range(2)]
        w_hi, w_lo = sem("wo_hi"), sem("wo_lo")
        c_in, st_in = sem("c_in3"), sem("st_in")
        y_in = [sem(f"y_in{s}") for s in range(2)]
        a_in = [sem(f"a_in{s}") for s in range(2)]
        x_in = [sem(f"x_in3{s}") for s in range(2)]
        o_out = [sem(f"o_out{s}") for s in range(2)]
        pe_m, act_m, ext_done, ys_done, uso_out = sem("pe_m"), sem("act_m"), sem("ext_done"), sem("ys_done"), sem("uso_out")
        eps_set, zeroed = sem("eps_set"), sem("zeroed3")
        mean_done, centred, squared, var_done, std_done, normed = [sem(x) for x in
            ("mean_done", "centred", "squared", "var_done", "std_done", "normed")]
        swish_in, block_done, hi_done, lo_done, pe_o, res_done, sq_done, rstd_done, fin_done = [sem(x) for x in
            ("swish_in", "block_done", "hi_done", "lo_done", "pe_o", "res_done", "sq_done3", "rstd_done3", "fin_done")]
        pstep = sem("pstep3")
        block_of = {i: (b, e) for b, tiles in enumerate(BLOCKS) for e, i in enumerate(tiles)}
        n_x = [len(tile_rows(i)) for i in order]
        block = ctx.enter_context(nc.Block())

        def in_turn(k):
            nxt = k + 1 if k + 1 < NB else None
            if nxt is not None:
                yield "a", nxt
            tiles = BLOCKS[k] if k >= 0 else []
            for e, i in enumerate(tiles):
                yield "tile", i
                if e == 0 and nxt is not None:
                    yield "b", nxt
                if e == min(1, len(tiles) - 1) and nxt is not None:
                    yield "c", nxt
            if not tiles:
                yield "b", nxt
                yield "c", nxt
        schedule = [x for k in range(-1, NB) for x in in_turn(k)]

        @block.sync
        def _(sp):
            col = lambda a: a.rearrange("(c p) -> p c", p=128)
            sp.dma_start(st[:, 0, :], t.state_conv[0, 0:NS // 2].rearrange("b k c -> (b k) c")).then_inc(st_in, 16)
            sp.dma_start(st[:, 1, :], t.state_conv[0, NS // 2:NS].rearrange("b k c -> (b k) c")).then_inc(st_in, 16)
            sp.dma_start(us[:, :, :], t.d_u[:, :, LAST * P + SROW:LAST * P + SROW + NS].rearrange("c p t -> p c t")).then_inc(st_in, 16)
            sp.dma_start(un[:, :, :], t.d_u[:, :, UW:LP].rearrange("c p t -> p c t")).then_inc(st_in, 16)
            for dst, src in ((lg, t.conv_ln_g), (lb, t.conv_ln_b), (cb, t.conv_b)):
                sp.dma_start(dst[:, :], col(src[0]), allow_slow_non_contiguous=True).then_inc(c_in, 16)
            for c in range(CC):
                sp.dma_start(cw[:, c, :], t.conv_w[0][:, c * P:(c + 1) * P].rearrange("k p -> p k"),
                             allow_slow_non_contiguous=True).then_inc(c_in, 16)
            sp.dma_start(gf[:, :], t.final_norm_g.unsqueeze(0).to_broadcast([128, D])).then_inc(c_in, 16)
            sp.dma_start(t.nconv_s[0, :, 0:TAPS - 2, :], t.state_conv[0, :, 1:TAPS - 1, :]).then_inc(uso_out, 16)

            def load_block(k):
                tiles = BLOCKS[k]
                tok = slice(tiles[0] * P, (tiles[-1] + 1) * P)
                w = len(tiles) * P
                if k >= 2:
                    sp.wait_ge(lo_done, sum(len(b) for b in BLOCKS[:k - 1]))
                sp.dma_start(y[:, k % 2, :, 0:w], t.d_y[:, :, tok].rearrange("c p t -> p c t")).then_inc(y_in[k % 2], 16)
                sp.dma_start(gc[:, k % 2, :, 0:w], t.d_gc[:, :, tok].rearrange("c p t -> p c t")).then_inc(y_in[k % 2], 16)

            def load_am(n):
                if n >= 2:
                    sp.wait_ge(lo_done, n - 1)
                sp.dma_start(am[:, n % 2], t.d_mix[order[n]]).then_inc(a_in[n % 2], 16)

            def load_x(n):
                i = order[n]
                if i == LAST:
                    sp.wait_ge(zeroed, 1)
                if n >= 2:
                    sp.wait_ge(res_done, n - 1)
                for p0, rows, what, r0 in tile_rows(i):
                    src = {"meta": t.meta_tokens, "x": t.x_prompt[0], "sample": t.x_sample[:, 0, :]}[what]
                    sp.dma_start(xr[p0:p0 + rows, n % 2, :], src[r0:r0 + rows, :]).then_inc(x_in[n % 2], 16)
            load_block(0)
            for c in range(KC):
                if c >= 2:
                    sp.wait_ge(w_lo, c - 1)
                if c < CC:
                    sp.dma_start(wst[:, c % 2, :], t.w_out[0, c * P:(c + 1) * P, :]).then_inc(w_ld[c % 2], 32)
                else:
                    for side in range(2):
                        r = C + 64 * (c - CC) + 256 * side
                        sp.dma_start(wst[64 * side:64 * side + 64, c % 2, :], t.w_out[0, r:r + 64, :]).then_inc(w_ld[c % 2], 16)
                if c == 0:
                    load_am(0)
                    load_x(0)
                    load_block(1)
                if c == 1:
                    load_am(1)
                    load_x(1)
            sp.wait_ge(act_m, 1)
            sp.dma_start(t.nconv_p[0, 0], uo[:, :]).then_inc(uso_out, 16)
            sp.wait_ge(act_m, 2)
            sp.dma_start(t.nconv_s[0, :, TAPS - 2, :], uso[:, :]).then_inc(uso_out, 16)
            for n, i in enumerate(order):
                if n + 2 < NT:
                    load_am(n + 2)
                    load_x(n + 2)
                b, e = block_of[i]
                if e == len(BLOCKS[b]) - 1 and b + 2 < NB:
                    load_block(b + 2)
                sp.wait_ge(fin_done, n + 1)
                rows = [(META, P - META, "p", 0)] if i == 0 else \
                    ([(0, LREM, "p", LAST * P - META), (SROW, NS, "s", 0)] if i == LAST else [(0, P, "p", i * P - META)])
                for p0, r, what, r0 in rows:
                    dst = t.y_prompt[0, r0:r0 + r, :] if what == "p" else t.y_sample[:, 0, :]
                    sp.dma_start(dst, fin[p0:p0 + r, n % 2, :]).then_inc(o_out[n % 2], 16)
            outs = [2] + [1] * (NT - 1)
            for s in range(2):
                sp.wait_ge(o_out[s], 16 * sum(outs[s::2]))
            sp.wait_ge(uso_out, 48)

        def x_arrived(eng, n):
            eng.wait_ge(x_in[n % 2], 16 * sum(n_x[n % 2:n + 1:2]))

        def out_written(eng, n):
            eng.wait_ge(o_out[n % 2], 16 * sum(([2] + [1] * (NT - 1))[n % 2:n + 1:2]))

        @block.gpsimd
        def _(pool):
            G = nc.gpsimd
            G.memset(epsb[:, :], LN_EPS).then_inc(eps_set, 1)
            G.memset(xr[:, 0, :], 0.0).then_inc(zeroed, 1)
            steps = [0]

            def chained(ins):
                steps[0] += 1
                ins.then_inc(pstep, 1)
                pool.wait_ge(pstep, steps[0])
            for c in range(KC):
                pool.wait_ge(w_hi, c + 1)
                G.tensor_tensor(out=wl[:, c, :], in0=wst[:, c % 2, :], in1=wh[:, c, :].bitcast(f32), op=ALU.subtract).then_inc(w_lo, 1)
            n = 0
            for what, k in schedule:
                if what == "c":
                    w = len(BLOCKS[k]) * P
                    pool.wait_ge(swish_in, k + 1)
                    chained(G.tensor_tensor(out=z[:, :, 0:w], in0=z[:, :, 0:w], in1=tmp[:, :, 0:w], op=ALU.mult))
                    G.tensor_tensor(out=gc[:, k % 2, :, 0:w], in0=z[:, :, 0:w], in1=gc[:, k % 2, :, 0:w], op=ALU.mult).then_inc(block_done, 1)
                elif what == "tile":
                    b, e = block_of[k]
                    s = n % 2
                    pool.wait_ge(hi_done, n + 1)
                    G.tensor_tensor(out=fl[:, s, 0:CC], in0=gc[:, b % 2, :, e * P:(e + 1) * P], in1=fh[:, s, 0:CC].bitcast(f32), op=ALU.subtract)
                    G.tensor_tensor(out=fl[:, s, CC:KC], in0=am[:, s], in1=fh[:, s, CC:KC].bitcast(f32), op=ALU.subtract).then_inc(lo_done, 1)
                    n += 1
            pool.wait_ge(lo_done, NT)

        @block.scalar
        def _(act):
            A = nc.scalar
            act.wait_ge(w_ld[0], 32)
            for c in range(KC):
                act.wait_ge(w_ld[c % 2], 32 * (c // 2 + 1))
                A.activation(wh[:, c, :], wst[:, c % 2, :], ACT.Copy).then_inc(w_hi, 1)
            act.wait_ge(pe_m, 1)
            A.activation(uo[:, :], M[0:TAPS - 1, 0, :], ACT.Copy).then_inc(act_m, 1)
            act.wait_ge(pe_m, 2)
            A.activation(uso[:, :], M[0:NS, 1, :], ACT.Copy).then_inc(act_m, 1)
            for e in range(4):
                act.wait_ge(pe_m, e + 3)
                c0, half = 2 * (e // 2), e % 2
                A.activation(ext[:, c0:c0 + 2, half * NS // 2:(half + 1) * NS // 2, 0:TAPS - 1],
                             M[:, e % 2, 0:2 * SB].rearrange("p (c b k) -> p c b k", c=2, b=NS // 2), ACT.Copy).then_inc(act_m, 1)
            A.activation(ext[:, :, :, TAPS - 1], us[:, :, :], ACT.Copy).then_inc(ext_done, 1)
            act.wait_ge(eps_set, 2)
            act.wait_ge(c_in, 128)
            n = 0

            def squares(n):
                act.wait_ge(res_done, n + 1)
                if n:
                    act.wait_ge(sq_done, n)
                A.activation(sq[:, :], res[:, n % 2, :], ACT.Square, accum_out=ssq[:, n:n + 1]).then_inc(sq_done, 1)
                act.wait_ge(sq_done, n + 1)
                A.activation(ms[:, n:n + 1], ssq[:, n:n + 1], ACT.Sqrt, scale=1.0 / D, bias=eps6[:, :]).then_inc(rstd_done, 1)
            for what, k in schedule:
                if what == "tile":
                    b, e = block_of[k]
                    s = n % 2
                    act.wait_ge(block_done, b + 1)
                    act.wait_ge(a_in[s], 16 * (n // 2 + 1))
                    if n >= 2:
                        act.wait_ge(pe_o, n - 1)
                    A.activation(fh[:, s, 0:CC], gc[:, b % 2, :, e * P:(e + 1) * P], ACT.Copy)
                    A.activation(fh[:, s, CC:KC], am[:, s], ACT.Copy).then_inc(hi_done, 1)
                    if n:
                        squares(n - 1)
                    n += 1
                    continue
                w = len(BLOCKS[k]) * P
                if what == "a":
                    act.wait_ge(centred, k + 1)
                    if k:
                        act.wait_ge(block_done, k)
                    A.activation(tmp[:, :, 0:w], y[:, k % 2, :, 0:w], ACT.Square).then_inc(squared, 1)
                elif what == "b":
                    act.wait_ge(var_done, k + 1)
                    if k >= 2:
                        act.wait_ge(normed, k - 1)
                    A.activation(std[:, k % 2, 0:w], ST[:, 1, 0:w], ACT.Sqrt, bias=epsb[:, :]).then_inc(std_done, 1)
                else:
                    act.wait_ge(normed, k + 1)
                    for c in range(CC):
                        A.activation(z[:, c, 0:w], y[:, k % 2, c, 0:w], ACT.Identity, bias=lb[:, c:c + 1], scale=lg[:, c:c + 1])
                        last = A.activation(tmp[:, c, 0:w], y[:, k % 2, c, 0:w], ACT.Sigmoid, bias=lb[:, c:c + 1], scale=lg[:, c:c + 1])
                    last.then_inc(swish_in, 1)
            squares(NT - 1)

        @block.vector
        def _(dve):
            V = nc.vector
            dr = V.drain
            TT = lambda out, a, b, op: V.tensor_tensor(out=out, in0=a, in1=b, op=op)
            V.memset(eps6[:, :], EPS).then_inc(eps_set, 1)
            dve.wait_ge(ext_done, 1)
            dve.wait_ge(c_in, 128)
            for c in range(CC):
                TT(ext[:, c], ext[:, c], cw[:, c, :].unsqueeze(1).to_broadcast([128, NS, TAPS]), ALU.mult)
            dr()
            for c in range(CC):
                V.tensor_reduce(ys[:, c, :], ext[:, c], AX.X, ALU.add)
            dr()
            TT(ys[:, :, :], ys[:, :, :], cb[:, :].unsqueeze(2).to_broadcast([128, CC, NS]), ALU.add)
            dr()
            dve.wait_ge(y_in[0], 32)
            V.tensor_copy(y[:, 0, :, SROW:SROW + NS], ys[:, :, :]).then_inc(ys_done, 1)
            n = 0

            def finish(n):
                s = n % 2
                dve.wait_ge(rstd_done, n + 1)
                V.reciprocal(rstd[:, n:n + 1], ms[:, n:n + 1])
                dr()
                if n >= 2:
                    out_written(dve, n - 2)
                V.scalar_tensor_tensor(fin[:, s, :], res[:, s, :], rstd[:, n:n + 1], gf[:, :], ALU.mult, ALU.mult).then_inc(fin_done, 1)
            for what, k in schedule:
                if what == "tile":
                    s = n % 2
                    dve.wait_ge(pe_o, n + 1)
                    x_arrived(dve, n)
                    if n >= 2:
                        dve.wait_ge(fin_done, n - 1)
                    TT(res[:, s, :], O[:, s, :], xr[:, s, :], ALU.add).then_inc(res_done, 1)
                    if n:
                        finish(n - 1)
                    n += 1
                    continue
                w = len(BLOCKS[k]) * P
                if what == "a":
                    dve.wait_ge(y_in[k % 2], 32 * (k // 2 + 1))
                    dve.wait_ge(mean_done, k + 1)
                    TT(y[:, k % 2, :, 0:w], y[:, k % 2, :, 0:w], ST[:, 0, 0:w].unsqueeze(1).to_broadcast([128, CC, w]), ALU.subtract).then_inc(centred, 1)
                elif what == "b":
                    dve.wait_ge(std_done, k + 1)
                    V.reciprocal(std[:, k % 2, 0:w], std[:, k % 2, 0:w])
                    dr()
                    TT(y[:, k % 2, :, 0:w], y[:, k % 2, :, 0:w], std[:, k % 2, 0:w].unsqueeze(1).to_broadcast([128, CC, w]), ALU.mult).then_inc(normed, 1)
            finish(NT - 1)

        @block.tensor
        def _(pe):
            ident = part(mem.cst, "ident")
            ones = part(mem.cst, "ones")
            T = nc.tensor
            pe.wait_ge(st_in, 64)
            for c in range(CC):
                last = T.transpose(M[0:TAPS - 1, 0, c * P:(c + 1) * P], un[:, c, :], ident)
            last.then_inc(pe_m, 1)
            for c in range(CC):
                last = T.transpose(M[0:NS, 1, c * P:(c + 1) * P], us[:, c, :], ident)
            last.then_inc(pe_m, 1)
            for e in range(4):
                pe.wait_ge(act_m, e + 1)
                c0, half = 2 * (e // 2), e % 2
                for c in range(2):
                    last = T.transpose(M[:, e % 2, c * SB:(c + 1) * SB], st[:, half, (c0 + c) * P:(c0 + c + 1) * P], ident[0:SB, 0:SB])
                last.then_inc(pe_m, 1)
            n = 0
            for what, k in schedule:
                if what == "tile":
                    s = n % 2
                    if n == 0:
                        pe.wait_ge(w_lo, KC)
                    pe.wait_ge(lo_done, n + 1)
                    if n >= 2:
                        pe.wait_ge(res_done, n - 1)
                    for c in range(KC):
                        for e, (a, b) in enumerate(((fh, wh), (fh, wl), (fl, wh))):
                            for h in range(2):
                                last = T.matmul(O[:, s, h * 512:(h + 1) * 512], a[:, s, c, :], b[:, c, h * 512:(h + 1) * 512],
                                                start=(c == 0 and e == 0), stop=(c == KC - 1 and e == 2))
                    last.then_inc(pe_o, 1)
                    n += 1
                    continue
                w = len(BLOCKS[k]) * P
                if what == "a":
                    pe.wait_ge(y_in[k % 2], 32 * (k // 2 + 1))
                    if k == 0:
                        pe.wait_ge(ys_done, 1)
                    else:
                        pe.wait_ge(centred, k)
                    for c in range(CC):
                        last = T.matmul(ST[:, 0, 0:w], ones, y[:, k % 2, c, 0:w], start=(c == 0), stop=(c == CC - 1))
                    last.then_inc(mean_done, 1)
                elif what == "b":
                    pe.wait_ge(squared, k + 1)
                    if k:
                        pe.wait_ge(std_done, k)
                    for c in range(CC):
                        last = T.matmul(ST[:, 1, 0:w], ones, tmp[:, c, 0:w], start=(c == 0), stop=(c == CC - 1))
                    last.then_inc(var_done, 1)


class Tensors:
    pass


class OnChip:

    def __init__(self, cst, g=None, iw=None, xh=None, xl=None, ikh=None, ikl=None):
        self.cst, self.g, self.iw, self.xh, self.xl, self.ikh, self.ikl = cst, g, iw, xh, xl, ikh, ikl


def build(nc, t):
    scratch = lambda name, shape, dt: nc.dram_tensor(name, shape, dt, kind="Internal").ap()
    t.d_xh = scratch("d_xh", (HALF, 128, D), f32)
    t.d_xl = scratch("d_xl", (HALF, 128, D), f32)
    t.d_q = scratch("d_q", (NT, 128, NH, P), f32)
    t.d_u = scratch("d_u", (CC, 128, NT * P), f32)
    t.d_gc = scratch("d_gc", (CC, 128, NT * P), f32)
    t.d_ga = scratch("d_ga", (CC, 128, NT * P), f32)
    t.d_mask = scratch("d_mask", (NT, 128, LP), bf16)
    t.d_qs = scratch("d_qs", (128, NS * NS * NH), f32)
    t.d_mix = scratch("d_mix", (NT, 128, CC, P), f32)
    t.d_y = scratch("d_y", (CC, 128, NT * P), f32)
    t.d_r = scratch("d_r", (P, NH, BANDX), f32)
    with ExitStack() as ctx:
        sb = lambda n, s, d=f32: ctx.enter_context(nc.sbuf_tensor(n, s, d))
        cst = sb("cst", [128, NCONST])
        with ExitStack() as proj:
            sp = lambda n, s, d=f32: proj.enter_context(nc.sbuf_tensor(n, s, d))
            mem = OnChip(cst=cst, g=sp("g", [128, KC]), iw=sp("iw", [128, NT, IH]),
                        xh=sp("xh", [128, SLOTS, KC, P], f32r), xl=sp("xl", [128, SLOTS, KC, P], f32r),
                        ikh=sp("ikh", [128, NT * P], f32r), ikl=sp("ikl", [128, NT * P], f32r))
            project_norm_and_keys(nc, t, mem)
            if STAGES > 1:
                project_and_select(nc, t, mem)
        if STAGES > 2:
            attend_and_convolve(nc, t, OnChip(cst=cst))
        if STAGES > 3:
            mix_out(nc, t, OnChip(cst=cst))


STAGES = 4
INS = ["x_prompt", "x_sample", "cache_k", "cache_v", "cache_idx_k", "state_conv", "page_table", "meta_tokens", "rel_bias",
       "norm_g", "w_in", "conv_w", "conv_b", "conv_ln_g", "conv_ln_b", "w_out", "final_norm_g"]
OUTS = [("y_prompt", (1, SEQ, D)), ("y_sample", (NS, 1, D)), ("nk_p", (1, 1, LP, NKV, HD)), ("nv_p", (1, 1, LP, NKV, HD)),
        ("nik_p", (1, 1, LP, 64)), ("nconv_p", (1, 1, TAPS - 1, C)), ("nk_s", (1, NS, 1, NKV, HD)),
        ("nv_s", (1, NS, 1, NKV, HD)), ("nik_s", (1, NS, 1, 64)), ("nconv_s", (1, NS, TAPS - 1, C))]


def declare(nc, shapes):
    shape_of = dict(OUTS)

    def inp(name):
        shape, dt = shapes[name]
        return nc.dram_tensor(f"in_{name}", shape, dt, kind="ExternalInput").ap()

    def out(name):
        return nc.dram_tensor(f"out_{name}", shape_of[name], f32, kind="ExternalOutput").ap()
    t = Tensors()
    t.x_prompt = inp("x_prompt")
    t.x_sample = inp("x_sample")
    t.cache_k = inp("cache_k")
    t.cache_v = inp("cache_v")
    t.cache_idx_k = inp("cache_idx_k")
    t.state_conv = inp("state_conv")
    t.page_table = inp("page_table")
    t.meta_tokens = inp("meta_tokens")
    t.rel_bias = inp("rel_bias")
    t.norm_g = inp("norm_g")
    t.w_in = inp("w_in")
    t.conv_w = inp("conv_w")
    t.conv_b = inp("conv_b")
    t.conv_ln_g = inp("conv_ln_g")
    t.conv_ln_b = inp("conv_ln_b")
    t.w_out = inp("w_out")
    t.final_norm_g = inp("final_norm_g")
    t.consts = inp("consts")
    t.y_prompt = out("y_prompt")
    t.y_sample = out("y_sample")
    t.nk_p = out("nk_p")
    t.nv_p = out("nv_p")
    t.nik_p = out("nik_p")
    t.nconv_p = out("nconv_p")
    t.nk_s = out("nk_s")
    t.nv_s = out("nv_s")
    t.nik_s = out("nik_s")
    t.nconv_s = out("nconv_s")
    return t


def kernel(**inputs):
    import concourse.bacc as bacc
    from concourse.bass_utils import run_bass_kernel_spmd
    nc = bacc.Bacc("TRN2", target_bir_lowering=False, num_devices=1)
    arrays = {n: np.ascontiguousarray(inputs[n]) for n in INS}
    arrays["consts"] = constants()
    t = declare(nc, {n: (a.shape, mybir.dt.from_np(a.dtype)) for n, a in arrays.items()})
    build(nc, t)
    r = run_bass_kernel_spmd(nc, [{f"in_{n}": a for n, a in arrays.items()}], core_ids=[0])
    return tuple(r.results[0][f"out_{n}"] for n, _ in OUTS)
```

```python
import concourse.bass as bass
from concourse import mybir
from contextlib import ExitStack
import math
import numpy as np

f32 = mybir.dt.float32
f32r = mybir.dt.float32r
bf16 = mybir.dt.bfloat16
i32 = mybir.dt.int32
ALU = mybir.AluOpType
ACT = mybir.ActivationFunctionType
AX = mybir.AxisListType

D = 1024
KC = D // 128
SEQ, META = 2048, 16
LP = SEQ + META
P = 128
NT = -(-LP // P)
LAST = NT - 1
LREM = LP - LAST * P
SROW, NS = 32, 8
C = 512
CC = C // 128
NH, HD, NKV, GRP = 8, 64, 2, 4
IH = 4
TAPS = 31
PAST, PAGE = 512, 128
NPAGE = PAST // PAGE
LS = PAST + 1
TOPK_P, TOPK_S = 256, 128
NBUCKET = 32
OFF = dict(ua=0, ub=512, gc=1024, q=1536, k=2048, v=2176, ga=2304, iq=2816, ik=3072, iw=3136)
NAT = 2 * 128 + 64 + IH
NEG = -1.0e30
EPS, LN_EPS = 1e-6, 1e-5
HALF = 8
SLOTS = NT - HALF
HALVES = ([[14, 15, 16], [11, 12, 13], [8, 9, 10]], [[5, 6, 7], [2, 3, 4], [0, 1]])
UNIT = 1024


def width(i):
    return min((i + 1) * P, LP)


def pieces(i):
    return [(a, min(UNIT, width(i) - a)) for a in range(0, width(i), UNIT)]


def t5_bucket(rel):
    n = np.maximum(rel, 0)
    exact = NBUCKET // 2
    large = exact + (np.log(np.maximum(n, 1).astype(np.float32) / np.float32(exact))
                     / np.float32(math.log(128 / exact)) * np.float32(NBUCKET - exact)).astype(np.int32)
    return np.where(n < exact, n, np.minimum(large, NBUCKET - 1))


BANDX = 384
CONST_COLS = dict(ident=(0, 128), causal=(128, 128), e8=(256, 64), e4=(320, 32), iota=(352, 24), kk=(376, NT),
                  ones=(393, 128), e8t=(521, 8), band=(529, BANDX), samp=(529 + BANDX, LS))
NCONST = 529


def constants():
    c = np.zeros((128, NCONST + BANDX + LS), np.float32)

    def at(name):
        a, n = CONST_COLS[name]
        return c[:, a:a + n]
    at("ident")[:] = np.eye(128)
    at("causal")[:] = np.where(np.arange(128)[None] <= np.arange(128)[:, None], 0, NEG)
    for b in range(NS):
        at("e8")[[b, SROW + b], b * NH:(b + 1) * NH] = 1
        at("e4")[SROW + b, b * IH:(b + 1) * IH] = 1
        at("e8t")[b * NH:(b + 1) * NH, b] = 1
    for x in range(BANDX):
        at("band")[t5_bucket(np.array(255 - x)), x] += 1
        at("band")[NBUCKET - 1, x] -= 1
    for s in range(LS):
        at("samp")[t5_bucket(np.array(PAST - s)), s] += 1
        at("samp")[NBUCKET - 1, s] -= 1
    at("iota")[:] = np.tile(np.arange(8), 3)
    at("kk")[:] = TOPK_P
    at("kk")[SROW:SROW + NS, LAST] = TOPK_S
    at("ones")[:] = 1.0 / C
    return c


def part(cst, name):
    a, n = CONST_COLS[name]
    return cst[:, a:a + n]


def tile_rows(i):
    if i == 0:
        return [(0, META, "meta", 0), (META, P - META, "x", 0)]
    if i == LAST:
        return [(0, LREM, "x", LAST * P - META), (SROW, NS, "sample", 0)]
    return [(0, P, "x", i * P - META)]


class Jobs:

    def __init__(self, jobs):
        self.jobs = jobs

    def count(self, n, kinds):
        return sum(1 for j in self.jobs[:n] if j[0] in kinds)


XS = 3


def index_pages(mem):
    return mem.scores[:, :, :].rearrange("p a b -> p (a b)")[:, 0:NS * NPAGE * 64].rearrange("p (n d) -> p n d", d=64)


def load_pages(eng, pages, ptab, cache, layout, dst, pages_in):
    for n in pages:
        v = eng.value_load(ptab[0:1, n:n + 1], min_val=0, max_val=cache.shape[1] - 1)
        eng.dma_start(dst[:, n, :], cache[0, bass.ds(v, 1)].rearrange(layout)).then_inc(pages_in, 16)


def project_norm_and_keys(nc, t, mem):
    jobs = [("xT", 0)]
    for i in range(NT):
        if i + 1 < NT:
            jobs.append(("xT", i + 1))
        jobs.append(("nat", i))
        if i:
            jobs.append(("ikT", i - 1))
    jobs.append(("ikT", NT - 1))
    J = Jobs(jobs)
    with ExitStack() as ctx:
        sb = lambda n, s, d=f32: ctx.enter_context(nc.sbuf_tensor(n, s, d))
        sem = lambda n: ctx.enter_context(nc.semaphore(n))
        xst = sb("xst", [128, XS, D])
        xs = sb("xs", [128, 2, D])
        sq = sb("sq", [128, D])
        ssq = sb("ssq", [128, NT])
        ms = sb("ms", [128, NT])
        rstd = sb("rstd", [128, NT])
        mhalf = sb("mhalf", [128, 1])
        wn = sb("wn", [128, KC, NAT])
        wnh = sb("wnh", [128, KC, NAT], f32r)
        wnl = sb("wnl", [128, KC, NAT], f32r)
        natst = sb("natst", [128, 2, 384])
        psum = ctx.enter_context(nc.psum_tensor("psum0", [128, 4, UNIT], f32))
        x_in = [sem(f"x_in{s}") for s in range(XS)]
        c_in, w_in_s = sem("c_in"), sem("w_in_s")
        sq_done, rstd_done, xs_done, zeroed = sem("sq_done"), sem("rstd_done"), sem("xs_done"), sem("zeroed")
        pool_step, w_mul, w_hi, w_lo = sem("pool_step"), sem("w_mul"), sem("w_hi"), sem("w_lo")
        pe_job, act_job, dve_job = sem("pe_job0"), sem("act_job0"), sem("dve_job0")
        nat_done = sem("nat_done")
        spill = [sem(f"x_spill{s}") for s in range(HALF)]
        nat_out = [sem(f"nat_out{s}") for s in range(2)]
        n_in = [len(tile_rows(i)) for i in range(NT)]
        ptab = sb("ptab", [1, NS * NPAGE], i32)
        ptab_in, pages_in = sem("ptab_in"), sem("pages_in")
        ikp = index_pages(mem)

        def x_arrived(eng, i):
            eng.wait_ge(x_in[i % XS], 16 * sum(n_in[i % XS:i + 1:XS]))

        def nat_written(eng, i):
            n = sum(3 * n for n in ([1] * LAST + [2])[i % 2:i + 1:2])
            eng.wait_ge(nat_out[i % 2], 16 * n)

        def slot(i):
            return i if i < HALF else i - HALF
        block = ctx.enter_context(nc.Block())

        @block.sync
        def _(sp):
            def load_x(i):
                if i >= XS:
                    sp.wait_ge(xs_done, i - XS + 1)
                if i == LAST:
                    sp.wait_ge(zeroed, 1)
                for p0, n, what, r0 in tile_rows(i):
                    src = {"meta": t.meta_tokens, "x": t.x_prompt[0], "sample": t.x_sample[:, 0, :]}[what]
                    sp.dma_start(xst[p0:p0 + n, i % XS, :], src[r0:r0 + n, :]).then_inc(x_in[i % XS], 16)

            def write_natural(i):
                sp.wait_ge(nat_done, i + 1)
                n = natst[:, i % 2]
                for p0, rows, what in ([(0, P, "p")] if i < LAST else [(0, LREM, "p"), (SROW, NS, "s")]):
                    r = slice(i * P, i * P + rows)
                    ko = t.nk_p[0, 0, r] if what == "p" else t.nk_s[0, :, 0]
                    vo = t.nv_p[0, 0, r] if what == "p" else t.nv_s[0, :, 0]
                    io = t.nik_p[0, 0, r] if what == "p" else t.nik_s[0, :, 0]
                    q = slice(p0, p0 + rows)
                    sp.dma_start(ko.rearrange("t n d -> t (n d)"), n[q, 0:128]).then_inc(nat_out[i % 2], 16)
                    sp.dma_start(vo.rearrange("t n d -> t (n d)"), n[q, 128:256]).then_inc(nat_out[i % 2], 16)
                    sp.dma_start(io, n[q, 256:320]).then_inc(nat_out[i % 2], 16)
            load_x(0)
            load_x(1)
            sp.dma_start(mem.cst[:, :], t.consts[:, 0:NCONST]).then_inc(c_in, 16)
            sp.dma_start(mem.g[:, :], t.norm_g[0].rearrange("(c p) -> p c", p=128),
                         allow_slow_non_contiguous=True).then_inc(c_in, 16)
            w3 = t.w_in[0].rearrange("(c p) n -> p c n", p=128)
            sp.dma_start(wn[:, :, 0:256], w3[:, :, OFF["k"]:OFF["k"] + 256]).then_inc(w_in_s, 16)
            sp.dma_start(wn[:, :, 256:NAT], w3[:, :, OFF["ik"]:OFF["ik"] + 68]).then_inc(w_in_s, 16)
            load_x(2)
            sp.dma_start(ptab[:, :], t.page_table.rearrange("b n -> (b n)").unsqueeze(0)).then_inc(ptab_in, 16)
            sp.wait_ge(ptab_in, 16)
            for i in range(NT + 1):
                if i < NT:
                    if i + XS < NT:
                        load_x(i + XS)
                    if i < HALF:
                        sp.wait_ge(dve_job, J.count(J.jobs.index(("xT", i)) + 1, ("xT", "ikT")))
                        sp.dma_start(t.d_xh[i], mem.xh[:, slot(i)].rearrange("p c t -> p (c t)").bitcast(f32)).then_inc(spill[i], 16)
                        sp.dma_start(t.d_xl[i], mem.xl[:, slot(i)].rearrange("p c t -> p (c t)").bitcast(f32)).then_inc(spill[i], 16)
                    if i < LAST:
                        load_pages(sp, range(2 * i, 2 * i + 2), ptab, t.cache_idx_k, "o s d -> (o s) d", ikp, pages_in)
                if i:
                    write_natural(i - 1)
            nat_written(sp, LAST)
            nat_written(sp, LAST - 1)
            sp.wait_ge(pages_in, 16 * NS * NPAGE)
            for s in range(HALF):
                sp.wait_ge(spill[s], 32)

        @block.gpsimd
        def _(pool):
            nc.gpsimd.memset(mhalf[:, :], -0.5).then_inc(pool_step, 1)
            pool.wait_ge(c_in, 32)
            pool.wait_ge(w_in_s, 32)
            nc.gpsimd.tensor_tensor(out=wn[:, :, :], in0=wn[:, :, :], in1=mem.g[:, :].unsqueeze(2).to_broadcast([128, KC, NAT]),
                                    op=ALU.mult).then_inc(w_mul, 1)
            pool.wait_ge(w_mul, 1)
            pool.wait_ge(w_hi, 1)
            nc.gpsimd.tensor_tensor(out=wnl[:, :, :], in0=wn[:, :, :], in1=wnh[:, :, :].bitcast(f32),
                                    op=ALU.subtract).then_inc(w_lo, 1)
            for i in range(NT):
                if i == LAST - XS + 1:
                    pool.wait_ge(xs_done, LAST - XS + 1)
                    nc.gpsimd.memset(xst[:, LAST % XS, :], 0.0).then_inc(zeroed, 1)
                pool.wait_ge(sq_done, i + 1)
                nc.gpsimd.tensor_scalar(ms[:, i:i + 1], ssq[:, i:i + 1], 1.0 / D, EPS, ALU.mult, ALU.add).then_inc(pool_step, 1)
                pool.wait_ge(pool_step, i + 2)
                nc.gpsimd.tensor_tensor(out=rstd[:, i:i + 1], in0=ms[:, i:i + 1], in1=mhalf[:, :], op=ALU.pow).then_inc(rstd_done, 1)

        @block.scalar
        def _(act):
            def square(i):
                x_arrived(act, i)
                if i:
                    act.wait_ge(sq_done, i)
                nc.scalar.activation(sq[:, :], xst[:, i % XS, :], ACT.Square, accum_out=ssq[:, i:i + 1]).then_inc(sq_done, 1)
            square(0)
            square(1)
            act.wait_ge(w_mul, 1)
            nc.scalar.activation(wnh[:, :, :], wn[:, :, :], ACT.Copy).then_inc(w_hi, 1)
            for n, (kind, i) in enumerate(J.jobs):
                if kind == "xT" and i + 2 < NT:
                    square(i + 2)
                act.wait_ge(pe_job, n + 1)
                u = psum[:, n % 4]
                if kind == "xT":
                    if i >= HALF:
                        if i < 2 * HALF:
                            act.wait_ge(spill[i - HALF], 32)
                    nc.scalar.activation(mem.xh[:, slot(i)].rearrange("p c t -> p (c t)"), u, ACT.Copy).then_inc(act_job, 1)
                elif kind == "nat":
                    if i >= 2:
                        nat_written(act, i - 2)
                    nc.scalar.activation(natst[:, i % 2, 0:256], u[:, 0:256], ACT.Copy)
                    nc.scalar.activation(natst[:, i % 2, 256:384].rearrange("p (a d) -> p a d", a=2),
                                         u[:, 256:320].unsqueeze(1).to_broadcast([128, 2, 64]), ACT.Copy).then_inc(nat_done, 1)
                    nc.scalar.activation(mem.iw[:, i], u[:, 320:324], ACT.Copy, scale=float(IH) ** -0.5).then_inc(act_job, 1)
                else:
                    nc.scalar.activation(mem.ikh[:, i * P:(i + 1) * P], u[:, 0:128], ACT.Copy).then_inc(act_job, 1)

        @block.vector
        def _(dve):
            def scale(i):
                dve.wait_ge(rstd_done, i + 1)
                if i >= 2:
                    dve.wait_ge(pe_job, J.jobs.index(("xT", i - 2)) + 1)
                nc.vector.tensor_scalar(xs[:, i % 2, :], xst[:, i % XS, :], rstd[:, i:i + 1], None, ALU.mult).then_inc(xs_done, 1)
            scale(0)
            for n, (kind, i) in enumerate(J.jobs):
                u = psum[:, n % 4]
                if kind == "xT":
                    if i + 1 < NT:
                        scale(i + 1)
                    dve.wait_ge(act_job, n + 1)
                    nc.vector.tensor_tensor(out=mem.xl[:, slot(i)].rearrange("p c t -> p (c t)"), in0=u,
                                            in1=mem.xh[:, slot(i)].rearrange("p c t -> p (c t)").bitcast(f32),
                                            op=ALU.subtract).then_inc(dve_job, 1)
                elif kind == "ikT":
                    dve.wait_ge(act_job, n + 1)
                    nc.vector.tensor_tensor(out=mem.ikl[:, i * P:(i + 1) * P], in0=u[:, 0:128],
                                            in1=mem.ikh[:, i * P:(i + 1) * P].bitcast(f32), op=ALU.subtract).then_inc(dve_job, 1)

        @block.tensor
        def _(pe):
            ident = part(mem.cst, "ident")
            for n, (kind, i) in enumerate(J.jobs):
                u = psum[:, n % 4]
                if n >= 4:
                    pe.wait_ge(act_job, n - 3)
                    if J.count(n - 3, ("xT", "ikT")):
                        pe.wait_ge(dve_job, J.count(n - 3, ("xT", "ikT")))
                if kind == "xT":
                    if n == 0:
                        pe.wait_ge(c_in, 32)
                    pe.wait_ge(xs_done, i + 1)
                    for c in range(KC):
                        last = nc.tensor.transpose(u[:, c * P:(c + 1) * P], xs[:, i % 2, c * P:(c + 1) * P], ident)
                elif kind == "nat":
                    if i == 0:
                        pe.wait_ge(w_lo, 1)
                    pe.wait_ge(dve_job, J.count(J.jobs.index(("xT", i)) + 1, ("xT", "ikT")))
                    xh, xl = mem.xh[:, slot(i)], mem.xl[:, slot(i)]
                    for c in range(KC):
                        for k, (a, b) in enumerate(((xh, wnh), (xh, wnl), (xl, wnh))):
                            last = nc.tensor.matmul(u[:, 0:NAT], a[:, c, :], b[:, c, :], start=(c == 0 and k == 0),
                                                    stop=(c == KC - 1 and k == 2))
                else:
                    pe.wait_ge(nat_done, i + 1)
                    last = nc.tensor.transpose(u[:, 0:128], natst[:, i % 2, 256:384], ident)
                last.then_inc(pe_job, 1)


INDEXER = [("iq", 0), ("iq", 1)]
OTHERS = [("q", j) for j in range(4)] + [(a, j) for j in range(4) for a in ("ub", "ua")] + \
        [(a, j) for a in ("gc", "ga") for j in range(4)]
IQ_AT = 4
CHUNKS = (INDEXER + OTHERS, OTHERS[:IQ_AT] + INDEXER + OTHERS[IQ_AT:])
NCHUNK = len(CHUNKS[0])
SCORE_AT = {(0, 2): 0, (0, 13): 1, (1, 0): 2, (1, 9): 3, (1, 17): 4}
GROUPS = [[16, 15, 14], [13, 12, 11], [10, 9, 8], [7, 6, 5], [4, 3, 2]]
SEARCH = 8
TINY = 2.0 ** -100


def chunk_columns(name, j):
    if name in ("q", "ga"):
        return [(OFF[name] + 64 * j, 64), (OFF[name] + 256 + 64 * j, 64)]
    return [(OFF[name] + 128 * j, 128)]


def select_jobs():
    jobs = []
    for h, blocks in enumerate(HALVES):
        for c, (name, j) in enumerate(CHUNKS[h]):
            if (h, c) in SCORE_AT:
                g = SCORE_AT[h, c]
                if g == 0:
                    jobs += [("we", 0)] + [("page", b) for b in range(NS)] + [("ss", 0), ("sw", 0)]
                jobs += [("score", i, head, a, n) for i in GROUPS[g] for head in range(IH) for a, n in pieces(i)]
            jobs += [("proj", h, c, b) for b in range(len(blocks))]
    return jobs


def project_and_select(nc, t, mem):
    jobs = select_jobs()
    uses = [(h, c) for h in range(2) for c in range(NCHUNK)]
    first = {}
    lastjob = {}
    for n, j in enumerate(jobs):
        if j[0] == "proj":
            first.setdefault((j[1], j[2]), n)
            lastjob[j[1], j[2]] = n
    W3 = 3 * P
    with ExitStack() as ctx:
        sb = lambda n, s, d=f32: ctx.enter_context(nc.sbuf_tensor(n, s, d))
        sem = lambda n: ctx.enter_context(nc.semaphore(n))
        wst = sb("wst", [128, 2, KC, P])
        wh = sb("wh", [128, 2, KC, P], f32r)
        wl = sb("wl", [128, 2, KC, P], f32r)
        iqs = sb("iqs", [128, IH, SLOTS * P], f32r)
        fst = sb("fst", [128, 2, W3])
        hst = sb("hst", [128, 2, W3], f32r)
        lst = sb("lst", [128, 2, W3], f32r)
        ust = sb("ust", [128, 2, W3])
        sig = sb("sig", [128, 3, W3])
        r = sb("r", [128, 2, UNIT])
        hit = sb("hit", [128, LP], bf16)
        run = sb("run", [128, LP])
        iqpad = sb("iqpad", [64, NS * NS * IH])
        qpad = sb("qpad", [128, NS * NS * NH])
        iks = sb("iks", [64, NS])
        we = sb("we", [SROW + NS, NS * IH])
        ws = sb("ws", [NS * IH, NS])
        sscore = sb("sscore", [SROW + NS, LS])
        G3 = lambda n, *s, d=f32: sb(n, [128, *s], d)
        amax, lo, hi, T = G3("amax", 3), G3("lo", 2, 3), G3("hi", 2, 3), G3("T", 2, 3)
        kt, k4, slope, sum4 = G3("kt", 3), G3("k4", 3), G3("slope", 3), G3("sum4", 3)
        m8s, m8, hot = G3("m8s", 3, 4, 8), G3("m8", 3, 8), G3("hot", 3, 8)
        gap, num, jj, jc, more, rest = G3("gap", 2, 3), G3("num", 3), G3("jj", 3), G3("jc", 3), G3("more", 3), G3("rest", 3)
        above, tie_room, tiny, zero = G3("above", 3), G3("tie_room", 3), G3("tiny", 3), G3("zero", 3)
        ge, lt, upd = G3("ge", 3, d=i32), G3("lt", 3, d=i32), G3("upd", 3, d=i32)
        gef, fall = G3("gef", 3), G3("fall", 3, d=i32)
        flag, flagT, flag1, flagi = G3("flag", 32), G3("flagT", 32), G3("flag1", 1), G3("flagi", 1, d=i32)
        psum = ctx.enter_context(nc.psum_tensor("psum1", [128, 4, UNIT], f32))
        scores = mem.scores
        kp = scores[:, :, :].rearrange("p a b -> p (a b)")
        ikp = index_pages(mem)
        ikTs = kp[0:64, NS * NPAGE * 64:NS * NPAGE * 64 + NS * PAST].rearrange("p (b s) -> p b s", b=NS)

        w_ld = [sem(f"w_ld{s}") for s in range(2)]
        x_ld = [sem(f"x_ld{s}") for s in range(HALF)]
        w_mul, w_hi, w_lo = sem("w_mul1"), sem("w_hi1"), sem("w_lo1")
        pe_job, act_job = sem("pe_job1"), sem("act_job1")
        staged, combined = sem("staged"), sem("combined")
        out_s = [sem(f"out_s{s}") for s in range(2)]
        added = sem("added")
        zero_pad, iks_done, we_done = sem("zero_pad"), sem("iks_done"), sem("we_done")
        mask_ready = sem("mask_ready")
        mask_out = [sem(f"mask_out{s}") for s in range(3)]
        qpad_done, qs_out = sem("qpad_done"), sem("qs_out")

        staged_jobs = [(n, *CHUNKS[j[1]][j[2]], j[1], j[3]) for n, j in enumerate(jobs) if j[0] == "proj"
                       and CHUNKS[j[1]][j[2]][0] != "ub"]
        stage_no = {s[0]: m for m, s in enumerate(staged_jobs)}
        dmas = lambda kind: 4 if kind in ("iq", "q") else 1

        def slot_written(eng, m):
            eng.wait_ge(out_s[m % 2], 16 * sum(dmas(s[1]) for s in staged_jobs[m % 2:m + 1:2]))

        def slots(h, b):
            tiles = HALVES[h][b]
            return tiles[0] - (HALF if h == 0 else 0), len(tiles)
        score_jobs = [n for n, j in enumerate(jobs) if j[0] == "score"]
        score_no = {n: m for m, n in enumerate(score_jobs)}
        act_no = lambda n: n + 1 - sum(1 for s in staged_jobs if s[0] <= n)
        block = ctx.enter_context(nc.Block())

        @block.sync
        def _(sp):
            w3 = t.w_in[0].rearrange("(c p) n -> p c n", p=128)

            def load_w(n):
                h, c = uses[n]
                if n >= 2:
                    sp.wait_ge(w_lo, n - 1)
                cols = chunk_columns(*CHUNKS[h][c])
                at = 0
                for a, k in cols:
                    sp.dma_start(wst[:, n % 2, :, at:at + k], w3[:, :, a:a + k]).then_inc(w_ld[n % 2], 32 // len(cols))
                    at += k
            load_w(0)
            load_w(1)

            def write_masks(g):
                for k, i in enumerate(GROUPS[g]):
                    sp.wait_ge(mask_ready, 3 * g + k + 1)
                    sp.dma_start(t.d_mask[i, :, 0:width(i)], scores[:, k, :].bitcast(bf16)[:, 0:width(i)]).then_inc(mask_out[k], 16)
            for n, (h, c) in enumerate(uses):
                if n + 2 < len(uses):
                    load_w(n + 2)
                if SCORE_AT.get((h, c)):
                    write_masks(SCORE_AT[h, c] - 1)
                if n == NCHUNK:
                    sp.wait_ge(pe_job, lastjob[0, NCHUNK - 1] + 1)
                    for i in range(HALF - 1, -1, -1):
                        sp.dma_start(mem.xh[:, i].rearrange("p c t -> p (c t)").bitcast(f32), t.d_xh[i]).then_inc(x_ld[i], 16)
                        sp.dma_start(mem.xl[:, i].rearrange("p c t -> p (c t)").bitcast(f32), t.d_xl[i]).then_inc(x_ld[i], 16)
                for m, (job, kind, j, hh, b) in enumerate(staged_jobs):
                    if (hh, jobs[job][2]) != (h, c):
                        continue
                    s0, k = slots(hh, b)
                    cols = slice(s0 * P, (s0 + k) * P)
                    tiles = HALVES[hh][b]
                    tok = slice(tiles[0] * P, (tiles[-1] + 1) * P)
                    sp.wait_ge(combined, m + 1)
                    s = m % 2
                    if kind in ("iq", "q"):
                        if kind == "iq" and hh == 1 and j == 0 and b == 0:
                            sp.wait_ge(pe_job, max(x for x in score_jobs if jobs[x][1] in GROUPS[2]) + 1)
                        for part_no, src in enumerate((hst, lst)):
                            for side in range(2):
                                rows = slice(64 * side, 64 * side + 64)
                                to = slice(64 * part_no, 64 * part_no + 64)
                                if kind == "iq":
                                    sp.dma_start(iqs[to, 2 * j + side, cols].bitcast(f32),
                                                 src[rows, s, 0:k * P].bitcast(f32)).then_inc(out_s[s], 16)
                                else:
                                    head = j + 4 * side
                                    sp.dma_start(t.d_q[tiles[0]:tiles[-1] + 1, to, head, :].rearrange("i p t -> p i t"),
                                                 src[rows, s, 0:k * P].bitcast(f32).rearrange("p (i t) -> p i t", t=P))\
                                      .then_inc(out_s[s], 16)
                    else:
                        dst = {"ua": t.d_u, "gc": t.d_gc, "ga": t.d_ga}[kind]
                        sp.dma_start(dst[j, :, tok], ust[:, s, 0:k * P]).then_inc(out_s[s], 16)
                if (h, c) == (0, 5):
                    sp.wait_ge(qpad_done, 8)
                    sp.dma_start(t.d_qs, qpad[:, :]).then_inc(qs_out, 16)
            write_masks(len(GROUPS) - 1)
            slot_written(sp, len(staged_jobs) - 1)
            slot_written(sp, len(staged_jobs) - 2)
            sp.wait_ge(qs_out, 16)
            for k in range(3):
                sp.wait_ge(mask_out[k], 16 * len(GROUPS))

        @block.gpsimd
        def _(pool):
            nc.gpsimd.memset(iqpad[:, :], 0.0).then_inc(zero_pad, 1)
            nc.gpsimd.memset(qpad[:, :], 0.0).then_inc(zero_pad, 1)
            own = slice(LAST * P + SROW, LAST * P + SROW + NS)
            nc.gpsimd.tensor_tensor(out=iks[:, :], in0=mem.ikh[0:64, own].bitcast(f32), in1=mem.ikl[0:64, own].bitcast(f32),
                                    op=ALU.add).then_inc(iks_done, 1)

            def gain(n):
                pool.wait_ge(w_ld[n % 2], 32 * (n // 2 + 1))
                nc.gpsimd.tensor_tensor(out=wst[:, n % 2], in0=wst[:, n % 2],
                                        in1=mem.g[:, :].unsqueeze(2).to_broadcast([128, KC, P]), op=ALU.mult).then_inc(w_mul, 1)

            def low(n):
                pool.wait_ge(w_hi, n + 1)
                nc.gpsimd.tensor_tensor(out=wl[:, n % 2], in0=wst[:, n % 2], in1=wh[:, n % 2].bitcast(f32),
                                        op=ALU.subtract).then_inc(w_lo, 1)
            gain(0)
            low(0)
            gain(1)
            for n, (h, c) in enumerate(uses):
                if n + 1 < len(uses):
                    low(n + 1)
                if n + 2 < len(uses):
                    gain(n + 2)
                for m, (job, kind, j, hh, b) in enumerate(staged_jobs):
                    if (hh, jobs[job][2]) != (h, c):
                        continue
                    k = slots(hh, b)[1] * P
                    s = m % 2
                    pool.wait_ge(staged, m + 1)
                    if kind in ("iq", "q"):
                        nc.gpsimd.tensor_tensor(out=lst[:, s, 0:k], in0=fst[:, s, 0:k], in1=hst[:, s, 0:k].bitcast(f32),
                                                op=ALU.subtract).then_inc(combined, 1)
                    elif kind == "ua":
                        if m >= 2:
                            slot_written(pool, m - 2)
                        nc.gpsimd.tensor_tensor(out=ust[:, s, 0:k], in0=fst[:, s, 0:k], in1=sig[:, b, 0:k],
                                                op=ALU.mult).then_inc(combined, 1)
                    else:
                        nc.gpsimd.tensor_tensor(out=ust[:, s, 0:k], in0=fst[:, s, 0:k], in1=ust[:, s, 0:k],
                                                op=ALU.mult).then_inc(combined, 1)

        @block.scalar
        def _(act):
            def high(n):
                act.wait_ge(w_mul, n + 1)
                if n >= 2:
                    act.wait_ge(pe_job, lastjob[uses[n - 2]] + 1)
                nc.scalar.activation(wh[:, n % 2], wst[:, n % 2], ACT.Copy).then_inc(w_hi, 1)
            high(0)
            for n, job in enumerate(jobs):
                if job[0] == "proj" and job[3] == 0:
                    c = uses.index(job[1:3])
                    if c + 1 < len(uses):
                        high(c + 1)
                act.wait_ge(pe_job, n + 1)
                u = psum[:, n % 4]
                if job[0] == "proj":
                    _, h, c, b = job
                    kind, j = CHUNKS[h][c]
                    k = slots(h, b)[1] * P
                    if kind == "ub":
                        if j or h:
                            act.wait_ge(combined, 1 + max(m for m, s in enumerate(staged_jobs) if s[0] < n and s[1] == "ua"))
                        nc.scalar.activation(sig[:, b, 0:k], u[:, 0:k], ACT.Sigmoid).then_inc(act_job, 1)
                        continue
                    m = stage_no[n]
                    s = m % 2
                    if m >= 2:
                        act.wait_ge(combined, m - 1)
                        slot_written(act, m - 2)
                    if kind in ("iq", "q"):
                        if h == 0 and b == 0:
                            cols = u[:, 2 * P + SROW:2 * P + SROW + NS]
                            act.wait_ge(zero_pad, 2)
                            if kind == "iq":
                                for side in range(2):
                                    nc.scalar.activation(iqpad[:, 2 * j + side::NS * IH + IH], cols[64 * side:64 * side + 64],
                                                         ACT.Copy, scale=0.125)
                            else:
                                for side in range(2):
                                    rows = slice(64 * side, 64 * side + 64)
                                    nc.scalar.activation(qpad[rows, j + 4 * side::NS * NH + NH], cols[rows],
                                                         ACT.Copy, scale=0.125).then_inc(qpad_done, 1)
                        nc.scalar.activation(fst[:, s, 0:k], u[:, 0:k], ACT.Copy, scale=0.125)
                        nc.scalar.activation(hst[:, s, 0:k], u[:, 0:k], ACT.Copy, scale=0.125).then_inc(staged, 1)
                    elif kind == "ua":
                        nc.scalar.activation(fst[:, s, 0:k], u[:, 0:k], ACT.Copy).then_inc(staged, 1)
                    else:
                        nc.scalar.activation(fst[:, s, 0:k], u[:, 0:k], ACT.Copy)
                        nc.scalar.activation(ust[:, s, 0:k], u[:, 0:k], ACT.Sigmoid).then_inc(staged, 1)
                elif job[0] == "score":
                    m = score_no[n]
                    if m >= 2:
                        act.wait_ge(added, m - 1)
                    nc.scalar.activation(r[:, m % 2, 0:job[4]], u[:, 0:job[4]], ACT.Relu).then_inc(act_job, 1)
                elif job[0] == "we":
                    nc.scalar.activation(ws[:, :], u[0:NS * IH, 0:NS], ACT.Copy).then_inc(act_job, 1)
                elif job[0] == "page":
                    nc.scalar.activation(ikTs[:, job[1]], u[0:64, 0:PAST], ACT.Copy).then_inc(act_job, 1)
                elif job[0] == "ss":
                    nc.scalar.activation(r[0:NS * IH, 0, 0:LS], u[0:NS * IH, 0:LS], ACT.Relu).then_inc(act_job, 1)
                elif job[0] == "sw":
                    nc.scalar.activation(sscore[SROW:SROW + NS, :], u[SROW:SROW + NS, 0:LS], ACT.Copy).then_inc(act_job, 1)

        @block.tensor
        def _(pe):
            ident = part(mem.cst, "ident")

            def arrived(n):
                if n in stage_no:
                    pe.wait_ge(staged, stage_no[n] + 1)
                else:
                    pe.wait_ge(act_job, act_no(n))
            for n, job in enumerate(jobs):
                u = psum[:, n % 4]
                if n >= 4:
                    arrived(n - 4)
                if job[0] == "proj":
                    _, h, c, b = job
                    w = uses.index((h, c))
                    s0, k = slots(h, b)
                    if b == 0:
                        pe.wait_ge(w_lo, w + 1)
                    if h == 1 and c == 0:
                        for i in range(s0, s0 + k):
                            pe.wait_ge(x_ld[i], 32)
                    for cc in range(KC):
                        for e, (a, x) in enumerate(((wh, mem.xh), (wh, mem.xl), (wl, mem.xh))):
                            last = nc.tensor.matmul(u[:, 0:k * P], a[:, w % 2, cc, :], x[:, s0:s0 + k, cc, :],
                                                    start=(cc == 0 and e == 0), stop=(cc == KC - 1 and e == 2))
                elif job[0] == "score":
                    _, i, head, a, k = job
                    need = max(m for m, x in enumerate(staged_jobs) if x[0] < n and x[1] == "iq")
                    for m in (need, need - 1):
                        slot_written(pe, m)
                    q = iqs[:, head, (i - (HALF if i >= HALF else 0)) * P:][:, 0:P]
                    for b0 in range(0, k, 512):
                        bn = min(512, k - b0)
                        nc.tensor.matmul(u[:, b0:b0 + bn], q, mem.ikh[:, a + b0:a + b0 + bn], start=True, stop=False)
                        last = nc.tensor.matmul(u[:, b0:b0 + bn], q, mem.ikl[:, a + b0:a + b0 + bn], start=False, stop=True)
                elif job[0] == "we":
                    pe.wait_ge(we_done, 1)
                    last = nc.tensor.matmul(u[0:NS * IH, 0:NS], we[SROW:SROW + NS, :], ident[SROW:SROW + NS, SROW:SROW + NS],
                                            start=True, stop=True)
                elif job[0] == "page":
                    for g in range(NPAGE):
                        last = nc.tensor.matmul(u[0:64, g * PAGE:(g + 1) * PAGE], ikp[:, job[1] * NPAGE + g, :], ident,
                                                start=True, stop=True)
                elif job[0] == "ss":
                    arrived(n - 1)
                    pe.wait_ge(iks_done, 1)
                    for b in range(NS):
                        q = iqpad[:, b * NS * IH:(b + 1) * NS * IH]
                        nc.tensor.matmul(u[0:NS * IH, 0:PAST], q, ikTs[:, b], start=(b == 0), stop=(b == NS - 1))
                    for b in range(NS):
                        q = iqpad[:, b * NS * IH:(b + 1) * NS * IH]
                        last = nc.tensor.matmul(u[0:NS * IH, PAST:LS], q, iks[:, b:b + 1], start=(b == 0), stop=(b == NS - 1))
                elif job[0] == "sw":
                    arrived(n - 1)
                    nc.tensor.matmul(u[SROW:SROW + NS, 0:PAST], ws[:, :], r[0:NS * IH, 0, 0:PAST], start=True, stop=True)
                    last = nc.tensor.matmul(u[SROW:SROW + NS, PAST:LS], ws[:, :], r[0:NS * IH, 0, PAST:LS], start=True, stop=True)
                last.then_inc(pe_job, 1)

        @block.vector
        def _(dve):
            V = nc.vector
            dr = V.drain
            B3 = lambda ap: ap.unsqueeze(1).to_broadcast([128, 2, 3])
            B8 = lambda ap: ap.unsqueeze(2).to_broadcast([128, 3, 8])
            TT = lambda out, a, b, op: V.tensor_tensor(out=out, in0=a, in1=b, op=op)
            own = slice(SROW, SROW + NS)
            TT(we[own, :].rearrange("p (b h) -> p b h", h=IH), part(mem.cst, "e4")[own].rearrange("p (b h) -> p b h", h=IH),
               mem.iw[own, LAST].unsqueeze(1).to_broadcast([NS, NS, IH]), ALU.mult).then_inc(we_done, 1)
            V.memset(flag[:, :], 0.0)
            V.memset(tiny[:, :], TINY)
            V.memset(zero[:, :], 0.0)
            sw_job = jobs.index(("sw", 0))
            m = 0
            for gno, tiles in enumerate(GROUPS):
                for c, i in enumerate(tiles):
                    if gno:
                        dve.wait_ge(mask_out[c], 16 * gno)
                    for head in range(IH):
                        for a, n in pieces(i):
                            dve.wait_ge(act_job, act_no(score_jobs[m]))
                            if head:
                                dve.wait_ge(added, m + 1 - len(pieces(i)))
                            w = mem.iw[:, i, head:head + 1]
                            o = scores[:, c, a:a + n]
                            if head == 0:
                                V.tensor_scalar(o, r[:, m % 2, 0:n], w, None, ALU.mult).then_inc(added, 1)
                            else:
                                V.scalar_tensor_tensor(o, r[:, m % 2, 0:n], w, o, ALU.mult, ALU.add).then_inc(added, 1)
                            m += 1
                dr()
                for c, i in enumerate(tiles):
                    V.tensor_reduce(amax[:, c:c + 1], scores[:, c, 0:width(i)], AX.X, ALU.max, apply_absolute_value=True)
                    V.tensor_copy(kt[:, c:c + 1], part(mem.cst, "kk")[:, i:i + 1])
                dr()
                for c, i in enumerate(tiles):
                    k = width(i) - i * P
                    o = scores[:, c, i * P:i * P + k]
                    TT(o, o, part(mem.cst, "causal")[:, 0:k], ALU.add)
                    if i == LAST:
                        dve.wait_ge(act_job, act_no(sw_job))
                        dr()
                        V.tensor_reduce(amax[own, c:c + 1], sscore[own, :], AX.X, ALU.max, apply_absolute_value=True)
                        V.memset(scores[own, c, :], NEG)
                        dr()
                        V.tensor_copy(scores[own, c, 0:LS], sscore[own, :])
                dr()
                V.tensor_scalar(hi[:, 0, :], amax[:, :], 1.0001, 1e-30, ALU.mult, ALU.add)
                V.memset(hi[:, 1, :], 0.0)
                V.memset(lo[:, 1, :], float(LP))
                V.tensor_scalar(k4[:, :], kt[:, :], -4.0, None, ALU.add)
                for c, i in enumerate(tiles):
                    for o in range(4):
                        V.max(m8s[:, c, o, :], scores[:, c, 8 * o:width(i):32])
                dr()
                V.tensor_scalar(lo[:, 0, :], hi[:, 0, :], -1.0, None, ALU.mult)
                V.tensor_reduce(sum4[:, :], m8s[:, :, :, 7], AX.X, ALU.add)
                V.tensor_reduce(slope[:, :], m8s[:, :, :, 3], AX.X, ALU.add)
                dr()
                TT(slope[:, :], slope[:, :], sum4[:, :], ALU.subtract)
                V.tensor_scalar(T[:, 0, :], sum4[:, :], 0.25, None, ALU.mult)
                dr()
                V.tensor_scalar(slope[:, :], slope[:, :], 0.25 / 128, None, ALU.mult)

                def inside():
                    TT(gef[:, :], T[:, 0, :], lo[:, 0, :], ALU.is_le)
                    TT(num[:, :], T[:, 0, :], hi[:, 0, :], ALU.is_ge)
                    TT(jj[:, :], lo[:, 0, :], hi[:, 0, :], ALU.add)
                    dr()
                    TT(fall[:, :], gef[:, :], num[:, :], ALU.max)
                    V.tensor_scalar(jj[:, :], jj[:, :], 0.5, None, ALU.mult)
                    dr()
                    V.copy_predicated(out=T[:, 0, :], mask=fall[:, :], data=jj[:, :])
                    dr()

                def count(at, into):
                    for c, i in enumerate(tiles):
                        V.tensor_scalar(hit[:, 0:width(i)], scores[:, c, 0:width(i)], at[:, c:c + 1] if len(at.shape) == 2 else at[:, c], 0.0,
                                        ALU.is_ge, ALU.add, accum_out=into[:, c:c + 1])
                        dr()

                def narrow():
                    count(T[:, 0, :], T[:, 1, :])
                    TT(ge[:, :], T[:, 1, :], kt[:, :], ALU.is_ge)
                    TT(lt[:, :], T[:, 1, :], kt[:, :], ALU.is_lt)
                    dr()
                    V.copy_predicated(out=lo[:, :, :], mask=B3(ge[:, :]), data=T[:, :, :])
                    V.copy_predicated(out=hi[:, :, :], mask=B3(lt[:, :]), data=T[:, :, :])
                    dr()
                inside()
                narrow()
                V.tensor_scalar(gef[:, :], ge[:, :], 8.0, -4.0, ALU.mult, ALU.add)
                TT(num[:, :], T[:, 1, :], k4[:, :], ALU.subtract)
                dr()
                TT(num[:, :], num[:, :], gef[:, :], ALU.add)
                dr()
                TT(num[:, :], num[:, :], slope[:, :], ALU.mult)
                dr()
                TT(T[:, 0, :], T[:, 0, :], num[:, :], ALU.add)
                dr()
                inside()
                narrow()
                def between():
                    TT(gap[:, :, :], lo[:, :, :], hi[:, :, :], ALU.subtract)
                    TT(num[:, :], lo[:, 1, :], k4[:, :], ALU.subtract)
                    dr()
                    V.reciprocal(jj[:, :], gap[:, 1, :])
                    dr()
                    TT(num[:, :], num[:, :], jj[:, :], ALU.mult)
                    dr()
                    V.tensor_scalar(num[:, :], num[:, :], 0.75, 0.125, ALU.mult, ALU.add)
                    dr()
                    TT(num[:, :], num[:, :], gap[:, 0, :], ALU.mult)
                    dr()
                    TT(T[:, 0, :], lo[:, 0, :], num[:, :], ALU.subtract)
                    dr()
                    TT(T[:, 0, :], T[:, 0, :], hi[:, 0, :], ALU.min)
                    dr()
                for op_lo, op_hi, guess in ((ALU.is_le, ALU.is_gt, tiny), (ALU.is_lt, ALU.is_equal, zero)):
                    between()
                    V.tensor_scalar(gef[:, :], lo[:, 0, :], 0.0, None, op_lo)
                    dr()
                    V.scalar_tensor_tensor(upd[:, :], hi[:, 0, :], TINY, gef[:, :], op_hi, ALU.mult)
                    dr()
                    V.copy_predicated(out=T[:, 0, :], mask=upd[:, :], data=guess[:, :])
                    dr()
                    narrow()
                with V.Fori(0, SEARCH - 4):
                    between()
                    narrow()

                def eight_below():
                    for c, i in enumerate(tiles):
                        s = scores[:, c, 0:width(i)]
                        V.tensor_scalar(run[:, 0:width(i)], s, hi[:, 0, c:c + 1], NEG, ALU.is_ge, ALU.mult)
                        dr()
                        TT(run[:, 0:width(i)], run[:, 0:width(i)], s, ALU.add)
                        dr()
                        V.max(m8[:, c, :], run[:, 0:width(i)])
                        dr()
                    TT(jj[:, :], kt[:, :], hi[:, 1, :], ALU.subtract)
                    TT(num[:, :], lo[:, 0, :], m8[:, :, 7], ALU.is_ge)
                    dr()
                    V.tensor_scalar(more[:, :], jj[:, :], 8.0, None, ALU.is_gt)
                    dr()
                    TT(more[:, :], more[:, :], num[:, :], ALU.is_gt)
                    dr()
                    V.tensor_reduce(flag[:, 0:1], more[:, :], AX.X, ALU.max)
                    dr()
                    V.transpose(flagT[:, :], flag[:, :])
                    dr()
                    V.reduce_max(flag1[:, :], flagT[:, :], AX.X)
                    dr()
                    V.tensor_copy(flagi[:, :], flag1[:, :])
                    dr()
                    return sum(V.value_load(flagi[32 * q:32 * q + 1, 0:1], min_val=0, max_val=1) for q in range(4))
                left = V.alloc_register(f"left{gno}")
                V.reg_mov(left, eight_below())
                with V.While(left):
                    V.tensor_copy(T[:, 0, :], m8[:, :, 7])
                    dr()
                    narrow()
                    V.reg_mov(left, eight_below())
                V.tensor_scalar(jc[:, :], jj[:, :], 8.0, -1.0, ALU.min, ALU.add)
                dr()
                TT(hot[:, :, :], part(mem.cst, "iota").rearrange("p (c e) -> p c e", e=8), B8(jc[:, :]), ALU.is_equal)
                dr()
                TT(hot[:, :, :], hot[:, :, :], m8[:, :, :], ALU.mult)
                dr()
                V.tensor_reduce(T[:, 0, :], hot[:, :, :], AX.X, ALU.add)
                dr()
                TT(hot[:, :, :], m8[:, :, :], B8(T[:, 0, :]), ALU.is_gt)
                dr()
                V.tensor_reduce(above[:, :], hot[:, :, :], AX.X, ALU.add)
                dr()
                TT(tie_room[:, :], jj[:, :], above[:, :], ALU.subtract)
                dr()
                for c, i in enumerate(tiles):
                    w = width(i)
                    s, e, k = scores[:, c, 0:w], hit[:, 0:w], run[:, 0:w]
                    V.tensor_scalar(e, s, T[:, 0, c:c + 1], None, ALU.is_equal)
                    dr()
                    V.tensor_tensor_scan(k, e, e, 0.0, ALU.add, ALU.max)
                    dr()
                    V.scalar_tensor_tensor(k, k, tie_room[:, c:c + 1], e, ALU.is_le, ALU.mult)
                    dr()
                    V.scalar_tensor_tensor(k, s, T[:, 0, c:c + 1], k, ALU.is_gt, ALU.add)
                    dr()
                    V.tensor_scalar(scores[:, c, :].bitcast(bf16)[:, 0:w], k, -1.0, -NEG, ALU.add, ALU.mult).then_inc(mask_ready, 1)
                    dr()

TILE_ORDER = [LAST] + list(range(LAST - 1, -1, -1))
HALFW = NT * P // 2


KEYS = [range(a, min(a + UNIT // P, NT)) for a in range(0, NT, UNIT // P)]


def attend_and_convolve(nc, t, mem):
    pairs = [(i, j) for i in TILE_ORDER for j in range(GRP)]
    NP_ = len(pairs)
    ujobs = [("kT", g, n) for g in range(len(KEYS)) for n in range(NKV)] + [("bias", 0), ("cw", 0), ("S", 0)]
    for p, (i, j) in enumerate(pairs):
        ujobs += [("L", p, side, a, k) for side in range(2) for a, k in pieces(i)]
    u_no = {j: n for n, j in enumerate(ujobs)}
    nblk = lambda i: -(-width(i) // P)
    groups = lambda i: [(b, min(2, nblk(i) - b)) for b in range(0, nblk(i), 2)]
    ptjobs = [("own", 0)] + [("page", b) for b in range(NS)] + [("sT", 0), ("sP", 0)]
    for p, (i, j) in enumerate(pairs):
        ptjobs += [("T", p, b, k) for b, k in groups(i)]
        if j == GRP - 1:
            ptjobs.append(("R", p))
    pt_no = {j: n for n, j in enumerate(ptjobs)}
    tjobs = [j for j in ptjobs if j[0] == "T"]
    t_no = {j: n for n, j in enumerate(tjobs)}
    pv_after = lambda p: NS + 1 + sum(len(groups(i)) for i, _ in pairs[:p + 1])
    tile_no = {i: n for n, i in enumerate(TILE_ORDER)}
    band0 = lambda i: max(0, (i - 1) * P)
    dconv = [(0, 0), (1, 0), (2, 0), (0, 1), (1, 1)]
    pconv = [(3, 0), (3, 1), (2, 1)]

    def spread(widths, units):
        total, work = sum(widths[:-2]), len(units) * TAPS
        return [min(work, -(-work * sum(widths[:n]) // total)) for n in range(len(widths) + 1)]
    dtaps = spread([width(i) for i, _ in pairs], dconv)
    ptaps = spread([width(i) for i in TILE_ORDER], pconv)
    LW = NT * P
    with ExitStack() as ctx:
        sb = lambda n, s, d=f32: ctx.enter_context(nc.sbuf_tensor(n, s, d))
        sem = lambda n: ctx.enter_context(nc.semaphore(n))
        kh = sb("kh", [128, NKV, LW], f32r)
        kl = sb("kl", [128, NKV, LW], f32r)
        vs = sb("vs", [128, NT, 128])
        L = sb("L", [128, 4, LW])
        kn = sb("kn", [128, NT, NKV, HD])
        cwn = sb("cwn", [TAPS, C])
        band = sb("band", [128, NH, 2 * P])
        bm = sb("bm", [128, 2, NH, 2 * P])
        mask = sb("mask", [128, 2, LP], bf16)
        qt = sb("qt", [128, 2, NH, P], f32r)
        gate = sb("gate", [128, 2, GRP, P])
        pts = sb("pts", [128, 3, 4 * P])
        rb = sb("rb", [128, 2, GRP, P])
        mix = sb("mix", [128, 2, GRP, P])
        es = sb("es", [128, 2, NH])
        ri = sb("ri", [128, 2, NH])
        rx = sb("rx", [128, GRP, 2, HD])
        mx = sb("mx", [128, 4, 6])
        nm = sb("nm", [128, 4])
        bc = sb("bc", [32, BANDX + LS])
        rel = sb("rel", [32, NH])
        relrep = sb("relrep", [32, NS, NH])
        rrow = sb("rrow", [NH, BANDX])
        qp = sb("qp", [128, NS, NS * NH])
        own = sb("own", [NS, 2 * 128])
        ownT = sb("ownT", [128, NS])
        m16b = sb("m16b", [NS, LS], bf16)
        m16 = sb("m16", [NS, LS])
        sS = sb("sS", [NS * NH, LS])
        smx, ssum = sb("smx", [NS * NH, 1]), sb("ssum", [NS * NH, 1])
        spick = sb("spick", [NS * NH, NS])
        sown = sb("sown", [NS, NS * NH])
        som = sb("som", [128, GRP, NS])
        cu = sb("cu", [128, 2, HALFW + TAPS - 1])
        cy = sb("cy", [128, 2, HALFW])
        pu = sb("pu", [128, HALFW + TAPS - 1])
        py = sb("py", [128, HALFW])
        ptmp = sb("ptmp", [128, HALFW])
        cw, cb = mem.cw, mem.cb
        ptab = sb("ptab2", [1, NS * NPAGE], i32)
        U = ctx.enter_context(nc.psum_tensor("psU", [128, 2, UNIT], f32))
        PT = ctx.enter_context(nc.psum_tensor("psT", [128, 2, 512], f32))
        OT = ctx.enter_context(nc.psum_tensor("psO", [128, 2, 512], f32))
        kpage = L[:, 0:2, :].rearrange("p a b -> p (a b)")[:, 0:NS * NPAGE * 128].rearrange("p (n d) -> p n d", d=128)
        vpage = L[:, 2:4, :].rearrange("p a b -> p (a b)")[:, 0:NS * NPAGE * 128].rearrange("p (n d) -> p n d", d=128)

        kn_in = [sem(f"kn_in{g}") for g in range(len(KEYS))]
        c_in, r_out, band_in, v_in, s_in, pg_in = sem("c_in2"), sem("r_out"), sem("band_in"), sem("v_in"), sem("s_in"), sem("pg_in")
        pt_in, vp_in = sem("pt_in2"), sem("vp_in")
        q_in = [sem(f"q_in{s}") for s in range(2)]
        m_in = [sem(f"m_in{s}") for s in range(2)]
        g_in = [sem(f"g_in{s}") for s in range(2)]
        pe_u, dve_u, kh_done = sem("pe_u"), sem("dve_u"), sem("kh_done")
        pe_pt, act_pt, pe_pv = sem("pe_pt"), sem("act_pt"), sem("pe_pv")
        nm_ready, exp_done, ri_ready, bm_ready, tile_done = sem("nm_ready"), sem("exp_done"), sem("ri_ready"), sem("bm_ready"), sem("tile_done")
        mix_out = [sem(f"mix_out{s}") for s in range(2)]
        rrow_done, rel_done, m16_done, s_neg, s_exp, s_norm = sem("rrow_done"), sem("rel_done"), sem("m16_done"), sem("s_neg"), sem("s_exp"), sem("s_norm")
        spick_done, som_done, pad_done = sem("spick_done"), sem("som_done"), sem("pad_done")
        cu_in = [sem(f"cu_in{s}") for s in range(2)]
        cy_out = [sem(f"cy_out{s}") for s in range(2)]
        pu_in, py_out, conv_done, pconv_done, cz, pstep, cw_in, cb_in, cw_done = [sem(x) for x in ("pu_in", "py_out", "conv_done", "pconv_done", "cz", "pstep", "cw_in", "cb_in", "cw_done")]
        block = ctx.enter_context(nc.Block())

        def tile_of_step(p):
            return pairs[p][0] if 0 <= p < NP_ and pairs[p][1] == GRP - 1 else None

        @block.sync
        def _(sp):
            sp.dma_start(ptab[:, :], t.page_table.rearrange("b n -> (b n)").unsqueeze(0)).then_inc(pt_in, 16)
            for g, tiles in enumerate(KEYS):
                r = slice(tiles[0] * P, (tiles[-1] + 1) * P)
                if tiles[-1] < LAST:
                    sp.dma_start(kn[:, tiles[0]:tiles[-1] + 1].rearrange("p i n d -> p i (n d)"),
                                 t.nk_p[0, 0, r].rearrange("(i p) n d -> p i (n d)", p=P)).then_inc(kn_in[g], 16)
                else:
                    sp.dma_start(kn[0:LREM, LAST].rearrange("p n d -> p (n d)"),
                                 t.nk_p[0, 0, LAST * P:LP].rearrange("p n d -> p (n d)")).then_inc(kn_in[g], 16)
            sp.dma_start(bc[:, :], t.consts[0:32, NCONST:NCONST + BANDX + LS]).then_inc(c_in, 16)
            sp.dma_start(rel[:, :], t.rel_bias).then_inc(c_in, 16)
            sp.dma_start(cwn[:, :], t.conv_w[0]).then_inc(cw_in, 16)
            sp.dma_start(cb[:, :], t.conv_b[0].rearrange("(c p) -> p c", p=128), allow_slow_non_contiguous=True).then_inc(cb_in, 16)
            sp.dma_start(qp[:, :, :].rearrange("p a b -> p (a b)"), t.d_qs).then_inc(s_in, 16)
            sp.dma_start(own[:, 0:128], t.nk_s[0, :, 0].rearrange("b n d -> b (n d)")).then_inc(s_in, 16)
            sp.dma_start(own[:, 128:256], t.nv_s[0, :, 0].rearrange("b n d -> b (n d)")).then_inc(s_in, 16)
            sp.dma_start(m16b[:, :], t.d_mask[LAST, SROW:SROW + NS, 0:LS]).then_inc(s_in, 16)

            def load_tile(n):
                i = TILE_ORDER[n]
                s = n % 2
                if n >= 2:
                    sp.wait_ge(tile_done, n - 1)
                sp.dma_start(qt[:, s].bitcast(f32), t.d_q[i]).then_inc(q_in[s], 16)
                sp.dma_start(gate[:, s], t.d_ga[:, :, i * P:(i + 1) * P].rearrange("c p t -> p c t")).then_inc(g_in[s], 16)
                if i >= 2:
                    sp.dma_start(mask[:, s, 0:width(i)], t.d_mask[i, :, 0:width(i)]).then_inc(m_in[s], 16)

            def load_u(e, units, dst, s):
                c, h = units[e]
                if h == 0:
                    sp.dma_start(dst[:, TAPS - 1:], t.d_u[c, :, 0:HALFW]).then_inc(s, 16)
                else:
                    sp.dma_start(dst[:, :], t.d_u[c, :, HALFW - (TAPS - 1):2 * HALFW]).then_inc(s, 16)
            sp.wait_ge(pt_in, 16)
            half = NS * NPAGE // 2
            load_pages(sp, range(half), ptab, t.cache_k, "o s n d -> (o s) (n d)", kpage, pg_in)
            load_pages(sp, range(NS * NPAGE), ptab, t.cache_v, "o s n d -> (o s) (n d)", vpage, vp_in)
            load_tile(0)
            sp.wait_ge(rrow_done, 1)
            sp.dma_start(t.d_r.rearrange("t h x -> h t x"), rrow[:, :].unsqueeze(1).to_broadcast([NH, P, BANDX])).then_inc(r_out, 16)
            sp.wait_ge(r_out, 16)
            sp.dma_start(band[:, :, :], bass.AP(t.d_r.tensor, P - 1, [[NH * BANDX - 1, P], [BANDX, NH], [1, 2 * P]])).then_inc(band_in, 16)
            sp.dma_start(vs[:, 0:LAST, :], t.nv_p[0, 0, 0:LAST * P].rearrange("(i p) n d -> p i (n d)", p=P)).then_inc(v_in, 16)
            sp.dma_start(vs[0:LREM, LAST, :], t.nv_p[0, 0, LAST * P:LP].rearrange("p n d -> p (n d)")).then_inc(v_in, 16)
            load_tile(1)
            sp.wait_ge(cz, 2)
            load_u(0, dconv, cu[:, 0], cu_in[0])
            load_u(1, dconv, cu[:, 1], cu_in[1])
            load_u(0, pconv, pu[:, :], pu_in)
            dunit = punit = 0
            for p in range(NP_ + 3):
                while dunit < len(dconv) and 1 <= p <= NP_ and dtaps[p - 1] >= (dunit + 1) * TAPS:
                    sp.wait_ge(conv_done, dunit + 1)
                    c, h = dconv[dunit]
                    sp.dma_start(t.d_y[c, :, h * HALFW:(h + 1) * HALFW], cy[:, dunit % 2]).then_inc(cy_out[dunit % 2], 16)
                    if dunit + 2 < len(dconv):
                        load_u(dunit + 2, dconv, cu[:, dunit % 2], cu_in[dunit % 2])
                    dunit += 1
                if tile_of_step(p - 2) is not None:
                    n = tile_no[tile_of_step(p - 2)]
                    sp.wait_ge(tile_done, n + 1)
                    sp.dma_start(t.d_mix[TILE_ORDER[n]], mix[:, n % 2]).then_inc(mix_out[n % 2], 16)
                    if n + 2 < NT:
                        load_tile(n + 2)
                    while punit < len(pconv) and ptaps[min(n + 2, NT)] > (punit + 1) * TAPS:
                        sp.wait_ge(pconv_done, punit + 1)
                        c, h = pconv[punit]
                        sp.dma_start(t.d_y[c, :, h * HALFW:(h + 1) * HALFW], py[:, :]).then_inc(py_out, 16)
                        if punit + 1 < len(pconv):
                            load_u(punit + 1, pconv, pu[:, :], pu_in)
                        punit += 1
            while dunit < len(dconv):
                sp.wait_ge(conv_done, dunit + 1)
                c, h = dconv[dunit]
                sp.dma_start(t.d_y[c, :, h * HALFW:(h + 1) * HALFW], cy[:, dunit % 2]).then_inc(cy_out[dunit % 2], 16)
                dunit += 1
            while punit < len(pconv):
                sp.wait_ge(pconv_done, punit + 1)
                c, h = pconv[punit]
                sp.dma_start(t.d_y[c, :, h * HALFW:(h + 1) * HALFW], py[:, :]).then_inc(py_out, 16)
                punit += 1
            for s in range(2):
                sp.wait_ge(mix_out[s], 16 * len(TILE_ORDER[s::2]))
                sp.wait_ge(cy_out[s], 16 * len(dconv[s::2]))
            sp.wait_ge(py_out, 16 * len(pconv))

        @block.gpsimd
        def _(pool):
            G = nc.gpsimd
            G.memset(cu[:, 0, 0:TAPS - 1], 0.0)
            G.memset(cu[:, 1, 0:TAPS - 1], 0.0).then_inc(cz, 1)
            G.memset(pu[:, 0:TAPS - 1], 0.0).then_inc(cz, 1)
            steps = [0]

            def chained(ins):
                steps[0] += 1
                ins.then_inc(pstep, 1)
                pool.wait_ge(pstep, steps[0])
            pool.wait_ge(cw_done, 1)
            pool.wait_ge(cb_in, 16)

            def conv_tap(tap):
                e, k = divmod(tap, TAPS)
                c, h = pconv[e]
                w = cw[:, c, k:k + 1]
                if k == 0:
                    pool.wait_ge(pu_in, 16 * (e + 1))
                    if e:
                        pool.wait_ge(py_out, 16 * e)
                    chained(G.tensor_scalar(py[:, :], pu[:, 0:HALFW], w, cb[:, c:c + 1], ALU.mult, ALU.add))
                else:
                    chained(G.tensor_scalar(ptmp[:, :], pu[:, k:k + HALFW], w, 0.0, ALU.mult, ALU.add))
                    chained(G.tensor_tensor(out=py[:, :], in0=py[:, :], in1=ptmp[:, :], op=ALU.add))
                if k == TAPS - 1:
                    G.sem_inc(pconv_done, 1)
            pool.wait_ge(band_in, 16)

            def band_mask(n):
                i = TILE_ORDER[n]
                s = n % 2
                a, k = band0(i), width(i) - band0(i)
                j0 = a - (i - 1) * P
                if n >= 2:
                    pool.wait_ge(tile_done, n - 1)
                if i >= 2:
                    pool.wait_ge(m_in[s], 16 * (n // 2 + 1))
                else:
                    chained(G.memset(mask[:, s, 0:P], 0.0))
                    chained(G.tensor_copy(mask[:, s, i * P:(i + 1) * P], part(mem.cst, "causal")))
                G.tensor_tensor(out=bm[:, s, :, 0:k], in0=band[:, :, j0:j0 + k],
                                in1=mask[:, s, a:a + k].unsqueeze(1).to_broadcast([128, NH, k]), op=ALU.add).then_inc(bm_ready, 1)
            band_mask(0)
            for n in range(NT):
                half = (ptaps[n] + ptaps[n + 1]) // 2
                for tap in range(ptaps[n], half):
                    conv_tap(tap)
                if n + 1 < NT:
                    band_mask(n + 1)
                for tap in range(half, ptaps[n + 1]):
                    conv_tap(tap)

        @block.scalar
        def _(act):
            A = nc.scalar

            def evac(job, out, src):
                act.wait_ge(pe_pt, pt_no[job] + 1)
                A.activation(out, src, ACT.Copy).then_inc(act_pt, 1)
            act.wait_ge(c_in, 32)
            A.activation(relrep[:, :, :], rel[:, :].unsqueeze(1).to_broadcast([32, NS, NH]), ACT.Copy).then_inc(rel_done, 1)
            for g, tiles in enumerate(KEYS):
                for n in range(NKV):
                    job = u_no["kT", g, n]
                    a = tiles[0] * P
                    k = width(tiles[-1]) - a
                    act.wait_ge(pe_u, job + 1)
                    A.activation(kh[:, n, a:a + k], U[:, job % 2, 0:k], ACT.Copy).then_inc(kh_done, 1)
            act.wait_ge(pt_in, 16)
            half = NS * NPAGE // 2
            load_pages(act, range(half, 2 * half), ptab, t.cache_k, "o s n d -> (o s) (n d)", kpage, pg_in)
            act.wait_ge(s_in, 64)
            A.activation(m16[:, :], m16b[:, :], ACT.Copy).then_inc(m16_done, 1)
            evac(("own", 0), ownT[:, :], PT[:, 0, 0:NS])
            for b in range(NS):
                if b >= 3:
                    act.wait_ge(pe_pv, b - 2)
                evac(("page", b), pts[:, b % 3, :], PT[:, pt_no["page", b] % 2, :])
            act.wait_ge(s_neg, 1)
            A.activation(sS[:, :], sS[:, :], ACT.Exp, bias=smx[:, :], accum_out=ssum[:, :]).then_inc(s_exp, 1)
            act.wait_ge(pe_pv, NS)
            evac(("sT", 0), pts[:, 0, 0:256], PT[:, pt_no["sT", 0] % 2, 0:256])
            evac(("sP", 0), sown[:, :], PT[0:NS, pt_no["sP", 0] % 2, 0:NS * NH])

            def exps(p):
                i, j = pairs[p]
                for side in range(2):
                    act.wait_ge(nm_ready, 2 * p + side + 1)
                    b = (2 * p + side) % 4
                    A.activation(L[:, b, 0:width(i)], L[:, b, 0:width(i)], ACT.Exp, bias=nm[:, b:b + 1],
                                 accum_out=es[:, tile_no[i] % 2, j + 4 * side:j + 4 * side + 1]).then_inc(exp_done, 1)
            exps(0)
            for p, (i, j) in enumerate(pairs):
                for b, k in groups(i):
                    job = ("T", p, b, k)
                    n = t_no[job]
                    act.wait_ge(pe_pv, NS + 1 + max(0, n - 2))
                    kk = min(P, width(i) - b * P)
                    m = 2 * k * P
                    evac(job, pts[:, n % 3, 0:m], PT[:, pt_no[job] % 2, 0:m])
                if j == GRP - 1:
                    n = tile_no[i]
                    if n >= 2:
                        act.wait_ge(tile_done, n - 1)
                    evac(("R", p), rb[:, n % 2].rearrange("p c t -> p (c t)"), PT[:, pt_no["R", p] % 2, :])
                if p + 1 < NP_:
                    if j == GRP - 1 and tile_no[i] >= 1:
                        act.wait_ge(ri_ready, tile_no[i])
                    exps(p + 1)

        @block.vector
        def _(dve):
            V = nc.vector
            dr = V.drain
            TT = lambda out, a, b, op: V.tensor_tensor(out=out, in0=a, in1=b, op=op)
            for g, tiles in enumerate(KEYS):
                for n in range(NKV):
                    job = u_no["kT", g, n]
                    a = tiles[0] * P
                    k = width(tiles[-1]) - a
                    dve.wait_ge(kh_done, NKV * g + n + 1)
                    TT(kl[:, n, a:a + k], U[:, job % 2, 0:k], kh[:, n, a:a + k].bitcast(f32), ALU.subtract).then_inc(dve_u, 1)
            job = u_no["bias", 0]
            dve.wait_ge(pe_u, job + 1)
            V.tensor_copy(rrow[:, :], U[0:NH, job % 2, 0:BANDX]).then_inc(dve_u, 1)
            dr().then_inc(rrow_done, 1)
            job = u_no["cw", 0]
            dve.wait_ge(pe_u, job + 1)
            V.tensor_copy(cw[:, :, :].rearrange("p c k -> p (c k)"), U[:, job % 2, 0:CC * TAPS]).then_inc(dve_u, 1)
            dr().then_inc(cw_done, 1)
            job = u_no["S", 0]
            dve.wait_ge(pe_u, job + 1)
            V.tensor_copy(sS[:, :], U[0:NS * NH, job % 2, 0:LS]).then_inc(dve_u, 1)
            dr()
            V.tensor_reduce(smx[:, :], sS[:, :], AX.X, ALU.max, negate=True).then_inc(s_neg, 1)
            dve.wait_ge(s_exp, 1)
            V.reciprocal(ssum[:, :], ssum[:, :])
            dr()
            V.tensor_scalar(sS[:, :], sS[:, :], ssum[:, 0:1], None, ALU.mult).then_inc(s_norm, 1)
            dr()
            V.tensor_scalar(spick[:, :], part(mem.cst, "e8t")[0:NS * NH, 0:NS], sS[:, PAST:LS], None, ALU.mult).then_inc(spick_done, 1)
            dve.wait_ge(pe_pv, NS + 1)
            for side in range(2):
                rows = slice(64 * side, 64 * side + 64)
                V.tensor_copy(som[rows, :, :], OT[rows, 0, 0:NS * NH].rearrange("p (b g h) -> p g h b", b=NS, g=2)[:, side])
            V.memset(L[:, :, LP:LW], 0.0).then_inc(pad_done, 1)
            dr().then_inc(som_done, 1)

            def conv_tap(tap):
                e, k = divmod(tap, TAPS)
                c, h = dconv[e]
                w = cw[:, c, k:k + 1]
                y, u = cy[:, e % 2], cu[:, e % 2]
                if k == 0:
                    dve.wait_ge(cu_in[e % 2], 16 * (e // 2 + 1))
                    if e >= 2:
                        dve.wait_ge(cy_out[e % 2], 16 * (e // 2))
                    V.tensor_scalar(y, u[:, 0:HALFW], w, cb[:, c:c + 1], ALU.mult, ALU.add)
                else:
                    V.scalar_tensor_tensor(y, u[:, k:k + HALFW], w, y, ALU.mult, ALU.add)
                if k == TAPS - 1:
                    dr().then_inc(conv_done, 1)
                else:
                    dr()

            def finish(n):
                i = TILE_ORDER[n]
                s = n % 2
                dve.wait_ge(act_pt, pt_no["R", (n + 1) * GRP - 1] + 1)
                dve.wait_ge(g_in[s], 16 * (n // 2 + 1))
                if n >= 2:
                    dve.wait_ge(mix_out[s], 16 * (n // 2))
                TT(rb[:, s], rb[:, s], gate[:, s], ALU.mult)
                dr()
                dve.wait_ge(pe_pv, pv_after((n + 1) * GRP - 1))
                TT(mix[:, s], OT[:, s, :].rearrange("p (c t) -> p c t", t=P), rb[:, s], ALU.mult)
                if i == LAST:
                    dr()
                    TT(mix[:, s, :, SROW:SROW + NS], som[:, :, :], gate[:, s, :, SROW:SROW + NS], ALU.mult)
                dr().then_inc(tile_done, 1)

            def invert(n):
                V.reciprocal(ri[:, n % 2, :], es[:, n % 2, :])
                dr()
                V.tensor_copy(rx[:, :, :, :], ri[:, n % 2, :].rearrange("p (a g) -> p g a", a=NKV).unsqueeze(3)
                              .to_broadcast([128, GRP, NKV, HD])).then_inc(ri_ready, 1)
            dve.wait_ge(cb_in, 16)
            for p, (i, j) in enumerate(pairs):
                n = tile_no[i]
                s = n % 2
                if j == 0:
                    dve.wait_ge(bm_ready, n + 1)
                    if i >= 2:
                        dve.wait_ge(m_in[s], 16 * (n // 2 + 1))
                if p >= 2:
                    dve.wait_ge(pe_pv, pv_after(p - 2))
                for side in range(2):
                    head, b = j + 4 * side, (2 * p + side) % 4
                    m = 0
                    for a, k in pieces(i):
                        job = u_no["L", p, side, a, k]
                        dve.wait_ge(pe_u, job + 1)
                        bs = band0(i)
                        spans = [(a, min(a + k, bs), mask[:, s, :]), (max(a, bs), a + k, None)]
                        spans = [x for x in spans if x[0] < x[1]]
                        for x0, x1, far in spans:
                            in1 = mask[:, s, x0:x1] if far is not None else bm[:, s, head, x0 - bs:x1 - bs]
                            last = V.tensor_tensor_reduce(out=L[:, b, x0:x1], in0=U[:, job % 2, x0 - a:x1 - a], in1=in1,
                                                          scale=1.0, scalar=3 * NEG, op0=ALU.add, op1=ALU.max, accum_out=mx[:, b, m:m + 1])
                            m += 1
                        last.then_inc(dve_u, 1)
                    dr()
                    V.tensor_reduce(nm[:, b:b + 1], mx[:, b, 0:m], AX.X, ALU.max, negate=True).then_inc(nm_ready, 1)
                if p and pairs[p - 1][1] == GRP - 1:
                    nn = tile_no[pairs[p - 1][0]]
                    dve.wait_ge(exp_done, 2 * p)
                    invert(nn)
                if p >= 2 and pairs[p - 2][1] == GRP - 1:
                    finish(tile_no[pairs[p - 2][0]])
                for tap in range(dtaps[p], dtaps[p + 1]):
                    conv_tap(tap)
            dve.wait_ge(exp_done, 2 * NP_)
            invert(NT - 1)
            finish(NT - 1)

        @block.tensor
        def _(pe):
            ident = part(mem.cst, "ident")
            T = nc.tensor

            def take_u(job):
                n = u_no[job]
                if n >= 2:
                    pe.wait_ge(dve_u, n - 1)
                return U[:, n % 2]

            def take_pt(job):
                n = pt_no[job]
                if n >= 2:
                    pe.wait_ge(act_pt, n - 1)
                return PT[:, n % 2]
            for g, tiles in enumerate(KEYS):
                pe.wait_ge(kn_in[g], 16)
                for n in range(NKV):
                    u = take_u(("kT", g, n))
                    for e, i in enumerate(tiles):
                        k = P if i < LAST else LREM
                        for side in range(2):
                            last = T.matmul(u[64 * side:64 * side + 64, e * P:e * P + k], kn[0:k, i, n], ident[0:k, 0:k],
                                            start=True, stop=True)
                    last.then_inc(pe_u, 1)
            pe.wait_ge(c_in, 32)
            T.matmul(take_u(("bias", 0))[0:NH, 0:BANDX], rel[:, :], bc[:, 0:BANDX], start=True, stop=True).then_inc(pe_u, 1)
            pe.wait_ge(cw_in, 16)
            u = take_u(("cw", 0))
            for c in range(CC):
                last = T.transpose(u[:, c * TAPS:(c + 1) * TAPS], cwn[:, c * P:(c + 1) * P], ident[0:TAPS, 0:TAPS])
            last.then_inc(pe_u, 1)
            pe.wait_ge(s_in, 64)
            T.transpose(take_pt(("own", 0))[:, 0:NS], own[:, 0:128], ident[0:NS, 0:NS]).then_inc(pe_pt, 1)
            pe.wait_ge(pg_in, 16 * NS * NPAGE)
            S = take_u(("S", 0))

            def page(b):
                pt = take_pt(("page", b))
                for g in range(NPAGE):
                    last = T.transpose(pt[:, g * P:(g + 1) * P], kpage[:, b * NPAGE + g, :], ident)
                last.then_inc(pe_pt, 1)
            page(0)
            for b in range(NS):
                if b + 1 < NS:
                    page(b + 1)
                pe.wait_ge(act_pt, pt_no["page", b] + 1)
                T.matmul(S[0:NS * NH, 0:PAST], qp[:, b, :], pts[:, b % 3, :], start=(b == 0), stop=False).then_inc(pe_pv, 1)
            pe.wait_ge(m16_done, 1)
            pe.wait_ge(rel_done, 1)
            e8 = part(mem.cst, "e8")[0:NS, :]
            rr = relrep[:, :, :].rearrange("p b h -> p (b h)")
            T.matmul(S[0:NS * NH, 0:PAST], e8, m16[:, 0:PAST], start=False, stop=False)
            T.matmul(S[0:NS * NH, 0:PAST], rr, bc[:, BANDX:BANDX + PAST], start=False, stop=True)
            for b in range(NS):
                T.matmul(S[0:NS * NH, PAST:LS], qp[:, b, :], ownT[:, b:b + 1], start=(b == 0), stop=False)
            T.matmul(S[0:NS * NH, PAST:LS], e8, m16[:, PAST:LS], start=False, stop=False)
            T.matmul(S[0:NS * NH, PAST:LS], rr, bc[:, BANDX + PAST:BANDX + LS], start=False, stop=True).then_inc(pe_u, 1)
            pe.wait_ge(s_norm, 1)
            pt = take_pt(("sT", 0))
            for g in range(NPAGE):
                last = T.transpose(pt[:, g * 64:(g + 1) * 64], sS[:, g * P:(g + 1) * P], ident[0:64, 0:64])
            last.then_inc(pe_pt, 1)
            pe.wait_ge(spick_done, 1)
            T.matmul(take_pt(("sP", 0))[0:NS, 0:NS * NH], spick[:, :], ident[0:64, 0:64], start=True, stop=True).then_inc(pe_pt, 1)
            pe.wait_ge(act_pt, pt_no["sP", 0] + 1)
            pe.wait_ge(vp_in, 16 * NS * NPAGE)
            T.matmul(OT[:, 0, 0:NS * NH], own[:, 128:256], sown[:, :], start=True, stop=False, skip_group_check=True)
            for b in range(NS):
                for g in range(NPAGE):
                    last = T.matmul(OT[:, 0, b * NH:(b + 1) * NH], vpage[:, b * NPAGE + g, :],
                                    pts[:, 0, g * 64 + b * NH:g * 64 + (b + 1) * NH], start=False,
                                    stop=(b == NS - 1 and g == NPAGE - 1), skip_group_check=True)
            last.then_inc(pe_pv, 1)

            def logits(p):
                i, j = pairs[p]
                s = tile_no[i] % 2
                if j == 0:
                    pe.wait_ge(q_in[s], 16 * (tile_no[i] // 2 + 1))
                if p == 0:
                    pe.wait_ge(dve_u, u_no["S", 0] + 1)
                for side in range(2):
                    q = qt[:, s, j + 4 * side, :]
                    for a, k in pieces(i):
                        u = take_u(("L", p, side, a, k))
                        for b0 in range(0, k, 512):
                            bn = min(512, k - b0)
                            T.matmul(u[:, b0:b0 + bn], q, kh[:, side, a + b0:a + b0 + bn], start=True, stop=False)
                            last = T.matmul(u[:, b0:b0 + bn], q, kl[:, side, a + b0:a + b0 + bn], start=False, stop=True)
                        last.then_inc(pe_u, 1)

            def transposes(p, b, k):
                pt = take_pt(("T", p, b, k))
                for side in range(2):
                    for e in range(k):
                        last = T.transpose(pt[:, (side * k + e) * P:(side * k + e + 1) * P],
                                           L[:, (2 * p + side) % 4, (b + e) * P:(b + e + 1) * P], ident)
                last.then_inc(pe_pt, 1)

            def products(p, b, k):
                i, j = pairs[p]
                job = ("T", p, b, k)
                pe.wait_ge(act_pt, pt_no[job] + 1)
                for e in range(k):
                    rows = min(P, width(i) - (b + e) * P)
                    for side in range(2):
                        last = T.matmul(OT[64 * side:64 * side + 64, tile_no[i] % 2, j * P:(j + 1) * P],
                                        vs[0:rows, b + e, 64 * side:64 * side + 64],
                                        pts[0:rows, t_no[job] % 3, (side * k + e) * P:(side * k + e + 1) * P],
                                        start=(b + e == 0), stop=(b + e == nblk(i) - 1))
                last.then_inc(pe_pv, 1)
            logits(0)
            pe.wait_ge(v_in, 32)
            pe.wait_ge(pad_done, 1)
            for p, (i, j) in enumerate(pairs):
                if p + 1 < NP_:
                    logits(p + 1)
                pe.wait_ge(exp_done, 2 * p + 2)
                if j == 0:
                    if p == 0:
                        pe.wait_ge(som_done, 1)
                    if tile_no[i] >= 2:
                        pe.wait_ge(tile_done, tile_no[i] - 1)
                gs = groups(i)
                transposes(p, *gs[0])
                for e, g in enumerate(gs):
                    if e + 1 < len(gs):
                        transposes(p, *gs[e + 1])
                    products(p, *g)
                if j == GRP - 1:
                    n = tile_no[i]
                    pe.wait_ge(ri_ready, n + 1)
                    pt = take_pt(("R", p))
                    for jj in range(GRP):
                        last = T.matmul(pt[:, jj * P:(jj + 1) * P],
                                        rx[:, jj].rearrange("p a d -> p (a d)"), ident, start=True, stop=True)
                    last.then_inc(pe_pt, 1)


WS = 3
FS = 3
BLOCKS = [[LAST]] + [list(range(i, i + 4)) for i in range(0, LAST, 4)]


def mix_out(nc, t, mem):
    order = [i for b in BLOCKS for i in b]
    NB = len(BLOCKS)
    UW = LP - (TAPS - 1)
    SB = NS // 2 * (TAPS - 1)
    with ExitStack() as ctx:
        sb = lambda n, s, d=f32: ctx.enter_context(nc.sbuf_tensor(n, s, d))
        sem = lambda n: ctx.enter_context(nc.semaphore(n))
        wst = sb("wost", [128, WS, D])
        wh = sb("woh", [128, KC, D], f32r)
        wl = sb("wol", [128, KC, D], f32r)
        y = sb("y", [128, 2, CC, 4 * P])
        gc = sb("gc", [128, 2, CC, 4 * P])
        tmp = sb("tmp", [128, CC, 4 * P])
        z = sb("z", [128, CC, 4 * P])
        std = sb("std", [128, 2, 4 * P])
        am = sb("am", [128, FS, CC, P])
        fh = sb("fh", [128, FS, KC, P], f32r)
        fl = sb("fl", [128, FS, KC, P], f32r)
        xr = sb("xr", [128, 2, D])
        res = sb("res", [128, 2, D])
        fin = sb("fin", [128, 2, D])
        sq = sb("sq3", [128, D])
        gf = sb("gf", [128, D])
        lg, lb = sb("lg", [128, CC]), sb("lb", [128, CC])
        cw, cb = mem.cw, mem.cb
        ssq, ms, rstd = sb("ssq3", [128, NT]), sb("ms3", [128, NT]), sb("rstd3", [128, NT])
        epsb, eps6 = sb("epsb", [128, 1]), sb("eps6", [128, 1])
        st = sb("st", [SB, 2, C])
        ext = sb("ext", [128, CC, NS, TAPS])
        ys = sb("ys", [128, CC, NS])
        un = sb("un", [128, CC, TAPS - 1])
        us = sb("us", [128, CC, NS])
        uo = sb("uo", [TAPS - 1, C])
        uso = sb("uso", [NS, C])
        O = ctx.enter_context(nc.psum_tensor("psO3", [128, 2, D], f32))
        ST = ctx.enter_context(nc.psum_tensor("psS3", [128, 2, 512], f32))
        M = ctx.enter_context(nc.psum_tensor("psM3", [128, 2, 512], f32))
        w_ld = [sem(f"wo_ld{s}") for s in range(WS)]
        w_hi, w_lo = sem("wo_hi"), sem("wo_lo")
        c_in, st_in = sem("c_in3"), sem("st_in")
        y_in = [sem(f"y_in{s}") for s in range(2)]
        a_in = [sem(f"a_in{s}") for s in range(FS)]
        x_in = [sem(f"x_in3{s}") for s in range(2)]
        o_out = [sem(f"o_out{s}") for s in range(2)]
        pe_m, act_m, ext_done, ys_done, uso_out = sem("pe_m"), sem("act_m"), sem("ext_done"), sem("ys_done"), sem("uso_out")
        eps_set, zeroed = sem("eps_set"), sem("zeroed3")
        mean_done, centred, squared, var_done, std_done, normed = [sem(x) for x in
            ("mean_done", "centred", "squared", "var_done", "std_done", "normed")]
        swish_in, block_done, hi_done, lo_done, pe_o, res_done, sq_done, rstd_done, fin_done = [sem(x) for x in
            ("swish_in", "block_done", "hi_done", "lo_done", "pe_o", "res_done", "sq_done3", "rstd_done3", "fin_done")]
        block_of = {i: (b, e) for b, tiles in enumerate(BLOCKS) for e, i in enumerate(tiles)}
        n_x = [len(tile_rows(i)) for i in order]
        block = ctx.enter_context(nc.Block())

        stages = [(stage, k) for k in range(2) for stage in "abc"]
        schedule = stages[:5] + [("tile", LAST)] + stages[5:]
        for k in range(1, NB):
            after = {0: "a", 1: "b", 2: "c"} if k + 1 < NB else {}
            for e, i in enumerate(BLOCKS[k]):
                schedule.append(("tile", i))
                if e in after:
                    schedule.append((after[e], k + 1))
        dve_schedule = stages + [("tile", LAST)] + schedule[7:]

        @block.sync
        def _(sp):
            col = lambda a: a.rearrange("(c p) -> p c", p=128)
            sp.dma_start(st[:, 0, :], t.state_conv[0, 0:NS // 2].rearrange("b k c -> (b k) c")).then_inc(st_in, 16)
            sp.dma_start(st[:, 1, :], t.state_conv[0, NS // 2:NS].rearrange("b k c -> (b k) c")).then_inc(st_in, 16)
            sp.dma_start(us[:, :, :], t.d_u[:, :, LAST * P + SROW:LAST * P + SROW + NS].rearrange("c p t -> p c t")).then_inc(st_in, 16)
            sp.dma_start(un[:, :, :], t.d_u[:, :, UW:LP].rearrange("c p t -> p c t")).then_inc(st_in, 16)
            for dst, src in ((lg, t.conv_ln_g), (lb, t.conv_ln_b)):
                sp.dma_start(dst[:, :], col(src[0]), allow_slow_non_contiguous=True).then_inc(c_in, 16)
            sp.dma_start(gf[:, :], t.final_norm_g.unsqueeze(0).to_broadcast([128, D])).then_inc(c_in, 16)
            sp.dma_start(t.nconv_s[0, :, 0:TAPS - 2, :], t.state_conv[0, :, 1:TAPS - 1, :]).then_inc(uso_out, 16)

            def load_block(k):
                tiles = BLOCKS[k]
                tok = slice(tiles[0] * P, (tiles[-1] + 1) * P)
                w = len(tiles) * P
                if k >= 2:
                    sp.wait_ge(lo_done, sum(len(b) for b in BLOCKS[:k - 1]))
                sp.dma_start(y[:, k % 2, :, 0:w], t.d_y[:, :, tok].rearrange("c p t -> p c t")).then_inc(y_in[k % 2], 16)
                sp.dma_start(gc[:, k % 2, :, 0:w], t.d_gc[:, :, tok].rearrange("c p t -> p c t")).then_inc(y_in[k % 2], 16)

            def load_am(n):
                if n >= FS:
                    sp.wait_ge(lo_done, n - FS + 1)
                sp.dma_start(am[:, n % FS], t.d_mix[order[n]]).then_inc(a_in[n % FS], 16)

            def load_x(n):
                i = order[n]
                if i == LAST:
                    sp.wait_ge(zeroed, 1)
                if n >= 2:
                    sp.wait_ge(res_done, n - 1)
                for p0, rows, what, r0 in tile_rows(i):
                    src = {"meta": t.meta_tokens, "x": t.x_prompt[0], "sample": t.x_sample[:, 0, :]}[what]
                    sp.dma_start(xr[p0:p0 + rows, n % 2, :], src[r0:r0 + rows, :]).then_inc(x_in[n % 2], 16)
            load_block(0)
            for c in range(KC):
                if c >= WS:
                    sp.wait_ge(w_lo, c - WS + 1)
                if c < CC:
                    sp.dma_start(wst[:, c % WS, :], t.w_out[0, c * P:(c + 1) * P, :]).then_inc(w_ld[c % WS], 32)
                else:
                    for side in range(2):
                        r = C + 64 * (c - CC) + 256 * side
                        sp.dma_start(wst[64 * side:64 * side + 64, c % WS, :], t.w_out[0, r:r + 64, :]).then_inc(w_ld[c % WS], 16)
                if c == 0:
                    load_am(0)
                    load_x(0)
                    load_block(1)
                if c == 1:
                    load_am(1)
                    load_x(1)
                    load_am(2)
            sp.wait_ge(act_m, 1)
            sp.dma_start(t.nconv_p[0, 0], uo[:, :]).then_inc(uso_out, 16)
            sp.wait_ge(act_m, 2)
            sp.dma_start(t.nconv_s[0, :, TAPS - 2, :], uso[:, :]).then_inc(uso_out, 16)
            for n, i in enumerate(order):
                if n + FS < NT:
                    load_am(n + FS)
                b, e = block_of[i]
                if e == len(BLOCKS[b]) - 1 and b + 2 < NB:
                    load_block(b + 2)
                if n + 2 < NT:
                    load_x(n + 2)
                sp.wait_ge(fin_done, n + 1)
                rows = [(META, P - META, "p", 0)] if i == 0 else \
                    ([(0, LREM, "p", LAST * P - META), (SROW, NS, "s", 0)] if i == LAST else [(0, P, "p", i * P - META)])
                for p0, r, what, r0 in rows:
                    dst = t.y_prompt[0, r0:r0 + r, :] if what == "p" else t.y_sample[:, 0, :]
                    sp.dma_start(dst, fin[p0:p0 + r, n % 2, :]).then_inc(o_out[n % 2], 16)
            outs = [2] + [1] * (NT - 1)
            for s in range(2):
                sp.wait_ge(o_out[s], 16 * sum(outs[s::2]))
            sp.wait_ge(uso_out, 48)

        def x_arrived(eng, n):
            eng.wait_ge(x_in[n % 2], 16 * sum(n_x[n % 2:n + 1:2]))

        def out_written(eng, n):
            eng.wait_ge(o_out[n % 2], 16 * sum(([2] + [1] * (NT - 1))[n % 2:n + 1:2]))

        @block.gpsimd
        def _(pool):
            G = nc.gpsimd
            G.memset(epsb[:, :], LN_EPS).then_inc(eps_set, 1)
            G.memset(xr[:, 0, :], 0.0).then_inc(zeroed, 1)
            for c in range(KC):
                pool.wait_ge(w_hi, c + 1)
                G.tensor_tensor(out=wl[:, c, :], in0=wst[:, c % WS, :], in1=wh[:, c, :].bitcast(f32), op=ALU.subtract).then_inc(w_lo, 1)
            n = 0
            for what, k in schedule:
                if what == "tile":
                    b, e = block_of[k]
                    s = n % FS
                    pool.wait_ge(hi_done, n + 1)
                    G.tensor_tensor(out=fl[:, s, 0:CC], in0=gc[:, b % 2, :, e * P:(e + 1) * P], in1=fh[:, s, 0:CC].bitcast(f32), op=ALU.subtract)
                    G.tensor_tensor(out=fl[:, s, CC:KC], in0=am[:, s], in1=fh[:, s, CC:KC].bitcast(f32), op=ALU.subtract).then_inc(lo_done, 1)
                    n += 1
            pool.wait_ge(lo_done, NT)

        @block.scalar
        def _(act):
            A = nc.scalar
            act.wait_ge(pe_m, 1)
            A.activation(uo[:, :], M[0:TAPS - 1, 0, :], ACT.Copy).then_inc(act_m, 1)
            act.wait_ge(pe_m, 2)
            A.activation(uso[:, :], M[0:NS, 1, :], ACT.Copy).then_inc(act_m, 1)
            for e in range(4):
                act.wait_ge(pe_m, e + 3)
                c0, half = 2 * (e // 2), e % 2
                A.activation(ext[:, c0:c0 + 2, half * NS // 2:(half + 1) * NS // 2, 0:TAPS - 1],
                             M[:, e % 2, 0:2 * SB].rearrange("p (c b k) -> p c b k", c=2, b=NS // 2), ACT.Copy).then_inc(act_m, 1)
            A.activation(ext[:, :, :, TAPS - 1], us[:, :, :], ACT.Copy).then_inc(ext_done, 1)

            def w_high(c):
                act.wait_ge(w_ld[c % WS], 32 * (c // WS + 1))
                A.activation(wh[:, c, :], wst[:, c % WS, :], ACT.Copy).then_inc(w_hi, 1)
            for c in range(WS):
                w_high(c)
            act.wait_ge(eps_set, 2)
            act.wait_ge(c_in, 48)
            n = 0

            def highs(n):
                b, e = block_of[order[n]]
                s = n % FS
                act.wait_ge(block_done, b + 1)
                act.wait_ge(a_in[s], 16 * (n // FS + 1))
                if n >= FS:
                    act.wait_ge(pe_o, n - FS + 1)
                A.activation(fh[:, s, 0:CC], gc[:, b % 2, :, e * P:(e + 1) * P], ACT.Copy)
                A.activation(fh[:, s, CC:KC], am[:, s], ACT.Copy).then_inc(hi_done, 1)

            def squares(n):
                act.wait_ge(res_done, n + 1)
                if n:
                    act.wait_ge(sq_done, n)
                A.activation(sq[:, :], res[:, n % 2, :], ACT.Square, accum_out=ssq[:, n:n + 1]).then_inc(sq_done, 1)
                act.wait_ge(sq_done, n + 1)
                A.activation(ms[:, n:n + 1], ssq[:, n:n + 1], ACT.Sqrt, scale=1.0 / D, bias=eps6[:, :]).then_inc(rstd_done, 1)
            w_next = WS
            for what, k in schedule:
                if what == "tile":
                    if n == 0:
                        highs(0)
                    elif n + 1 < NT:
                        highs(n + 1)
                    if n:
                        squares(n - 1)
                    n += 1
                    continue
                w = len(BLOCKS[k]) * P
                if what == "a":
                    act.wait_ge(centred, k + 1)
                    if k:
                        act.wait_ge(block_done, k)
                    A.activation(tmp[:, :, 0:w], y[:, k % 2, :, 0:w], ACT.Square).then_inc(squared, 1)
                elif what == "b":
                    act.wait_ge(var_done, k + 1)
                    if k >= 2:
                        act.wait_ge(normed, k - 1)
                    A.activation(std[:, k % 2, 0:w], ST[:, 1, 0:w], ACT.Sqrt, bias=epsb[:, :]).then_inc(std_done, 1)
                else:
                    act.wait_ge(normed, k + 1)
                    for c in range(CC):
                        A.activation(z[:, c, 0:w], y[:, k % 2, c, 0:w], ACT.Identity, bias=lb[:, c:c + 1], scale=lg[:, c:c + 1])
                        last = A.activation(tmp[:, c, 0:w], y[:, k % 2, c, 0:w], ACT.Sigmoid, bias=lb[:, c:c + 1], scale=lg[:, c:c + 1])
                    last.then_inc(swish_in, 1)
                    if k == 1:
                        highs(1)
                if w_next < KC:
                    w_high(w_next)
                    w_next += 1
            squares(NT - 1)

        @block.vector
        def _(dve):
            V = nc.vector
            dr = V.drain
            TT = lambda out, a, b, op: V.tensor_tensor(out=out, in0=a, in1=b, op=op)
            V.memset(eps6[:, :], EPS).then_inc(eps_set, 1)
            dve.wait_ge(ext_done, 1)
            dve.wait_ge(c_in, 48)
            for c in range(CC):
                TT(ext[:, c], ext[:, c], cw[:, c, :].unsqueeze(1).to_broadcast([128, NS, TAPS]), ALU.mult)
            dr()
            for c in range(CC):
                V.tensor_reduce(ys[:, c, :], ext[:, c], AX.X, ALU.add)
            dr()
            TT(ys[:, :, :], ys[:, :, :], cb[:, :].unsqueeze(2).to_broadcast([128, CC, NS]), ALU.add)
            dr()
            dve.wait_ge(y_in[0], 32)
            V.tensor_copy(y[:, 0, :, SROW:SROW + NS], ys[:, :, :]).then_inc(ys_done, 1)
            n = 0

            def finish(n):
                s = n % 2
                dve.wait_ge(rstd_done, n + 1)
                V.reciprocal(rstd[:, n:n + 1], ms[:, n:n + 1])
                dr()
                if n >= 2:
                    out_written(dve, n - 2)
                V.scalar_tensor_tensor(fin[:, s, :], res[:, s, :], rstd[:, n:n + 1], gf[:, :], ALU.mult, ALU.mult).then_inc(fin_done, 1)
            for what, k in dve_schedule:
                if what == "tile":
                    s = n % 2
                    dve.wait_ge(pe_o, n + 1)
                    x_arrived(dve, n)
                    if n >= 2:
                        dve.wait_ge(fin_done, n - 1)
                    TT(res[:, s, :], O[:, s, :], xr[:, s, :], ALU.add).then_inc(res_done, 1)
                    if n:
                        finish(n - 1)
                    n += 1
                    continue
                w = len(BLOCKS[k]) * P
                if what == "a":
                    dve.wait_ge(y_in[k % 2], 32 * (k // 2 + 1))
                    dve.wait_ge(mean_done, k + 1)
                    TT(y[:, k % 2, :, 0:w], y[:, k % 2, :, 0:w], ST[:, 0, 0:w].unsqueeze(1).to_broadcast([128, CC, w]), ALU.subtract).then_inc(centred, 1)
                elif what == "b":
                    dve.wait_ge(std_done, k + 1)
                    V.reciprocal(std[:, k % 2, 0:w], std[:, k % 2, 0:w])
                    dr()
                    TT(y[:, k % 2, :, 0:w], y[:, k % 2, :, 0:w], std[:, k % 2, 0:w].unsqueeze(1).to_broadcast([128, CC, w]), ALU.mult).then_inc(normed, 1)
                else:
                    dve.wait_ge(swish_in, k + 1)
                    TT(z[:, :, 0:w], z[:, :, 0:w], tmp[:, :, 0:w], ALU.mult)
                    dr()
                    TT(gc[:, k % 2, :, 0:w], z[:, :, 0:w], gc[:, k % 2, :, 0:w], ALU.mult).then_inc(block_done, 1)
            finish(NT - 1)

        @block.tensor
        def _(pe):
            ident = part(mem.cst, "ident")
            ones = part(mem.cst, "ones")
            T = nc.tensor
            pe.wait_ge(st_in, 64)
            for c in range(CC):
                last = T.transpose(M[0:TAPS - 1, 0, c * P:(c + 1) * P], un[:, c, :], ident)
            last.then_inc(pe_m, 1)
            for c in range(CC):
                last = T.transpose(M[0:NS, 1, c * P:(c + 1) * P], us[:, c, :], ident)
            last.then_inc(pe_m, 1)
            for e in range(4):
                pe.wait_ge(act_m, e + 1)
                c0, half = 2 * (e // 2), e % 2
                for c in range(2):
                    last = T.transpose(M[:, e % 2, c * SB:(c + 1) * SB], st[:, half, (c0 + c) * P:(c0 + c + 1) * P], ident[0:SB, 0:SB])
                last.then_inc(pe_m, 1)
            n = 0
            for what, k in schedule:
                if what == "tile":
                    s = n % 2
                    if n == 0:
                        pe.wait_ge(w_lo, KC)
                    pe.wait_ge(lo_done, n + 1)
                    if n >= 2:
                        pe.wait_ge(res_done, n - 1)
                    for c in range(KC):
                        for e, (a, b) in enumerate(((fh, wh), (fh, wl), (fl, wh))):
                            for h in range(2):
                                last = T.matmul(O[:, s, h * 512:(h + 1) * 512], a[:, n % FS, c, :], b[:, c, h * 512:(h + 1) * 512],
                                                start=(c == 0 and e == 0), stop=(c == KC - 1 and e == 2))
                    last.then_inc(pe_o, 1)
                    n += 1
                    continue
                w = len(BLOCKS[k]) * P
                if what == "a":
                    pe.wait_ge(y_in[k % 2], 32 * (k // 2 + 1))
                    if k == 0:
                        pe.wait_ge(ys_done, 1)
                    else:
                        pe.wait_ge(centred, k)
                    for c in range(CC):
                        last = T.matmul(ST[:, 0, 0:w], ones, y[:, k % 2, c, 0:w], start=(c == 0), stop=(c == CC - 1))
                    last.then_inc(mean_done, 1)
                elif what == "b":
                    pe.wait_ge(squared, k + 1)
                    if k:
                        pe.wait_ge(std_done, k)
                    for c in range(CC):
                        last = T.matmul(ST[:, 1, 0:w], ones, tmp[:, c, 0:w], start=(c == 0), stop=(c == CC - 1))
                    last.then_inc(var_done, 1)


class Tensors:
    pass


class OnChip:

    def __init__(self, cst, g=None, iw=None, xh=None, xl=None, ikh=None, ikl=None, scores=None,
                 cw=None, cb=None):
        self.cst, self.g, self.iw, self.xh, self.xl, self.ikh, self.ikl = cst, g, iw, xh, xl, ikh, ikl
        self.scores, self.cw, self.cb = scores, cw, cb


def build(nc, t):
    scratch = lambda name, shape, dt: nc.dram_tensor(name, shape, dt, kind="Internal").ap()
    t.d_xh = scratch("d_xh", (HALF, 128, D), f32)
    t.d_xl = scratch("d_xl", (HALF, 128, D), f32)
    t.d_q = scratch("d_q", (NT, 128, NH, P), f32)
    t.d_u = scratch("d_u", (CC, 128, NT * P), f32)
    t.d_gc = scratch("d_gc", (CC, 128, NT * P), f32)
    t.d_ga = scratch("d_ga", (CC, 128, NT * P), f32)
    t.d_mask = scratch("d_mask", (NT, 128, LP), bf16)
    t.d_qs = scratch("d_qs", (128, NS * NS * NH), f32)
    t.d_mix = scratch("d_mix", (NT, 128, CC, P), f32)
    t.d_y = scratch("d_y", (CC, 128, NT * P), f32)
    t.d_r = scratch("d_r", (P, NH, BANDX), f32)
    with ExitStack() as ctx:
        sb = lambda n, s, d=f32: ctx.enter_context(nc.sbuf_tensor(n, s, d))
        cst = sb("cst", [128, NCONST])
        with ExitStack() as proj:
            sp = lambda n, s, d=f32: proj.enter_context(nc.sbuf_tensor(n, s, d))
            mem = OnChip(cst=cst, g=sp("g", [128, KC]), iw=sp("iw", [128, NT, IH]),
                         xh=sp("xh", [128, SLOTS, KC, P], f32r), xl=sp("xl", [128, SLOTS, KC, P], f32r),
                         ikh=sp("ikh", [128, NT * P], f32r), ikl=sp("ikl", [128, NT * P], f32r),
                         scores=sp("scores", [128, 3, LP]))
            project_norm_and_keys(nc, t, mem)
            project_and_select(nc, t, mem)
        cw, cb = sb("cw", [128, CC, TAPS]), sb("cb", [128, CC])
        attend_and_convolve(nc, t, OnChip(cst=cst, cw=cw, cb=cb))
        mix_out(nc, t, OnChip(cst=cst, cw=cw, cb=cb))


INS = ["x_prompt", "x_sample", "cache_k", "cache_v", "cache_idx_k", "state_conv", "page_table", "meta_tokens", "rel_bias",
       "norm_g", "w_in", "conv_w", "conv_b", "conv_ln_g", "conv_ln_b", "w_out", "final_norm_g"]
OUTS = [("y_prompt", (1, SEQ, D)), ("y_sample", (NS, 1, D)), ("nk_p", (1, 1, LP, NKV, HD)), ("nv_p", (1, 1, LP, NKV, HD)),
        ("nik_p", (1, 1, LP, 64)), ("nconv_p", (1, 1, TAPS - 1, C)), ("nk_s", (1, NS, 1, NKV, HD)),
        ("nv_s", (1, NS, 1, NKV, HD)), ("nik_s", (1, NS, 1, 64)), ("nconv_s", (1, NS, TAPS - 1, C))]


def declare(nc, shapes):
    shape_of = dict(OUTS)

    def inp(name):
        shape, dt = shapes[name]
        return nc.dram_tensor(f"in_{name}", shape, dt, kind="ExternalInput").ap()

    def out(name):
        return nc.dram_tensor(f"out_{name}", shape_of[name], f32, kind="ExternalOutput").ap()
    t = Tensors()
    t.x_prompt = inp("x_prompt")
    t.x_sample = inp("x_sample")
    t.cache_k = inp("cache_k")
    t.cache_v = inp("cache_v")
    t.cache_idx_k = inp("cache_idx_k")
    t.state_conv = inp("state_conv")
    t.page_table = inp("page_table")
    t.meta_tokens = inp("meta_tokens")
    t.rel_bias = inp("rel_bias")
    t.norm_g = inp("norm_g")
    t.w_in = inp("w_in")
    t.conv_w = inp("conv_w")
    t.conv_b = inp("conv_b")
    t.conv_ln_g = inp("conv_ln_g")
    t.conv_ln_b = inp("conv_ln_b")
    t.w_out = inp("w_out")
    t.final_norm_g = inp("final_norm_g")
    t.consts = inp("consts")
    t.y_prompt = out("y_prompt")
    t.y_sample = out("y_sample")
    t.nk_p = out("nk_p")
    t.nv_p = out("nv_p")
    t.nik_p = out("nik_p")
    t.nconv_p = out("nconv_p")
    t.nk_s = out("nk_s")
    t.nv_s = out("nv_s")
    t.nik_s = out("nik_s")
    t.nconv_s = out("nconv_s")
    return t


def kernel(**inputs):
    import concourse.bacc as bacc
    from concourse.bass_utils import run_bass_kernel_spmd
    nc = bacc.Bacc("TRN2", target_bir_lowering=False, num_devices=1)
    arrays = {n: np.ascontiguousarray(inputs[n]) for n in INS}
    arrays["consts"] = constants()
    t = declare(nc, {n: (a.shape, mybir.dt.from_np(a.dtype)) for n, a in arrays.items()})
    build(nc, t)
    r = run_bass_kernel_spmd(nc, [{f"in_{n}": a for n, a in arrays.items()}], core_ids=[0])
    return tuple(r.results[0][f"out_{n}"] for n, _ in OUTS)
```
